# Optimizing a Trainium2 kernel written in Bass

```python
import math
import jax
import jax.numpy as jnp
from jax import lax
import numpy as np

D_MODEL = 1024
BATCH = 1
SEQ = 512
DEPTH = 1
DEC_BATCH = 1
DEC_SEQ = 32
PAST_LEN = 256

CHUNK = 64
EPS = 1e-6
MLA_HEADS = 8
Q_LORA = 256
KV_LORA = 128
NOPE_DIM = 64
ROPE_DIM = 32
V_DIM = 64
ROPE_THETA = 10000.0
QBLK = 128
GLA_HEADS = 4
GLA_DK = 128
GLA_DV = 256
GATE_RANK = 16
GATE_TEMP = 16.0
GLA_BLOCK = 16
N_GROUPS = 4
EXPERTS_PER_GROUP = 8
N_EXPERTS = 32
TOP_K = 2
EXPERT_FF = 512
ROUTE_BLOCK = 128
IN_SPLITS = (Q_LORA, KV_LORA, ROPE_DIM, GLA_HEADS * GLA_DK, GLA_HEADS * GLA_DK, GLA_HEADS * GLA_DV, GATE_RANK, GLA_HEADS * GLA_DV, D_MODEL, D_MODEL)
IN_COLS = Q_LORA + KV_LORA + ROPE_DIM + 2 * GLA_HEADS * GLA_DK + 2 * GLA_HEADS * GLA_DV + GATE_RANK + 2 * D_MODEL

kernel_name = "streaming_mla_gla_hier_moe"

def rmsnorm(x, g):
    xf = x.astype(jnp.float32)
    y = xf * lax.rsqrt(jnp.mean(xf * xf, axis=-1, keepdims=True) + EPS)
    return (y * g.astype(jnp.float32)).astype(x.dtype)

def rope(x, pos):
    half = ROPE_DIM // 2
    inv = ROPE_THETA ** (-jnp.arange(half, dtype=jnp.float32) / half)
    ang = pos.astype(jnp.float32)[:, None] * inv[None, :]
    cos = jnp.cos(ang)[None, :, None, :]
    sin = jnp.sin(ang)[None, :, None, :]
    x1 = x[..., :half].astype(jnp.float32)
    x2 = x[..., half:].astype(jnp.float32)
    return jnp.concatenate([x1 * cos - x2 * sin, x2 * cos + x1 * sin], axis=-1).astype(x.dtype)

def split_cols(z):
    idx = np.cumsum(np.array(IN_SPLITS))[:-1].tolist()
    return jnp.split(z, idx, axis=-1)

def attend_block(qn, qp, q_pos, k_nope, k_pe, v, k_pos):
    scale = 1.0 / math.sqrt(NOPE_DIM + ROPE_DIM)
    s = (jnp.einsum("bqhd,bkhd->bhqk", qn, k_nope) + jnp.einsum("bqhr,bkr->bhqk", qp, k_pe)).astype(jnp.float32) * scale
    allowed = (k_pos[None, :] // CHUNK) <= (q_pos[:, None] // CHUNK)
    s = jnp.where(allowed[None, None], s, -jnp.inf)
    p = jax.nn.softmax(s, axis=-1).astype(v.dtype)
    return jnp.einsum("bhqk,bkhd->bqhd", p, v)

def mla_attention(qn, qp, q_pos, ckv_all, kpe_all, k_pos, w_ukv):
    b, t, _ = ckv_all.shape
    l = qn.shape[1]
    kv = (ckv_all @ w_ukv).reshape(b, t, MLA_HEADS, NOPE_DIM + V_DIM)
    k_nope, v = kv[..., :NOPE_DIM], kv[..., NOPE_DIM:]
    if l % QBLK == 0 and l > QBLK:
        nb = l // QBLK
        qn_b = qn.reshape(b, nb, QBLK, MLA_HEADS, NOPE_DIM).swapaxes(0, 1)
        qp_b = qp.reshape(b, nb, QBLK, MLA_HEADS, ROPE_DIM).swapaxes(0, 1)
        pos_b = q_pos.reshape(nb, QBLK)

        def blk(args):
            a_qn, a_qp, a_pos = args
            return attend_block(a_qn, a_qp, a_pos, k_nope, kpe_all, v, k_pos)

        o = lax.map(blk, (qn_b, qp_b, pos_b))
        o = o.swapaxes(0, 1).reshape(b, l, MLA_HEADS * V_DIM)
    else:
        o = attend_block(qn, qp, q_pos, k_nope, kpe_all, v, k_pos).reshape(b, l, MLA_HEADS * V_DIM)
    return o

def gla_block(q, k, v, la, s):
    q = q.astype(jnp.float32)
    k = k.astype(jnp.float32)
    v = v.astype(jnp.float32)
    bcum = jnp.cumsum(la, axis=1)
    qe = q * jnp.exp(bcum)
    ke = k * jnp.exp(-bcum)
    n = q.shape[1]
    causal = jnp.tril(jnp.ones((n, n), dtype=bool))
    att = jnp.where(causal[None, None], jnp.einsum("blhk,bmhk->bhlm", qe, ke), 0.0)
    o = jnp.einsum("blhk,bhkv->blhv", qe, s) + jnp.einsum("bhlm,bmhv->blhv", att, v)
    b_last = bcum[:, -1]
    s_new = jnp.exp(b_last)[..., None] * s + jnp.einsum("blhk,blhv->bhkv", k * jnp.exp(b_last[:, None] - bcum), v)
    return o, s_new

def gla(q, k, v, la, s0):
    b, l = q.shape[:2]
    if l % GLA_BLOCK == 0:
        nb = l // GLA_BLOCK

        def to_blocks(t):
            return t.reshape((b, nb, GLA_BLOCK) + t.shape[2:]).swapaxes(0, 1)

        def step(s, xs):
            o, s = gla_block(xs[0], xs[1], xs[2], xs[3], s)
            return s, o

        s_fin, o = lax.scan(step, s0, (to_blocks(q), to_blocks(k), to_blocks(v), to_blocks(la)))
        o = o.swapaxes(0, 1).reshape(b, l, GLA_HEADS, GLA_DV)
    else:
        o, s_fin = gla_block(q, k, v, la, s0)
    return o, s_fin

def hier_moe(h, w_rg, b_rg, w_re, b_re, w_gate, w_up, w_down):
    n, d = h.shape
    g_prob = jax.nn.softmax((h @ w_rg + b_rg).astype(jnp.float32), axis=-1)
    p_top, g_top = lax.top_k(g_prob, 1)
    e_logits = (h @ w_re + b_re).astype(jnp.float32).reshape(n, N_GROUPS, EXPERTS_PER_GROUP)
    e_in_group = e_logits[jnp.arange(n), g_top[:, 0]]
    v_top, i_top = lax.top_k(e_in_group, TOP_K)
    gates = jax.nn.softmax(v_top, axis=-1) * p_top
    expert_id = g_top * EXPERTS_PER_GROUP + i_top
    a = n * TOP_K
    flat_e = expert_id.reshape(a)
    flat_w = gates.reshape(a)
    flat_tok = jnp.arange(a, dtype=jnp.int32) // TOP_K
    order = jnp.argsort(flat_e)
    sorted_e = flat_e[order]
    counts = jnp.bincount(flat_e, length=N_EXPERTS)
    padded = (counts + ROUTE_BLOCK - 1) // ROUTE_BLOCK * ROUTE_BLOCK
    pad_end = jnp.cumsum(padded)
    pad_start = pad_end - padded
    seg_start = jnp.cumsum(counts) - counts
    dest = pad_start[sorted_e] + jnp.arange(a, dtype=jnp.int32) - seg_start[sorted_e]
    n_blocks = -(-a // ROUTE_BLOCK) + N_EXPERTS
    total = n_blocks * ROUTE_BLOCK
    tok_buf = jnp.full((total,), n, dtype=jnp.int32).at[dest].set(flat_tok[order])
    w_buf = jnp.zeros((total,), dtype=jnp.float32).at[dest].set(flat_w[order])
    block_expert = jnp.minimum(jnp.searchsorted(pad_end, jnp.arange(n_blocks, dtype=jnp.int32) * ROUTE_BLOCK, side="right"), N_EXPERTS - 1)
    h_pad = jnp.concatenate([h, jnp.zeros((1, d), h.dtype)], axis=0)
    x_blocks = h_pad[tok_buf].reshape(n_blocks, ROUTE_BLOCK, d)

    def expert_block(args):
        xb, e = args
        return (jax.nn.silu(xb @ w_gate[e]) * (xb @ w_up[e])) @ w_down[e]

    out = lax.map(expert_block, (x_blocks, block_expert)).reshape(total, d)
    y = jax.ops.segment_sum(out * w_buf[:, None], tok_buf, num_segments=n + 1)[:n]
    return y.astype(h.dtype)

def trunk_layer(x, ckv_past, kpe_past, s0, p):
    b, l, d = x.shape
    past = ckv_past.shape[1]
    pos = past + jnp.arange(l, dtype=jnp.int32)
    h = rmsnorm(x, p["g_norm_mix"])
    cq, ckv_raw, kpe_raw, gq, gk, gv, glr, gr, ga, gb = split_cols(h @ p["w_in"])
    q = (rmsnorm(cq, p["g_qnorm"]) @ p["w_uq"]).reshape(b, l, MLA_HEADS, NOPE_DIM + ROPE_DIM)
    q_nope = q[..., :NOPE_DIM]
    q_pe = rope(q[..., NOPE_DIM:], pos)
    ckv = rmsnorm(ckv_raw, p["g_kvnorm"])
    kpe = rope(kpe_raw[:, :, None, :], pos)[:, :, 0, :]
    ckv_all = jnp.concatenate([ckv_past.astype(ckv.dtype), ckv], axis=1)
    kpe_all = jnp.concatenate([kpe_past.astype(kpe.dtype), kpe], axis=1)
    k_pos = jnp.arange(past + l, dtype=jnp.int32)
    o_a = mla_attention(q_nope, q_pe, pos, ckv_all, kpe_all, k_pos, p["w_ukv"])
    qg = gq.reshape(b, l, GLA_HEADS, GLA_DK) * (GLA_DK ** -0.5)
    kg = gk.reshape(b, l, GLA_HEADS, GLA_DK)
    vg = gv.reshape(b, l, GLA_HEADS, GLA_DV)
    la = jax.nn.log_sigmoid((glr @ p["w_gate2"] + p["b_gate2"]).astype(jnp.float32)).reshape(b, l, GLA_HEADS, GLA_DK) / GATE_TEMP
    o_g, s_new = gla(qg, kg, vg, la, s0)
    o_b = (rmsnorm(o_g, p["g_gla_norm"]) * jax.nn.silu(gr.astype(jnp.float32)).reshape(b, l, GLA_HEADS, GLA_DV)).reshape(b, l, GLA_HEADS * GLA_DV)
    merged = jax.nn.sigmoid(ga) * (o_a @ p["w_branch_a"]) + jax.nn.sigmoid(gb) * (o_b.astype(x.dtype) @ p["w_branch_b"])
    x = x + (merged.astype(x.dtype) @ p["w_out"]).astype(x.dtype)
    h2 = rmsnorm(x, p["g_norm_ffn"]).reshape(b * l, d)
    y = hier_moe(h2, p["w_router_group"], p["b_router_group"], p["w_router_expert"], p["b_router_expert"], p["w_exp_gate"], p["w_exp_up"], p["w_exp_down"])
    x = x + y.reshape(b, l, d)
    return x, ckv, kpe, s_new

def setup_inputs(seed: int = 0) -> dict:
    key = jax.random.key(seed)
    ks = jax.random.split(key, 28)
    f32 = jnp.float32

    def nrm(k, shape, scale):
        return jax.random.normal(k, shape, f32) * scale

    def gain(k, shape):
        return 1.0 + 0.1 * jax.random.normal(k, shape, f32)

    return {
        "x_prompt": nrm(ks[0], (BATCH, SEQ, D_MODEL), 1.0),
        "x_sample": nrm(ks[1], (DEC_BATCH, DEC_SEQ, D_MODEL), 1.0),
        "cache_ckv": nrm(ks[2], (DEPTH, DEC_BATCH, PAST_LEN, KV_LORA), 1.0),
        "cache_krope": nrm(ks[3], (DEPTH, DEC_BATCH, PAST_LEN, ROPE_DIM), 1.0),
        "state_gla": nrm(ks[4], (DEPTH, DEC_BATCH, GLA_HEADS, GLA_DK, GLA_DV), 0.5),
        "w_in": nrm(ks[5], (DEPTH, D_MODEL, IN_COLS), D_MODEL ** -0.5),
        "g_norm_mix": gain(ks[6], (DEPTH, D_MODEL)),
        "g_qnorm": gain(ks[7], (DEPTH, Q_LORA)),
        "w_uq": nrm(ks[8], (DEPTH, Q_LORA, MLA_HEADS * (NOPE_DIM + ROPE_DIM)), Q_LORA ** -0.5),
        "g_kvnorm": gain(ks[9], (DEPTH, KV_LORA)),
        "w_ukv": nrm(ks[10], (DEPTH, KV_LORA, MLA_HEADS * (NOPE_DIM + V_DIM)), KV_LORA ** -0.5),
        "w_gate2": nrm(ks[11], (DEPTH, GATE_RANK, GLA_HEADS * GLA_DK), GATE_RANK ** -0.5),
        "b_gate2": nrm(ks[12], (DEPTH, GLA_HEADS * GLA_DK), 0.1),
        "g_gla_norm": gain(ks[13], (DEPTH, GLA_DV)),
        "w_branch_a": nrm(ks[14], (DEPTH, MLA_HEADS * V_DIM, D_MODEL), (MLA_HEADS * V_DIM) ** -0.5),
        "w_branch_b": nrm(ks[15], (DEPTH, GLA_HEADS * GLA_DV, D_MODEL), (GLA_HEADS * GLA_DV) ** -0.5),
        "w_out": nrm(ks[16], (DEPTH, D_MODEL, D_MODEL), D_MODEL ** -0.5),
        "g_norm_ffn": gain(ks[17], (DEPTH, D_MODEL)),
        "w_router_group": nrm(ks[18], (DEPTH, D_MODEL, N_GROUPS), D_MODEL ** -0.5),
        "b_router_group": nrm(ks[19], (DEPTH, N_GROUPS), 0.01),
        "w_router_expert": nrm(ks[20], (DEPTH, D_MODEL, N_EXPERTS), D_MODEL ** -0.5),
        "b_router_expert": nrm(ks[21], (DEPTH, N_EXPERTS), 0.01),
        "w_exp_gate": nrm(ks[22], (DEPTH, N_EXPERTS, D_MODEL, EXPERT_FF), D_MODEL ** -0.5),
        "w_exp_up": nrm(ks[23], (DEPTH, N_EXPERTS, D_MODEL, EXPERT_FF), D_MODEL ** -0.5),
        "w_exp_down": nrm(ks[24], (DEPTH, N_EXPERTS, EXPERT_FF, D_MODEL), EXPERT_FF ** -0.5),
        "g_norm_final": gain(ks[25], (D_MODEL,)),
    }

def reference(x_prompt, x_sample, cache_ckv, cache_krope, state_gla, w_in, g_norm_mix, g_qnorm, w_uq, g_kvnorm, w_ukv, w_gate2, b_gate2, g_gla_norm, w_branch_a, w_branch_b, w_out, g_norm_ffn, w_router_group, b_router_group, w_router_expert, b_router_expert, w_exp_gate, w_exp_up, w_exp_down, g_norm_final):
    bp = x_prompt.shape[0]
    yp, ys = x_prompt, x_sample
    ckv_p, kpe_p, gla_p, ckv_s, kpe_s, gla_s = [], [], [], [], [], []
    for l in range(DEPTH):
        p = {
            "w_in": w_in[l], "g_norm_mix": g_norm_mix[l], "g_qnorm": g_qnorm[l], "w_uq": w_uq[l],
            "g_kvnorm": g_kvnorm[l], "w_ukv": w_ukv[l], "w_gate2": w_gate2[l], "b_gate2": b_gate2[l],
            "g_gla_norm": g_gla_norm[l], "w_branch_a": w_branch_a[l], "w_branch_b": w_branch_b[l],
            "w_out": w_out[l], "g_norm_ffn": g_norm_ffn[l], "w_router_group": w_router_group[l],
            "b_router_group": b_router_group[l], "w_router_expert": w_router_expert[l],
            "b_router_expert": b_router_expert[l], "w_exp_gate": w_exp_gate[l], "w_exp_up": w_exp_up[l],
            "w_exp_down": w_exp_down[l],
        }
        yp, c1, k1, s1 = trunk_layer(
            yp,
            jnp.zeros((bp, 0, KV_LORA), x_prompt.dtype),
            jnp.zeros((bp, 0, ROPE_DIM), x_prompt.dtype),
            jnp.zeros((bp, GLA_HEADS, GLA_DK, GLA_DV), jnp.float32),
            p)
        ys, c2, k2, s2 = trunk_layer(ys, cache_ckv[l], cache_krope[l], state_gla[l].astype(jnp.float32), p)
        ckv_p.append(c1); kpe_p.append(k1); gla_p.append(s1)
        ckv_s.append(c2); kpe_s.append(k2); gla_s.append(s2)
    y_prompt = rmsnorm(yp, g_norm_final)
    y_sample = rmsnorm(ys, g_norm_final)
    return (y_prompt, y_sample, jnp.stack(ckv_p), jnp.stack(kpe_p), jnp.stack(gla_p), jnp.stack(ckv_s), jnp.stack(kpe_s), jnp.stack(gla_s))


_drawn_inputs = setup_inputs


def setup_inputs(seed=0):
    import zlib

    import numpy as np

    out = dict(_drawn_inputs(seed))
    spreads = {}
    factors = {'g_qnorm': 3.185, 'b_router_group': 4.077, 'b_router_expert': 8.0}
    for name, (base, spread) in spreads.items():
        noise = np.random.default_rng([zlib.crc32(name.encode()), seed]).standard_normal(out[name].shape)
        drawn = base * np.exp(spread * noise) if base else spread * noise
        out[name] = jnp.asarray(drawn.astype(out[name].dtype))
    for name, factor in factors.items():
        out[name] = (out[name] * factor).astype(out[name].dtype)
    return out
```

```python
from contextlib import ExitStack

import numpy as np

import concourse.bass as bass
from concourse import mybir

ALU = mybir.AluOpType
ACT = mybir.ActivationFunctionType
AX = mybir.AxisListType
F32 = mybir.dt.float32
F32R = mybir.dt.float32r
BF16 = mybir.dt.bfloat16
U32 = mybir.dt.uint32
I32 = mybir.dt.int32

P = 128
D = 1024
SEQ, DEC, PAST = 512, 32, 256
TOK = SEQ + DEC
HALF = TOK // 2
NT = 5
ROWS = [P, P, P, P, DEC]
KD = D // P
EPS = 1e-6
HEADS, Q_LORA, KV_LORA, NOPE, ROPE, VD = 8, 256, 128, 64, 32, 64
QK = NOPE + ROPE
ATT_SCALE = float(1.0 / np.sqrt(QK))
GH, DK, DV, RANK = 4, 128, 256, 16
SUB = 32
GROUPS, PER_GROUP, NE, FF = 4, 8, 32, 512
SLOTS = 64
NMAIN = NE * SLOTS
NOVER = (2 * TOK) // (SLOTS + 1)
NSLOT = NMAIN + NOVER * SLOTS
KEYS = SEQ + PAST + DEC
BIG = 1e30
EXP_CAP = 80.0

COLS = {}
_c = 0
for _name, _n in (("cq", Q_LORA), ("kv", KV_LORA), ("kr", ROPE), ("gq", GH * DK), ("gk", GH * DK), ("gv", GH * DV),
                  ("lr", RANK), ("gr", GH * DV), ("ga", D), ("gb", D)):
    COLS[_name] = _c
    _c += _n

CONST_AT = {}
_c = 0
for _name, _n in (("ident", P), ("tri16", P), ("causal", P), ("before", P), ("rope", TOK), ("iota4", GROUPS),
                  ("iota32", NE), ("base", NE), ("steps", 8), ("blocks", NOVER), ("valid", NT)):
    CONST_AT[_name] = (_c, _n)
    _c += _n
NCONST = _c


def shape_constants():
    c = np.zeros((P, NCONST), np.float32)

    def put(name, a):
        at, n = CONST_AT[name]
        c[:, at:at + n] = a

    r = np.arange(P)
    put("ident", np.eye(P))
    put("tri16", (r[:, None] <= r[None, :]) / 16.0)
    put("causal", r[None, :] <= r[:, None])
    put("before", r[:, None] < r[None, :])
    half = ROPE // 2
    inv = np.float32(10000.0) ** (-np.arange(half, dtype=np.float32) / np.float32(half))
    pos = np.concatenate([np.arange(SEQ), PAST + np.arange(DEC)]).astype(np.float32)
    ang = (pos[None, :] * inv[:, None].astype(np.float32)).astype(np.float32)
    rope = np.zeros((P, TOK), np.float32)
    rope[64:80] = rope[80:96] = np.cos(ang)
    rope[96:112], rope[112:128] = -np.sin(ang), np.sin(ang)
    put("rope", rope)
    put("iota4", np.arange(GROUPS) - 64.0)
    put("iota32", np.arange(NE) - 64.0)
    put("base", np.arange(NE) * float(SLOTS))
    put("steps", np.arange(1, 9) * float(SLOTS))
    put("blocks", np.arange(NOVER) * 1.0)
    valid = np.ones((P, NT), np.float32)
    valid[DEC:, NT - 1] = 0.0
    put("valid", valid)
    return c


def weight_tiles():
    t = [("cq", 0), ("cq", 1), ("kv", 0), ("kr", 0), ("uq", 0), ("uq", 1)]
    t += [("gq", j) for j in range(4)] + [("gk", j) for j in range(4)] + [("gv", j) for j in range(8)]
    t += [("gr", j) for j in range(8)]
    for j in range(8):
        t += [("ga", j), ("wa", j), ("gb", j), ("wb", j)]
    t += [("wo", j) for j in range(8)]
    return t


WT = weight_tiles()
WT_INDEX = {w: n for n, w in enumerate(WT)}
NRAW, NSPLIT = 3, 2
NPAIR = HEADS // 2


def outputs():
    o = []
    for n, (k, j) in enumerate(WT):
        if k == "gr":
            continue
        o += [(k, 4 * j + m, n) for m in range(4)] if k == "uq" else [(k, j, n)]
        if (k, j) == ("uq", 1):
            o += [("V", b, None) for b in range(7)] + [("K", hp, None) for hp in range(NPAIR)]
        if (k, j) == ("gv", 7):
            for c in range(NT):
                if c < 4:
                    o += [("gr", 2 * c + m, WT_INDEX["gr", 2 * c + m]) for m in range(2)]
                o += [("og", c, None), ("st", c, None)]
            o += [("om", h, None) for h in range(GH)]
    return o + [("lg", i, None) for i in range(NT)]


OUT = outputs()
OUT_INDEX = {(k, j): n for n, (k, j, _) in enumerate(OUT)}
LAST_OUT = {}
for _o, (_k, _j, _w) in enumerate(OUT):
    if _w is not None:
        LAST_OUT[_w] = _o


def n_loads(w):
    return {"kr": 4, "uq": 6}.get(w[0], 1)


UNITS = [(hp, i, a) for hp in range(HEADS // 2) for i in range(NT) for a in range(2)]


def unit_shape(i):
    if i < 4:
        return P, i * P, 0, P * (i + 1)
    return DEC, SEQ, SEQ, PAST + DEC


class Steps:

    def __init__(self, eng, sem):
        self.eng, self.sem, self.n = eng, sem, 0

    def __call__(self, ins):
        ins.then_inc(self.sem, 1)
        self.n += 1

    def settle(self):
        self.eng.wait_ge(self.sem, self.n)


def hT_high(nc, act, i, hTf_ready, hT_hi, hT_f, hT_hi_ready):
    act.wait_ge(hTf_ready, i + 1)
    nc.scalar.copy(hT_hi[:, :, i * P:i * P + ROWS[i]], hT_f[i % 2][:, :, 0:ROWS[i]]).then_inc(hT_hi_ready, 1)


def build(nc, t):
    ctx = ExitStack()
    with ctx:
        _build(nc, t, ctx)


def _build(nc, t, ctx):
    def sem(name):
        return ctx.enter_context(nc.semaphore(name))

    def flat(name):
        return t[name].rearrange("a b c -> (a b) c")

    BASE = 16512

    class Region:
        def __init__(self, at):
            self.at = at

        def __call__(self, name, shape, dt=F32, after=None):
            n = 1
            for s in shape[1:]:
                n *= s
            size = n * mybir.dt.size(dt)
            h = nc.alloc_sbuf_tensor_at(name, shape, dt, offset=self.at)
            self.at += (size + 31) // 32 * 32
            return h

    R = Region(BASE)
    X = R("x_rows", [P, NT, D])
    cst = R("cst", [P, NCONST])
    mean256 = R("mean256", [P, P])
    mean128 = R("mean128", [P, P])
    ones = R("ones", [P, P])
    eps_col = R("eps_col", [P, 1])
    qlow = R("qlow", [1, P], BF16)
    khigh = R("khigh", [1, P], BF16)
    g_mix = R("g_mix", [P, KD])
    g_q = R("g_q", [P, 2])
    g_kv = R("g_kv", [P, 1])
    g_gla = R("g_gla", [P, 2])
    g_ffn = R("g_ffn", [P, D])
    g_fin = R("g_fin", [P, D])
    w_rt = R("w_rt", [P, KD, P])
    b_rt = R("b_rt", [P, GROUPS + NE])
    w_g2 = R("w_g2", [RANK + 1, GH * DK])
    st_x = R("st_x", [P, 6, NT])
    meta = R("meta", [1, NOVER + 1], I32)
    slotU = R("slotU", [P, 2 * NT], U32)
    gate = R("gate", [P, 2, NT])
    RING = R.at
    raw = [R(f"raw{n}", [P, D]) for n in range(NRAW)]
    whi = [R(f"whi{n}", [P, D], F32R) for n in range(NSPLIT)]
    wlo = [R(f"wlo{n}", [P, D], F32R) for n in range(NSPLIT)]
    HT = R.at
    hT_hi = R("hT_hi", [P, KD, TOK], F32R)
    hT_lo = R("hT_lo", [P, KD, TOK], F32R)
    ARENA = R.at
    LAST = 229344

    A0 = Region(ARENA)
    xn = [A0(f"xn{n}", [P, D]) for n in range(2)]
    hT_f = [A0(f"hT_f{n}", [P, KD, P]) for n in range(2)]

    A = Region(ARENA)
    oa_hi = A("oa_hi", [P, 4, TOK], F32R)
    oa_lo = A("oa_lo", [P, 4, TOK], F32R)
    glr = A("glr", [RANK + 1, TOK])
    AFTER_OA = A.at
    w_kv = A("w_kv", [P, D])
    ckvA = A("ckvA", [P, KEYS])
    kpeA = A("kpeA", [P, KEYS])
    V = A("V", [P, 7, HEADS * VD])
    qT = A("qT", [P, HEADS, TOK])
    KC = A.at
    kcat = [A(f"kcat{n}", [P, 2, KEYS]) for n in range(2)]
    rtmp = A("rtmp", [P, 2, TOK])
    caches = A("caches", [P, 2, 2, P])
    obuf = A("obuf", [P, NT, KV_LORA])
    kbuf = A("kbuf", [P, NT, ROPE])
    SM = A.at
    cqn_hi = A("cqn_hi", [P, 2, TOK], F32R)
    cqn_lo = A("cqn_lo", [P, 2, TOK], F32R)
    kr = A("kr", [P, TOK])
    kvr = A("kvr", [P, TOK])
    kvs = A("kvs", [P, TOK])
    rk = A("rk", [P, TOK])
    zero = nc.alloc_sbuf_tensor_at("zero", [P, D], F32, offset=LAST - 4096)
    assert A.at <= LAST - 4096, A.at
    Q_ = Region(KC)
    cq = Q_("cq", [P, 2, TOK])
    cqs = Q_("cqs", [P, 2, TOK])
    rq = Q_("rq", [P, TOK])
    S_ = Region(SM)
    prob = [S_(f"prob{n}", [P, SEQ]) for n in range(3)]
    probT = [S_(f"probT{n}", [P, SEQ]) for n in range(2)]
    stat = S_("stat", [P, 4, len(UNITS)])

    G = Region(AFTER_OA)
    OG = G.at
    gqk = G("gqk", [P, 2 * GH, TOK])
    AFTER_OG = G.at
    gvT = [G(f"gvT{n}", [P, TOK]) for n in range(2)]
    vtok = G("vtok", [P, NT, GH * DV])
    la = G("la", [P, NT, GH * DK])
    GS = G.at
    S_st = G("S_st", [P, GH, DV])
    bS = G("bS", [P, GH, P])
    NX = GH * 4 * P + 3 * GH * P + GH
    ex = G("ex", [P, NX])
    att = G("att", [P, GH, P])
    kdT = G("kdT", [P, GH, P])
    attT = G("attT", [P, GH, P])
    assert G.at <= LAST - 4096, G.at
    S_smp = nc.alloc_sbuf_tensor_at("S_smp", [P, GH, DV], F32, offset=LAST - 4096)
    grs = nc.alloc_sbuf_tensor_at("grs", [P, 8, TOK], F32, offset=BASE)
    G2 = Region(GS)
    lmin = G2("lmin", [P, NT, GH * DK])

    N_ = Region(AFTER_OG)
    ob_lo = nc.alloc_sbuf_tensor_at("ob_lo", [P, 8, TOK], F32R, offset=OG)
    ob_hi = N_("ob_hi", [P, 8, TOK], F32R)
    sg = [N_(f"sg{n}", [P, TOK]) for n in range(2)]
    mtmp = N_("mtmp", [P, TOK])
    msum = [N_(f"msum{n}", [P, TOK]) for n in range(2)]
    MG0 = N_.at
    osq = [N_(f"osq{n}", [P, 2, TOK]) for n in range(2)]
    ors = [N_(f"ors{n}", [P, TOK]) for n in range(2)]
    assert N_.at <= LAST, N_.at
    MG = (LAST - 2 * 8 * TOK * 4) // 32 * 32
    YT = MG - 8 * TOK * 4
    assert MG >= MG0
    E_ = Region(YT)
    yT = E_("yT", [P, 8, TOK])
    mg_hi = E_("mg_hi", [P, 8, TOK], F32R)
    mg_lo = E_("mg_lo", [P, 8, TOK], F32R)
    F_ = Region(MG)
    h2 = F_("h2", [P, NT, D])
    h2T = F_("h2T", [P, KD, P])
    RT = F_.at
    W_ = Region(HT)
    we = [[W_(f"we{s}_{n}", [P, 4096]) for n in range(3)] for s in range(2)]
    assert W_.at - 16384 <= YT and W_.at <= MG
    K_ = Region(RING)
    xsb = K_("xsb", [P, D])
    xsT = K_("xsT", [P, KD, P])
    hg = K_("hg", [P, 2, FF])
    hT2 = K_("hT2", [P, 2, 4, SLOTS])
    yo = K_("yo", [P, 2, FF])
    assert K_.at <= HT
    Z_ = Region(MG)
    zg = [Z_(f"zg{n}", [P, D]) for n in range(4)]
    zo = [Z_(f"zo{n}", [P, D]) for n in range(2)]
    assert Z_.at <= RT

    def con(name, rows=P):
        at, n = CONST_AT[name]
        return cst[0:rows, at:at + n]

    proj = ctx.enter_context(nc.psum_tensor("proj", [P, 2, 2, 512], F32))
    bank = ctx.enter_context(nc.psum_tensor("bank", [P, 4, 512], F32))

    xs = nc.dram_tensor("expert_rows", (NSLOT, D), F32, kind="Internal").ap()
    ys = nc.dram_tensor("expert_out", (NSLOT, D), F32, kind="Internal").ap()
    w_in, w_uq, w_ukv = flat("w_in"), flat("w_uq"), flat("w_ukv")
    w_a, w_b, w_o = flat("w_branch_a"), flat("w_branch_b"), flat("w_out")
    w_eg = t["w_exp_gate"].rearrange("a e (k p) f -> (a e) p k f", p=P)
    w_eu = t["w_exp_up"].rearrange("a e (k p) f -> (a e) p k f", p=P)
    w_ed = t["w_exp_down"].rearrange("a e (k p) f -> (a e) p k f", p=P)

    def x_src(i):
        return flat("x_prompt")[i * P:(i + 1) * P, :] if i < 4 else flat("x_sample")

    x_loaded = [sem(f"x_loaded{i}") for i in range(NT)]
    w_loaded = [sem(f"w_loaded{n}") for n in range(NRAW)]
    proj_read = [sem(f"proj_read{n}") for n in range(2)]
    gathered = [sem(f"gathered{n}") for n in range(2)]
    y_stored = [sem(f"y_stored{n}") for n in range(2)]
    we_loaded = [[sem(f"we_loaded{s}_{n}") for n in range(3)] for s in range(2)]
    up_done = [sem(f"up_done{s}") for s in range(2)]
    silu_done = [sem(f"silu_done{s}") for s in range(2)]
    act_done = [sem(f"act_done{s}") for s in range(2)]
    hT2_done = [sem(f"hT2_done{s}") for s in range(2)]
    hT2_copied = [sem(f"hT2_copied{s}") for s in range(2)]
    down_done = [sem(f"down_done{s}") for s in range(2)]
    yo_ready = [sem(f"yo_ready{s}") for s in range(2)]
    ys_stored = [sem(f"ys_stored{s}") for s in range(2)]
    x_rms = sem("x_rms")
    xn_ready = sem("xn_ready")
    xT_ready = sem("xT_ready")
    hTf_ready = sem("hTf_ready")
    hT_hi_ready = sem("hT_hi_ready")
    hT_ready = sem("hT_ready")
    w_split = sem("w_split")
    proj_done = sem("proj_done")
    lat_mean = sem("lat_mean")
    lat_rms = sem("lat_rms")
    cqn_ready = sem("cqn_ready")
    ckv_ready = sem("ckv_ready")
    kpe_ready = sem("kpe_ready")
    q_ready = sem("q_ready")
    cache_T = sem("cache_T")
    keys_ready = sem("keys_ready")
    out_T = sem("out_T")
    out_copied = sem("out_copied")
    kcat_pe = sem("kcat_pe")
    scores_ready = sem("scores_ready")
    negmax_ready = sem("negmax_ready")
    exp_done = sem("exp_done")
    prob_ready = sem("prob_ready")
    probT_done = sem("probT_done")
    probT_copied = sem("probT_copied")
    pv_done = sem("pv_done")
    oa_done = sem("oa_done")
    gvT_done = sem("gvT_done")
    vtok_ready = sem("vtok_ready")
    gate_done = sem("gate_done")
    gate_abs = sem("gate_abs")
    gate_min = sem("gate_min")
    la_log = sem("la_log")
    la_ready = sem("la_ready")
    cum_done = sem("cum_done")
    bS_ready = sem("bS_ready")
    ex_arg = sem("ex_arg")
    ex_ready = sem("ex_ready")
    kq_ready = sem("kq_ready")
    att_done = sem("att_done")
    att_masked = sem("att_masked")
    attT_done = sem("attT_done")
    attT_copied = sem("attT_copied")
    kdT_done = sem("kdT_done")
    kdT_copied = sem("kdT_copied")
    S_ready = sem("S_ready")
    S_stored = sem("S_stored")
    osq_ready = sem("osq_ready")
    ob_ready = sem("ob_ready")
    mg_ready = sem("mg_ready")
    yrow_done = sem("yrow_done")
    x2_ready = sem("x2_ready")
    x2_rms = sem("x2_rms")
    h2_ready = sem("h2_ready")
    h2T_done = sem("h2T_done")
    h2T_copied = sem("h2T_copied")
    rt_exp_in = sem("rt_exp_in")
    rt_exp_out = sem("rt_exp_out")
    chosen = sem("chosen")
    ranks_done = sem("ranks_done")
    slots_ready = sem("slots_ready")
    zero_set = sem("zero_set")
    xs_zeroed = sem("xs_zeroed")
    xs_written = sem("xs_written")
    xs_loaded = sem("xs_loaded")
    xsT_done = sem("xsT_done")
    xsT_copied = sem("xsT_copied")
    more_x = sem("more_x")
    more_w = sem("more_w")
    more_xT = sem("more_xT")
    more_xT_copied = sem("more_xT_copied")
    more_up = sem("more_up")
    more_silu = sem("more_silu")
    more_act = sem("more_act")
    more_hT = sem("more_hT")
    more_hT_copied = sem("more_hT_copied")
    more_down = sem("more_down")
    more_yo = sem("more_yo")
    more_stored = sem("more_stored")
    more_all = sem("more_all")
    more_free = sem("more_free")
    yo_free = [sem(f"yo_free{s}") for s in range(2)]
    comb_done = sem("comb_done")
    comb_rms = sem("comb_rms")
    y_ready = sem("y_ready")
    lat_stored = sem("lat_stored")
    const_loaded = sem("const_loaded")
    sides_loaded = sem("sides_loaded")
    kv_loaded = sem("kv_loaded")
    caches_loaded = sem("caches_loaded")
    state_loaded = sem("state_loaded")
    consts_set = sem("consts_set")
    act_seq, dve_seq, pool_seq = sem("act_seq"), sem("dve_seq"), sem("pool_seq")

    def chunk_views(L):
        ns = L // SUB
        n0 = GH * ns * L
        n1 = GH * L

        def part(at, n):
            return ex[:, at:at + n]
        return (part(0, n0).rearrange("p (h s l) -> p h s l", h=GH, s=ns),
                part(n0, n1).rearrange("p (h s l) -> p h s l", h=GH, s=ns),
                part(n0 + n1, n1).rearrange("p (h l) -> p h l", h=GH),
                part(n0 + 2 * n1, n1).rearrange("p (h l) -> p h l", h=GH),
                part(n0 + 3 * n1, GH).rearrange("p (h l) -> p h l", h=GH))

    T_ = Region(RT)
    LG = T_("LG", [P, NT, GROUPS + NE])
    r5 = [T_(f"r5_{n}", [P, NT])[:, :] for n in range(4)]
    rG = T_("rG", [P, NT, GROUPS])[:, :, :]
    rOG = T_("rOG", [P, NT, GROUPS])[:, :, :]
    rPen = T_("rPen", [P, NT, GROUPS])[:, :, :]
    rE = T_("rE", [P, NT, NE])[:, :, :]
    rT = T_("rT", [P, NT, NE])[:, :, :]
    O1 = T_("O1", [P, NT, NE])[:, :, :]
    O2 = T_("O2", [P, NT, NE])[:, :, :]
    picks = T_("picks", [P, NT, NE])
    rank = T_("rank", [P, NT, NE])[:, :, :]
    base = T_("tile_base", [P, NT + 1, NE])
    rd = T_("rd", [P, NT])[:, :]
    cum = [T_(f"cum{n}", [P, NE])[:, :] for n in range(2)]
    nb = T_("nb", [P, NE])[:, :]
    nb8 = T_("nb8", [P, NE, 8])[:, :, :]
    nbe = T_("nbe", [1, NOVER, NE])[:, :, :]
    bef = T_("bef", [1, NOVER])[:, :]
    assert T_.at <= LAST, T_.at

    block = ctx.enter_context(nc.Block())

    @block.sync
    def _(sp):
        def weight_source(n):
            kind, j = WT[n]
            dst = raw[n % NRAW]
            if kind == "kr":
                d3 = dst[:, :].rearrange("p (k c) -> p k c", k=KD)
                src = w_in.rearrange("(k p) c -> p k c", p=P)
                lr, k0 = COLS["lr"], COLS["kr"]
                return [(d3[:, :, 0:64], src[:, :, lr:lr + 64]), (d3[:, :, 64:96], src[:, :, k0:k0 + 32]),
                        (d3[:, :, 96:112], src[:, :, k0 + 16:k0 + 32]), (d3[:, :, 112:128], src[:, :, k0:k0 + 16])]
            if kind == "uq":
                d4 = dst[:, :].rearrange("p (k h c) -> p k h c", k=2, h=4)
                src = w_uq.rearrange("(k p) (h c) -> p k h c", p=P, c=QK)
                return [p for k in range(2) for p in (
                    (d4[:, k, :, 0:96], src[:, k, 4 * j:4 * j + 4, :]),
                    (d4[:, k, :, 96:112], src[:, k, 4 * j:4 * j + 4, 80:96]),
                    (d4[:, k, :, 112:128], src[:, k, 4 * j:4 * j + 4, 64:80]))]
            w = {"wa": w_a, "wb": w_b, "wo": w_o}.get(kind, w_in)
            k = {"wa": 4}.get(kind, KD)
            c0 = COLS.get(kind, 0) + j * P
            return [(dst[:, 0:k * P].rearrange("p (k c) -> p k c", k=k),
                     w.rearrange("(k p) c -> p k c", p=P)[:, :, c0:c0 + P])]

        def load_weights(n):
            if n >= NRAW:
                sp.wait_ge(w_split, n - NRAW + 1)
            for dst, src in weight_source(n):
                sp.dma_start(dst, src).then_inc(w_loaded[n % NRAW], 16)

        for i in range(NT):
            sp.dma_start(X[0:ROWS[i], i, :], x_src(i)).then_inc(x_loaded[i], 16)
            if i == 0:
                sp.dma_start(cst[:, :], t["shape_constants"]).then_inc(const_loaded, 16)
                sp.dma_start(g_mix[:, :], t["g_mix_cols"]).then_inc(const_loaded, 16)
                sp.dma_start(g_q[:, :], t["g_q_cols"]).then_inc(const_loaded, 16)
                sp.dma_start(g_kv[:, :], t["g_kv_cols"]).then_inc(const_loaded, 16)
                sp.dma_start(g_gla[:, :], t["g_gla_cols"]).then_inc(const_loaded, 16)
        for n in range(NRAW):
            load_weights(n)
        for part in range(2):
            sp.dma_start(w_kv[:, part * FF:(part + 1) * FF].rearrange("p (h c) -> p h c", c=NOPE),
                         w_ukv.rearrange("p (h t c) -> p t h c", t=2, c=NOPE)[:, part]).then_inc(kv_loaded, 16)
        sp.dma_start(caches[:, 0, :, :], t["cache_ckv"].rearrange("a b (c p) d -> p (a b c) d", p=P)).then_inc(caches_loaded, 16)
        sp.dma_start(caches[:, 1, :, 64:96], t["cache_krope"].rearrange("a b (c p) d -> p (a b c) d", p=P)).then_inc(caches_loaded, 16)
        sp.dma_start(w_g2[0:RANK, :], flat("w_gate2")).then_inc(sides_loaded, 16)
        sp.dma_start(w_g2[RANK:RANK + 1, :], t["b_gate2"]).then_inc(sides_loaded, 16)
        sp.dma_start(g_ffn[:, :], t["g_norm_ffn"].to_broadcast([P, D])).then_inc(sides_loaded, 16)
        sp.dma_start(g_fin[:, :], t["g_norm_final"].rearrange("(a d) -> a d", a=1).to_broadcast([P, D])).then_inc(sides_loaded, 16)
        sp.dma_start(b_rt[:, 0:GROUPS], t["b_router_group"].to_broadcast([P, GROUPS])).then_inc(sides_loaded, 16)
        sp.dma_start(b_rt[:, GROUPS:], t["b_router_expert"].to_broadcast([P, NE])).then_inc(sides_loaded, 16)
        sp.dma_start(w_rt[:, :, 0:GROUPS], flat("w_router_group").rearrange("(k p) c -> p k c", p=P)).then_inc(sides_loaded, 16)
        sp.dma_start(w_rt[:, :, GROUPS:GROUPS + NE], flat("w_router_expert").rearrange("(k p) c -> p k c", p=P)).then_inc(sides_loaded, 16)
        for n in range(NRAW, len(WT)):
            load_weights(n)
            if n == WT_INDEX["gq", 2]:
                sp.wait_ge(out_copied, 1)
                sp.dma_start(t["ckv_prompt"].rearrange("a b (c p) d -> p (a b c) d", p=P), obuf[:, 0:4, :]).then_inc(lat_stored, 16)
                sp.dma_start(t["ckv_sample"].rearrange("a b p d -> (a b p) d"), obuf[0:DEC, 4, :]).then_inc(lat_stored, 16)
                sp.dma_start(t["krope_prompt"].rearrange("a b (c p) d -> p (a b c) d", p=P), kbuf[:, 0:4, :]).then_inc(lat_stored, 16)
                sp.dma_start(t["krope_sample"].rearrange("a b p d -> (a b p) d"), kbuf[0:DEC, 4, :]).then_inc(lat_stored, 16)
            if n == WT_INDEX["gv", 5]:
                sp.wait_ge(xs_zeroed, 32)
                sp.dma_start(S_smp[:, :, :], t["state_gla"].rearrange("a b h p v -> p (a b h) v")).then_inc(state_loaded, 16)
            if n == WT_INDEX["wa", 0]:
                sp.wait_ge(S_ready, 4)
                sp.dma_start(t["gla_prompt"].rearrange("a b h p v -> p (a b h) v"), S_st[:, :, :]).then_inc(S_stored, 16)
                sp.wait_ge(S_ready, 5)
                sp.dma_start(t["gla_sample"].rearrange("a b h p v -> p (a b h) v"), S_smp[:, :, :]).then_inc(S_stored, 16)
            if n == WT_INDEX["gb", 1]:
                sp.wait_ge(ob_ready, GH)
                for i in range(NT):
                    sp.dma_start(X[0:ROWS[i], i, :], x_src(i)).then_inc(x_loaded[i], 16)

        def load_expert(s, part, e):
            w = (w_eg, w_eu, w_ed)[part]
            k = (KD, KD, 4)[part]
            sp.dma_start(we[s][part][:, :].rearrange("p (k f) -> p k f", k=k),
                         w[bass.ds(e, 1)].rearrange("o p k f -> (o p) k f")).then_inc(we_loaded[s][part], 16)

        sp.wait_ge(proj_done, OUT_INDEX["wb", 7] + 1)
        sp.wait_ge(mg_ready, 8)
        for s in range(2):
            for part in range(3):
                if (s, part) == (1, 2):
                    sp.wait_ge(x2_ready, NT)
                load_expert(s, part, s)
        sp.wait_ge(xs_written, 16 * 2 * NT)
        sp.wait_ge(proj_done, len(OUT))
        sp.dma_start(xsb[:, :], xs[0:P, :]).then_inc(xs_loaded, 16)
        with sp.Fori(0, NE // 2 - 1) as q:
            sp.wait_ge(xsT_done, q + 1)
            sp.dma_start(xsb[:, :], xs[bass.ds(q * P + P, P), :]).then_inc(xs_loaded, 16)
            for s in range(2):
                sp.wait_ge(up_done[s], q + 1)
                load_expert(s, 0, q * 2 + 2 + s)
                load_expert(s, 1, q * 2 + 2 + s)
                sp.wait_ge(down_done[s], q + 1)
                load_expert(s, 2, q * 2 + 2 + s)

        sp.wait_ge(down_done[1], NE // 2)
        n_more = sp.value_load(meta[0:1, NOVER:NOVER + 1], min_val=0, max_val=NOVER)
        with sp.Fori(0, NOVER) as b:
            with sp.If(b < n_more):
                e = sp.value_load(meta[0:1, bass.ds(b, 1)], min_val=0, max_val=NE - 1)
                sp.wait_ge(more_free, b + 1)
                sp.dma_start(xsb[0:SLOTS, :], xs[bass.ds(b * SLOTS + NMAIN, SLOTS), :]).then_inc(more_x, 16)
                for part in range(3):
                    w = (w_eg, w_eu, w_ed)[part]
                    sp.dma_start(we[0][part][:, :].rearrange("p (k f) -> p k f", k=(KD, KD, 4)[part]),
                                 w[bass.ds(e, 1)].rearrange("o p k f -> (o p) k f")).then_inc(more_w, 16)

        for i in range(NT):
            sp.wait_ge(y_ready, i + 1)
            dst = flat("y_prompt")[i * P:(i + 1) * P, :] if i < 4 else flat("y_sample")
            sp.dma_start(dst, zo[i % 2][0:ROWS[i], :]).then_inc(y_stored[i % 2], 16)
        sp.wait_ge(y_stored[0], 48)
        sp.wait_ge(y_stored[1], 32)
        sp.wait_ge(S_stored, 32)
        sp.wait_ge(lat_stored, 64)

    @block.gpsimd
    def _(pool):
        step = Steps(pool, pool_seq)
        need = [0] * NRAW

        def split(n):
            kind, _ = WT[n]
            c = 4 * P if kind == "wa" else D
            need[n % NRAW] += 16 * n_loads(WT[n])
            pool.wait_ge(w_loaded[n % NRAW], need[n % NRAW])
            if n >= NSPLIT:
                pool.wait_ge(proj_done, LAST_OUT[n - NSPLIT] + 1)
            hi, lo = whi[n % NSPLIT], wlo[n % NSPLIT]
            step(nc.gpsimd.tensor_copy(hi[:, 0:c], raw[n % NRAW][:, 0:c]))
            step.settle()
            nc.gpsimd.tensor_tensor(lo[:, 0:c], raw[n % NRAW][:, 0:c], hi[:, 0:c].bitcast(F32),
                                    ALU.subtract).then_inc(w_split, 1)

        nc.gpsimd.memset(zero[:, :], 0.0).then_inc(zero_set, 1)
        split(0)
        split(1)
        for i in range(NT):
            pool.wait_ge(hT_hi_ready, i + 1)
            tok = slice(i * P, i * P + ROWS[i])
            nc.gpsimd.tensor_tensor(hT_lo[:, :, tok], hT_f[i % 2][:, :, 0:ROWS[i]], hT_hi[:, :, tok].bitcast(F32),
                                    ALU.subtract).then_inc(hT_ready, 1)
        pool.wait_ge(zero_set, 1)
        pool.dma_start(xs.rearrange("(p r) d -> p r d", p=P), zero[:, :].unsqueeze(1).to_broadcast([P, NSLOT // P, D]))\
            .then_inc(xs_zeroed, 16)
        more = ys[NMAIN:NSLOT, :].rearrange("(p r) d -> p r d", p=P)
        pool.dma_start(more, zero[:, :].unsqueeze(1).to_broadcast([P, (NSLOT - NMAIN) // P, D])).then_inc(xs_zeroed, 16)
        for n in range(2, len(WT)):
            split(n)

        pool.wait_ge(xs_zeroed, 32)
        pool.wait_ge(h2_ready, NT)
        pool.wait_ge(slots_ready, 1)
        for i in range(NT):
            for c in range(2):
                pool.indirect_dma_start(
                    out=xs[:, :], out_offset=bass.IndirectOffsetOnAxis(ap=slotU[0:ROWS[i], c * NT + i:c * NT + i + 1], axis=0),
                    in_=h2[0:ROWS[i], i, :], in_offset=None).then_inc(xs_written, 16)

        def store(s, row, ready, n, done):
            pool.wait_ge(ready, n)
            for half in range(2):
                pool.dma_start(ys[bass.ds(row, SLOTS), half * FF:(half + 1) * FF],
                               yo[64 * half:64 * half + 64, s, :]).then_inc(done, 16)

        for s in range(2):
            pool.sem_inc(yo_free[s], 1)
        pool.sem_inc(more_free, 1)
        with pool.Fori(0, NE // 2) as q:
            for s in range(2):
                store(s, q * P + s * SLOTS, yo_ready[s], q + 1, ys_stored[s])
            for s in range(2):
                pool.wait_ge(ys_stored[s], q * 32 + 32)
                pool.sem_inc(yo_free[s], 1)
        n_more = pool.value_load(meta[0:1, NOVER:NOVER + 1], min_val=0, max_val=NOVER)
        with pool.Fori(0, NOVER) as b:
            with pool.If(b < n_more):
                store(0, b * SLOTS + NMAIN, more_yo, b + 1, more_stored)
                pool.wait_ge(more_stored, b * 32 + 32)
                pool.sem_inc(more_free, 1)

        pool.wait_ge(xs_written, 16 * 2 * NT)
        pool.wait_ge(more_all, 1)
        pool.wait_ge(ys_stored[0], 32 * NE // 2)
        pool.wait_ge(ys_stored[1], 32 * NE // 2)
        for i in range(NT):
            if i >= 2:
                pool.wait_ge(comb_done, i - 1)
            for c in range(2):
                pool.indirect_dma_start(
                    out=zg[2 * (i % 2) + c][0:ROWS[i], :], out_offset=None, in_=ys[:, :],
                    in_offset=bass.IndirectOffsetOnAxis(ap=slotU[0:ROWS[i], c * NT + i:c * NT + i + 1], axis=0))\
                    .then_inc(gathered[i % 2], 16)

    @block.tensor
    def _(pe):
        ident = con("ident")
        emitted = [0]

        def take(kind, j):
            o = emitted[0]
            assert OUT[o][:2] == (kind, j), (OUT[o], kind, j)
            emitted[0] += 1
            if o >= 2:
                pe.wait_ge(proj_read[o % 2], o // 2)
            return o, o % 2

        def product(kind, j):
            o, slot = take(kind, j)
            n = OUT[o][2]
            pe.wait_ge(w_split, n + 1)
            hi, lo = whi[n % NSPLIT], wlo[n % NSPLIT]
            nk, rhi, rlo = {"uq": (2, cqn_hi, cqn_lo), "wa": (4, oa_hi, oa_lo), "wb": (8, ob_hi, ob_lo),
                            "wo": (8, mg_hi, mg_lo)}.get(kind, (KD, hT_hi, hT_lo))
            terms = [(k, w, r) for k in range(nk) for w, r in ((hi, rhi), (hi, rlo), (lo, rhi))]
            for m, (k, w, r) in enumerate(terms):
                at = (k * 4 + j % 4) * P if kind == "uq" else k * P
                for half in range(2):
                    mm = pe.matmul(proj[:, slot, half, 0:HALF], w[:, at:at + P], r[:, k, half * HALF:(half + 1) * HALF],
                                   start=(m == 0), stop=(m == len(terms) - 1))
            mm.then_inc(proj_done, 1)

        pe.wait_ge(const_loaded, 80)
        for i in range(NT):
            r = ROWS[i]
            pe.wait_ge(xn_ready, i + 1)
            if i >= 2:
                pe.wait_ge(hTf_ready, i - 1)
            for k in range(KD):
                at = (k % 4) * P
                mm = pe.transpose(bank[:, 2 * (i % 2) + k // 4, at:at + r], xn[i % 2][0:r, k * P:(k + 1) * P], ident[0:r, 0:r])
            mm.then_inc(xT_ready, 1)
        pe.wait_ge(hT_ready, NT)
        product("cq", 0)
        product("cq", 1)
        product("kv", 0)
        product("kr", 0)

        pe.wait_ge(consts_set, 1)
        pe.wait_ge(hTf_ready, NT)
        pe.wait_ge(proj_read[1], OUT_INDEX["cq", 1] // 2 + 1)
        pe.wait_ge(proj_read[0], OUT_INDEX["cq", 0] // 2 + 1)
        for half in range(2):
            for j in range(2):
                mm = pe.matmul(bank[:, half, 0:HALF], mean256[:, :], cqs[:, j, half * HALF:(half + 1) * HALF],
                               start=(j == 0), stop=(j == 1))
        mm.then_inc(lat_mean, 1)
        pe.wait_ge(proj_read[0], OUT_INDEX["kv", 0] // 2 + 1)
        for half in range(2):
            mm = pe.matmul(bank[:, 2 + half, 0:HALF], mean128[:, :], kvs[:, half * HALF:(half + 1) * HALF],
                           start=True, stop=True)
        mm.then_inc(lat_mean, 1)
        pe.wait_ge(caches_loaded, 32)
        pe.wait_ge(lat_rms, 2)
        for b in range(4):
            mm = pe.transpose(bank[:, 0, b * P:(b + 1) * P], caches[:, b // 2, b % 2, :], ident)
        mm.then_inc(cache_T, 1)
        pe.wait_ge(ckv_ready, 1)
        for i in range(4):
            pe.transpose(bank[:, 1, i * P:(i + 1) * P], ckvA[:, i * P:(i + 1) * P], ident)
        pe.transpose(bank[0:DEC, 2, 0:P], ckvA[:, SEQ + PAST:KEYS], ident)
        pe.wait_ge(kpe_ready, 1)
        for i in range(4):
            pe.transpose(bank[:, 2, P + i * ROPE:P + (i + 1) * ROPE], kpeA[64:96, i * P:(i + 1) * P], ident[64:96, 64:96])
        pe.transpose(bank[0:DEC, 2, 256:256 + ROPE], kpeA[64:96, SEQ + PAST:KEYS], ident[64:96, 64:96]).then_inc(out_T, 1)

        pe.wait_ge(cqn_ready, 1)
        for h in range(HEADS):
            product("uq", h)

        pe.wait_ge(kv_loaded, 32)
        pe.wait_ge(keys_ready, 1)
        for b in range(7):
            o, slot = take("V", b)
            r = P if b < 6 else DEC
            pe.matmul(proj[0:r, slot, 0, :], ckvA[:, b * P:b * P + r], w_kv[:, FF:2 * FF], start=True, stop=True)\
                .then_inc(proj_done, 1)

        def keys(hp):
            o, slot = take("K", hp)
            for half in range(2):
                mm = pe.matmul(proj[:, slot, half, 0:KEYS // 2], w_kv[:, hp * P:(hp + 1) * P],
                               ckvA[:, half * (KEYS // 2):(half + 1) * (KEYS // 2)], start=True, stop=True)
            mm.then_inc(proj_done, 1)

        def scores(u):
            hp, i, a = UNITS[u]
            h = 2 * hp + a
            r, q0, k0, n = unit_shape(i)
            if i == 0 and a == 0:
                ko = OUT_INDEX["K", hp]
                pe.wait_ge(proj_read[ko % 2], ko // 2 + 1)
                pe.wait_ge(q_ready, h + 2)
            if u == 0:
                pe.wait_ge(kcat_pe, 1)
                pe.wait_ge(out_copied, 1)
            if u >= 2:
                pe.wait_ge(exp_done, u - 1)
            mm = pe.matmul(bank[0:r, u % 2, 0:n], qT[0:QK, h, q0:q0 + r], kcat[hp % 2][0:QK, a, k0:k0 + n],
                           start=True, stop=(i == 4))
            if i < 4:
                mm = pe.matmul(bank[0:r, u % 2, n - P:n], qlow[0:1, :], khigh[0:1, :], start=False, stop=True)
            mm.then_inc(scores_ready, 1)

        def key_blocks(i):
            return [(b, P, b) for b in range(i + 1)] if i < 4 else [(0, P, 4), (1, P, 5), (2, DEC, 6)]

        def turn_probs(u):
            hp, i, a = UNITS[u]
            r = unit_shape(i)[0]
            pe.wait_ge(prob_ready, u + 1)
            if u >= 1:
                pe.wait_ge(probT_copied, u)
            for b, kr_, _ in key_blocks(i):
                mm = pe.transpose(bank[0:kr_, 2, b * r:(b + 1) * r], prob[u % 3][0:r, b * P:b * P + kr_], ident[0:r, 0:r])
            mm.then_inc(probT_done, 1)

        def pv(u):
            hp, i, a = UNITS[u]
            h = 2 * hp + a
            r = unit_shape(i)[0]
            v = u // 2
            pe.wait_ge(probT_copied, u + 1)
            if a == 0 and v >= 1:
                pe.wait_ge(oa_done, v)
            blocks = key_blocks(i)
            for b, kr_, vb in blocks:
                mm = pe.matmul(bank[64 * a:64 * a + 64, 3, 0:r],
                               V[0:kr_, vb, h * VD:(h + 1) * VD], probT[u % 2][0:kr_, b * r:(b + 1) * r],
                               start=(b == 0), stop=(b == len(blocks) - 1))
            mm.then_inc(pv_done, 1)

        keys(0)
        keys(1)
        NU = len(UNITS)
        for u in range(NU + 3):
            if u < NU:
                scores(u)
                if u % 10 == 0 and u // 10 in (1, 2):
                    keys(u // 10 + 1)
            if 2 <= u < NU + 2:
                turn_probs(u - 2)
            if u >= 3:
                pv(u - 3)

        for j in range(4):
            product("gq", j)
        for j in range(4):
            product("gk", j)
        pe.wait_ge(sides_loaded, 128)
        pe.wait_ge(oa_done, 20)
        for c in range(NT):
            L = ROWS[c]
            if c == 4:
                pe.wait_ge(gate_abs, 1)
                pe.wait_ge(gate_min, 1)
            pe.matmul(bank[0:L, c % 4, :], glr[0:RANK + 1, c * P:c * P + L], w_g2[0:RANK + 1, :], start=True, stop=True)\
                .then_inc(gate_done, 1)
        pe.wait_ge(gate_abs, NT)
        pe.wait_ge(gate_min, NT)
        for j in range(8):
            product("gv", j)
            o = OUT_INDEX["gv", j]
            pe.wait_ge(proj_read[o % 2], o // 2 + 1)
            if j >= 2:
                pe.wait_ge(vtok_ready, j - 1)
            for i in range(4):
                pe.transpose(bank[:, j % 2, i * P:(i + 1) * P], gvT[j % 2][:, i * P:(i + 1) * P], ident)
            pe.transpose(bank[0:DEC, 2 + j % 2, 0:P], gvT[j % 2][:, SEQ:TOK], ident).then_inc(gvT_done, 1)
        pe.wait_ge(vtok_ready, 8)

        for c in range(NT):
            L = ROWS[c]
            if c == 0:
                pe.wait_ge(la_ready, 2)
            else:
                pe.wait_ge(bS_ready, c)
            for h in range(GH):
                mm = pe.matmul(bank[:, 0, h * P:h * P + L], la[0:L, c, h * DK:(h + 1) * DK], con("tri16")[0:L, 0:L],
                               start=True, stop=True)
            mm.then_inc(cum_done, 1)
            if c < 4:
                product("gr", 2 * c)
                product("gr", 2 * c + 1)
            exK, exQ2, exKd, exQ1, _ = chunk_views(L)
            pe.wait_ge(kq_ready, c + 1)
            if c >= 1:
                pe.wait_ge(att_masked, c)
                pe.wait_ge(kdT_copied, c)
            for h in range(GH):
                for s in range(L // SUB):
                    mm = pe.matmul(bank[32 * s:32 * s + 32, 1, h * P:h * P + L], exQ2[:, h, s, :], exK[:, h, s, :],
                                   start=True, stop=True)
            mm.then_inc(att_done, 1)
            for h in range(GH):
                mm = pe.transpose(bank[0:L, 3, h * P:(h + 1) * P], exKd[:, h, :], ident)
            mm.then_inc(kdT_done, 1)
            pe.wait_ge(att_masked, c + 1)
            if c >= 1:
                pe.wait_ge(attT_copied, c)
            for h in range(GH):
                mm = pe.transpose(bank[0:L, 2, h * P:h * P + L], att[0:L, h, 0:L], ident[0:L, 0:L])
            mm.then_inc(attT_done, 1)
            o, slot = take("og", c)
            pe.wait_ge(attT_copied, c + 1)
            state = None
            if c == 4:
                pe.wait_ge(state_loaded, 16)
                state = S_smp
            elif c:
                pe.wait_ge(S_ready, c)
                state = S_st
            for n in range(8):
                h = n // 2
                out = proj[:, slot, n // 4, (n % 4) * P:(n % 4) * P + L]
                mm = pe.matmul(out, vtok[0:L, c, n * P:(n + 1) * P], attT[0:L, h, 0:L], start=True, stop=state is None)
                if state is not None:
                    mm = pe.matmul(out, state[:, h, (n % 2) * P:(n % 2 + 1) * P], exQ1[:, h, :], start=False, stop=True)
            mm.then_inc(proj_done, 1)
            o, slot = take("st", c)
            pe.wait_ge(kdT_copied, c + 1)
            for h in range(GH):
                mm = pe.matmul(proj[:, slot, h // 2, (h % 2) * DV:(h % 2 + 1) * DV], kdT[0:L, h, :],
                               vtok[0:L, c, h * DV:(h + 1) * DV], start=True, stop=True)
            mm.then_inc(proj_done, 1)

        for h in range(GH):
            o, slot = take("om", h)
            pe.wait_ge(osq_ready, h + 1)
            for half in range(2):
                for j in range(2):
                    mm = pe.matmul(proj[:, slot, half, 0:HALF], mean256[:, :], osq[h % 2][:, j, half * HALF:(half + 1) * HALF],
                                   start=(j == 0), stop=(j == 1))
            mm.then_inc(proj_done, 1)

        for j in range(8):
            product("ga", j)
            product("wa", j)
            product("gb", j)
            if j == 0:
                pe.wait_ge(ob_ready, GH)
            product("wb", j)
        pe.wait_ge(mg_ready, 8)
        for j in range(8):
            product("wo", j)
        o = OUT_INDEX["wo", 7]
        pe.wait_ge(proj_read[o % 2], o // 2 + 1)
        o -= 1
        pe.wait_ge(proj_read[o % 2], o // 2 + 1)

        def router(i):
            r = ROWS[i]
            pe.wait_ge(h2_ready, i + 1)
            if i >= 1:
                pe.wait_ge(h2T_copied, i)
            for k in range(KD):
                mm = pe.transpose(bank[:, 2 + k // 4, (k % 4) * P:(k % 4) * P + r], h2[0:r, i, k * P:(k + 1) * P], ident[0:r, 0:r])
            mm.then_inc(h2T_done, 1)
            o, slot = take("lg", i)
            pe.wait_ge(h2T_copied, i + 1)
            for k in range(KD):
                mm = pe.matmul(proj[0:r, slot, 0, 0:P], h2T[:, k, 0:r], w_rt[:, k, :], start=(k == 0), stop=(k == KD - 1))
            mm.then_inc(proj_done, 1)

        for i in range(NT):
            r = ROWS[i]
            if i >= 1:
                pe.wait_ge(x2_ready, i)
            for j in range(8):
                mm = pe.transpose(bank[0:r, j // 4, (j % 4) * P:(j % 4 + 1) * P], yT[:, j, i * P:i * P + r], ident)
            mm.then_inc(yrow_done, 1)
            if i >= 1:
                router(i - 1)
        router(NT - 1)
        pe.wait_ge(chosen, 1)
        pe.wait_ge(x2_ready, NT)
        Mf = picks[:, :, :].rearrange("p i e -> p (i e)")
        pe.matmul(bank[:, 0, 0:NT * NE], con("before"), Mf, start=True, stop=True)
        pe.matmul(bank[:, 1, 0:NT * NE], ones[:, :], Mf, start=True, stop=True).then_inc(ranks_done, 1)

        pe.wait_ge(proj_read[0], len([o for o in range(len(OUT)) if o % 2 == 0]))
        pe.wait_ge(proj_read[1], len([o for o in range(len(OUT)) if o % 2 == 1]))
        pe.wait_ge(slots_ready, 1)
        pe.wait_ge(h2T_copied, NT)

        def up(s, cols, wg, wu, done):
            for k in range(KD):
                pe.matmul(proj[0:SLOTS, s, 0, :], xsT[:, k, cols], wg[:, k * FF:(k + 1) * FF],
                          start=(k == 0), stop=(k == KD - 1))
                mm = pe.matmul(proj[64:64 + SLOTS, s, 0, :], xsT[:, k, cols], wu[:, k * FF:(k + 1) * FF],
                               start=(k == 0), stop=(k == KD - 1))
            mm.then_inc(done, 1)

        def turn_hidden(s, done):
            for k in range(4):
                mm = pe.transpose(bank[:, 2 + s, k * SLOTS:(k + 1) * SLOTS], hg[0:SLOTS, s, k * P:(k + 1) * P],
                                  ident[0:SLOTS, 0:SLOTS])
            mm.then_inc(done, 1)

        def down(s, wd, done):
            for k in range(4):
                pe.matmul(proj[0:SLOTS, s, 1, :], hT2[:, s, k, :], wd[:, k * D:k * D + FF], start=(k == 0), stop=(k == 3))
                mm = pe.matmul(proj[64:64 + SLOTS, s, 1, :], hT2[:, s, k, :], wd[:, k * D + FF:(k + 1) * D],
                               start=(k == 0), stop=(k == 3))
            mm.then_inc(done, 1)

        with pe.Fori(0, NE // 2) as q:
            pe.wait_ge(xs_loaded, q * 16 + 16)
            for k in range(KD):
                mm = pe.transpose(bank[:, k // 4, (k % 4) * P:(k % 4 + 1) * P], xsb[:, k * P:(k + 1) * P], ident)
            mm.then_inc(xsT_done, 1)
            pe.wait_ge(xsT_copied, q + 1)
            for s in range(2):
                pe.wait_ge(we_loaded[s][0], q * 16 + 16)
                pe.wait_ge(we_loaded[s][1], q * 16 + 16)
                up(s, slice(s * SLOTS, (s + 1) * SLOTS), we[s][0], we[s][1], up_done[s])
            for s in range(2):
                pe.wait_ge(consts_set, 1)
                pe.wait_ge(act_done[s], q + 1)
                turn_hidden(s, hT2_done[s])
                pe.wait_ge(hT2_copied[s], q + 1)
                pe.wait_ge(we_loaded[s][2], q * 16 + 16)
                down(s, we[s][2], down_done[s])

        pe.wait_ge(yo_ready[0], NE // 2)
        n_more = pe.value_load(meta[0:1, NOVER:NOVER + 1], min_val=0, max_val=NOVER)
        with pe.Fori(0, NOVER) as b:
            with pe.If(b < n_more):
                pe.wait_ge(more_x, b * 16 + 16)
                for k in range(KD):
                    mm = pe.transpose(bank[:, k // 4, (k % 4) * P:(k % 4 + 1) * P], xsb[:, k * P:(k + 1) * P], ident)
                mm.then_inc(more_xT, 1)
                pe.wait_ge(more_xT_copied, b + 1)
                pe.wait_ge(more_w, b * 48 + 48)
                up(0, slice(0, SLOTS), we[0][0], we[0][1], more_up)
                pe.wait_ge(consts_set, 1)
                pe.wait_ge(more_act, b + 1)
                turn_hidden(0, more_hT)
                pe.wait_ge(more_hT_copied, b + 1)
                down(0, we[0][2], more_down)

    @block.scalar
    def _(act):
        step = Steps(act, act_seq)

        def out_of(kind, j):
            o = OUT_INDEX[kind, j]
            act.wait_ge(proj_done, o + 1)
            return o, proj[:, o % 2, :, 0:HALF]

        def halves(ap):
            return ap.rearrange("p (a b) -> p a b", a=2)

        def root_mean_square(junk, src, out, done):
            step(nc.scalar.activation(junk, src, ACT.Square, accum_out=out))
            step.settle()
            nc.scalar.activation(out, out, ACT.Sqrt, scale=1.0 / D, bias=eps_col[0:out.shape[0], :]).then_inc(done, 1)

        act.wait_ge(consts_set, 1)
        for i in range(NT):
            r = ROWS[i]
            act.wait_ge(x_loaded[i], 16)
            if i >= 2:
                act.wait_ge(xT_ready, i - 1)
            root_mean_square(xn[i % 2][0:r, :], X[0:r, i, :], st_x[0:r, 0, i:i + 1], x_rms)
            if i >= 1:
                hT_high(nc, act, i - 1, hTf_ready, hT_hi, hT_f, hT_hi_ready)
        hT_high(nc, act, NT - 1, hTf_ready, hT_hi, hT_f, hT_hi_ready)

        for j in range(2):
            o, ps = out_of("cq", j)
            nc.scalar.copy(halves(cq[:, j, :]), ps)
            nc.scalar.activation(halves(cqs[:, j, :]), ps, ACT.Square).then_inc(proj_read[o % 2], 1)
        o, ps = out_of("kv", 0)
        nc.scalar.copy(halves(kvr[:, :]), ps)
        nc.scalar.activation(halves(kvs[:, :]), ps, ACT.Square).then_inc(proj_read[o % 2], 1)
        o, ps = out_of("kr", 0)
        act.wait_ge(consts_set, 1)
        nc.scalar.copy(halves(kr[:, :]), ps)
        nc.scalar.copy(halves(glr[0:RANK, :]), ps[0:RANK]).then_inc(proj_read[o % 2], 1)
        for n, root in enumerate((rq, rk)):
            act.wait_ge(lat_mean, n + 1)
            nc.scalar.activation(halves(root[:, :]), bank[:, 2 * n:2 * n + 2, 0:HALF], ACT.Sqrt, bias=eps_col[:, :]).then_inc(lat_rms, 1)
        for h in range(HEADS):
            o, ps = out_of("uq", h)
            nc.scalar.copy(halves(qT[:, h, :]), ps).then_inc(proj_read[o % 2], 1)
        for b in range(7):
            o, _ = out_of("V", b)
            r = P if b < 6 else DEC
            nc.scalar.copy(V[0:r, b, :], proj[0:r, o % 2, 0, :]).then_inc(proj_read[o % 2], 1)

        def keys(hp):
            o, _ = out_of("K", hp)
            if hp >= 2:
                act.wait_ge(scores_ready, 10 * (hp - 1))
            if hp == 0:
                act.wait_ge(cqn_ready, 1)
            for a in range(2):
                last = nc.scalar.copy(kcat[hp % 2][0:NOPE, a, :].rearrange("p (c k) -> p c k", c=2),
                                      proj[64 * a:64 * a + 64, o % 2, :, 0:KEYS // 2])
            last.then_inc(proj_read[o % 2], 1)

        keys(0)
        keys(1)

        def exps(u):
            hp, i, a = UNITS[u]
            r, _, _, n = unit_shape(i)
            act.wait_ge(negmax_ready, u + 1)
            if u >= 3:
                act.wait_ge(probT_done, u - 2)
            nc.scalar.activation(prob[u % 3][0:r, 0:n], bank[0:r, u % 2, 0:n], ACT.Exp, bias=stat[0:r, 1, u:u + 1],
                                 scale=ATT_SCALE, accum_out=stat[0:r, 2, u:u + 1]).then_inc(exp_done, 1)

        def copy_turned(u):
            _, i, _ = UNITS[u]
            n = unit_shape(i)[3]
            act.wait_ge(probT_done, u + 1)
            if u >= 2:
                act.wait_ge(pv_done, u - 1)
            if i < 4:
                nc.scalar.copy(probT[u % 2][:, 0:n], bank[:, 2, 0:n]).then_inc(probT_copied, 1)
            else:
                nc.scalar.copy(probT[u % 2][:, 0:2 * DEC], bank[:, 2, 0:2 * DEC])
                nc.scalar.copy(probT[u % 2][0:DEC, 2 * DEC:3 * DEC], bank[0:DEC, 2, 2 * DEC:3 * DEC]).then_inc(probT_copied, 1)

        NU = len(UNITS)
        for u in range(NU + 2):
            if u < NU:
                exps(u)
                if u % 10 == 0 and u // 10 in (1, 2):
                    keys(u // 10 + 1)
            if u >= 2:
                copy_turned(u - 2)

        act.wait_ge(pv_done, NU)
        act.wait_ge(oa_done, NU // 2)
        act.wait_ge(lat_stored, 64)
        for j in range(4):
            o, ps = out_of("gq", j)
            nc.scalar.mul(halves(gqk[:, j, :]), ps, float(DK) ** -0.5).then_inc(proj_read[o % 2], 1)
        for j in range(4):
            o, ps = out_of("gk", j)
            nc.scalar.copy(halves(gqk[:, 4 + j, :]), ps).then_inc(proj_read[o % 2], 1)
        for c in range(NT):
            L = ROWS[c]
            act.wait_ge(gate_min, c + 1)
            nc.scalar.activation(la[0:L, c, :], bank[0:L, c % 4, :], ACT.Abs).then_inc(gate_abs, 1)
        act.wait_ge(gate_abs, NT)
        for func, scale, bias in ((ACT.Exp, -1.0, 0.0), (ACT.Ln, 1.0, 1.0)):
            step(nc.scalar.activation(la[:, 0:4, :], la[:, 0:4, :], func, bias=bias, scale=scale))
            step(nc.scalar.activation(la[0:DEC, 4, :], la[0:DEC, 4, :], func, bias=bias, scale=scale))
            step.settle()
        nc.scalar.nop().then_inc(la_log, 1)
        for j in range(8):
            o, ps = out_of("gv", j)
            if j >= 2:
                act.wait_ge(gvT_done, j - 1)
            nc.scalar.copy(halves(gvT[j % 2][:, :]), ps).then_inc(proj_read[o % 2], 1)

        for c in range(NT):
            L = ROWS[c]
            exK, exQ2, exKd, exQ1, exD = chunk_views(L)
            act.wait_ge(cum_done, c + 1)
            if c == 0:
                act.wait_ge(la_ready, 2)
            if c >= 1:
                act.wait_ge(ex_ready, c)
            nc.scalar.copy(bS[:, :, 0:L], bank[:, 0, :].rearrange("p (h l) -> p h l", h=GH)[:, :, 0:L]).then_inc(bS_ready, 1)
            act.wait_ge(bS_ready, c + 1)
            act.wait_ge(ex_arg, c + 1)
            n = GH * (L // SUB) * L + 2 * GH * L
            nc.scalar.activation(ex[:, 0:n], ex[:, 0:n], ACT.Exp)
            nc.scalar.activation(exQ1, bS[:, :, 0:L], ACT.Exp)
            nc.scalar.activation(exD, bS[:, :, L - 1:L], ACT.Exp).then_inc(ex_ready, 1)
            if c < 4:
                for j in (2 * c, 2 * c + 1):
                    o, ps = out_of("gr", j)
                    nc.scalar.activation(halves(grs[:, j, :]), ps, ACT.Silu).then_inc(proj_read[o % 2], 1)
            act.wait_ge(kdT_done, c + 1)
            ost = OUT_INDEX["st", c - 1] if c else 0
            if c:
                act.wait_ge(proj_done, ost + 1)
            nc.scalar.copy(kdT[0:L, :, :], bank[0:L, 3, :].rearrange("p (h l) -> p h l", h=GH)).then_inc(kdT_copied, 1)
            act.wait_ge(attT_done, c + 1)
            nc.scalar.copy(attT[0:L, :, 0:L], bank[0:L, 2, :].rearrange("p (h l) -> p h l", h=GH)[:, :, 0:L])\
                .then_inc(attT_copied, 1)
            o, _ = out_of("og", c)
            src = proj[:, o % 2, :, :].rearrange("p a (n l) -> p (a n) l", n=4)[:, :, 0:L]
            nc.scalar.copy(gqk[:, :, c * P:c * P + L], src).then_inc(proj_read[o % 2], 1)

        def o_root(h):
            o, ps = out_of("om", h)
            if h >= 2:
                act.wait_ge(ob_ready, h - 1)
            nc.scalar.activation(halves(ors[h % 2][:, :]), ps, ACT.Sqrt, bias=eps_col[:, :]).then_inc(proj_read[o % 2], 1)

        ogo = OUT_INDEX["og", 4]
        act.wait_ge(proj_read[ogo % 2], ogo // 2 + 1)
        act.wait_ge(S_stored, 32)
        for h in range(GH):
            if h >= 2:
                act.wait_ge(proj_done, OUT_INDEX["om", h - 2] + 1)
            nc.scalar.activation(osq[h % 2][:, :, :], gqk[:, 2 * h:2 * h + 2, :], ACT.Square).then_inc(osq_ready, 1)
            if h >= 1:
                o_root(h - 1)
        o_root(GH - 1)

        for j in range(8):
            for n, kind in enumerate(("ga", "gb")):
                o, ps = out_of(kind, j)
                if j >= 1:
                    u = OUT_INDEX[("wa", "wb")[n], j - 1]
                    act.wait_ge(proj_read[u % 2], u // 2 + 1)
                nc.scalar.activation(halves(sg[n][:, :]), ps, ACT.Sigmoid).then_inc(proj_read[o % 2], 1)

        for j in range(8):
            o, ps = out_of("wo", j)
            nc.scalar.copy(halves(yT[:, j, :]), ps).then_inc(proj_read[o % 2], 1)

        def h2T_copy(i):
            act.wait_ge(h2T_done, i + 1)
            if i >= 1:
                act.wait_ge(proj_done, OUT_INDEX["lg", i - 1] + 1)
            r = ROWS[i]
            nc.scalar.copy(h2T[:, :, 0:r], bank[:, 2:4, :].rearrange("p a (k l) -> p (a k) l", k=4)[:, :, 0:r]).then_inc(h2T_copied, 1)

        for i in range(NT):
            r = ROWS[i]
            act.wait_ge(x2_ready, i + 1)
            root_mean_square(h2[0:r, i, :], X[0:r, i, :], st_x[0:r, 1, i:i + 1], x2_rms)
            if i >= 1:
                h2T_copy(i - 1)
        h2T_copy(NT - 1)
        for n in range(2):
            act.wait_ge(rt_exp_in, n + 1)
            v = (rG, rd)[n]
            nc.scalar.activation(v, v, ACT.Exp).then_inc(rt_exp_out, 1)

        def xsT_copy(r, done):
            nc.scalar.copy(xsT[:, :, 0:r], bank[:, 0:2, :].rearrange("p a (k l) -> p (a k) l", k=4)[:, :, 0:r]).then_inc(done, 1)

        with act.Fori(0, NE // 2) as q:
            act.wait_ge(xsT_done, q + 1)
            xsT_copy(P, xsT_copied)
            for s in range(2):
                act.wait_ge(up_done[s], q + 1)
                nc.scalar.activation(hg[0:SLOTS, s, :], proj[0:SLOTS, s, 0, :], ACT.Silu).then_inc(silu_done[s], 1)
        act.wait_ge(hT2_done[0], NE // 2)
        n_more = act.value_load(meta[0:1, NOVER:NOVER + 1], min_val=0, max_val=NOVER)
        with act.Fori(0, NOVER) as b:
            with act.If(b < n_more):
                act.wait_ge(more_xT, b + 1)
                xsT_copy(P, more_xT_copied)
                act.wait_ge(more_up, b + 1)
                nc.scalar.activation(hg[0:SLOTS, 0, :], proj[0:SLOTS, 0, 0, :], ACT.Silu).then_inc(more_silu, 1)

        for i in range(NT):
            r = ROWS[i]
            act.wait_ge(comb_done, i + 1)
            if i >= 2:
                act.wait_ge(y_stored[i % 2], 16 * (i // 2))
            root_mean_square(zo[i % 2][0:r, :], X[0:r, i, :], st_x[0:r, 2, i:i + 1], comb_rms)

    @block.vector
    def _(dve):
        step = Steps(dve, dve_seq)
        v = nc.vector

        def out_of(kind, j):
            o = OUT_INDEX[kind, j]
            dve.wait_ge(proj_done, o + 1)
            return o, proj[:, o % 2, :, 0:HALF]

        def halves(ap):
            return ap.rearrange("p (a b) -> p a b", a=2)

        def inverse(out, root):
            step(v.reciprocal(out, root))
            step.settle()

        v.memset(eps_col[:, :], EPS)
        v.memset(mean256[:, :], 1.0 / 256)
        v.memset(mean128[:, :], 1.0 / 128)
        v.memset(ones[:, :], 1.0)
        v.memset(qlow[0:1, 0:64], 1.0)
        v.memset(qlow[0:1, 64:P], 0.0)
        v.memset(khigh[0:1, 0:64], 0.0)
        v.memset(khigh[0:1, 64:P], -BIG)
        v.memset(w_rt[:, :, GROUPS + NE:], 0.0)
        v.memset(caches[:, 1, :, 0:64], 0.0)
        v.memset(caches[:, 1, :, 96:P], 0.0)
        v.memset(glr[0:RANK + 1, :], 1.0).then_inc(consts_set, 1)

        for i in range(NT):
            r = ROWS[i]
            dve.wait_ge(x_rms, i + 1)
            inverse(st_x[0:r, 3, i:i + 1], st_x[0:r, 0, i:i + 1])
            v.tensor_scalar(xn[i % 2][0:r, :], X[0:r, i, :], st_x[0:r, 3, i:i + 1], None, ALU.mult).then_inc(xn_ready, 1)
            dve.wait_ge(xT_ready, i + 1)
            dve.wait_ge(const_loaded, 80)
            if i >= 2:
                dve.wait_ge(hT_ready, i - 1)
            for b in range(2):
                src = bank[:, 2 * (i % 2) + b, :].rearrange("p (k c) -> p k c", k=4)[:, :, 0:r]
                last = v.tensor_tensor(hT_f[i % 2][:, 4 * b:4 * b + 4, 0:r], src,
                                       g_mix[:, 4 * b:4 * b + 4].unsqueeze(2).to_broadcast([P, 4, r]), ALU.mult)
            last.then_inc(hTf_ready, 1)

        dve.wait_ge(lat_rms, 1)
        inverse(rq[:, :], rq[:, :])
        for j in range(2):
            step(v.scalar_tensor_tensor(cq[:, j, :], cq[:, j, :], g_q[:, j:j + 1], rq[:, :], ALU.mult, ALU.mult))
        step.settle()
        step(v.tensor_copy(cqn_hi[:, :, :], cq[:, :, :]))
        step.settle()
        v.tensor_tensor(cqn_lo[:, :, :], cq[:, :, :], cqn_hi[:, :, :].bitcast(F32), ALU.subtract).then_inc(cqn_ready, 1)
        dve.wait_ge(lat_rms, 2)
        inverse(rk[:, :], rk[:, :])
        for dst, c0, n in ((0, 0, SEQ), (SEQ + PAST, SEQ, DEC)):
            last = v.scalar_tensor_tensor(ckvA[:, dst:dst + n], kvr[:, c0:c0 + n], g_kv[:, 0:1], rk[:, c0:c0 + n],
                                          ALU.mult, ALU.mult)
        last.then_inc(ckv_ready, 1)
        o = OUT_INDEX["kr", 0]
        dve.wait_ge(proj_read[o % 2], o // 2 + 1)

        def rotate(src, outs, done):
            step.settle()
            step(v.tensor_tensor(rtmp[64:96, 0, :], src[64:96], con("rope")[64:96], ALU.mult))
            step(v.tensor_tensor(rtmp[64:96, 1, :], src[96:128], con("rope")[96:128], ALU.mult))
            step.settle()
            for dst, c0, n in outs:
                last = v.tensor_tensor(dst, rtmp[64:96, 0, c0:c0 + n], rtmp[64:96, 1, c0:c0 + n], ALU.add)
            last.then_inc(done, 1)
            dve.wait_ge(done, rotated[done.name])
            rotated[done.name] += 1

        rotated = {kpe_ready.name: 1, q_ready.name: 1}
        rotate(kr[:, :], ((kpeA[64:96, 0:SEQ], 0, SEQ), (kpeA[64:96, SEQ + PAST:KEYS], SEQ, DEC)), kpe_ready)
        dve.wait_ge(cache_T, 1)
        v.tensor_copy(ckvA[:, SEQ:SEQ + PAST], bank[:, 0, 0:2 * P])
        v.tensor_copy(kpeA[64:96, SEQ:SEQ + PAST], bank[64:96, 0, 2 * P:4 * P]).then_inc(keys_ready, 1)
        dve.wait_ge(out_T, 1)
        v.tensor_copy(obuf[:, 0:4, :], bank[:, 1, :].rearrange("p (c d) -> p c d", c=4))
        v.tensor_copy(obuf[0:DEC, 4, :], bank[0:DEC, 2, 0:P])
        v.tensor_copy(kbuf[:, 0:4, :], bank[:, 2, P:2 * P].rearrange("p (c d) -> p c d", c=4))
        v.tensor_copy(kbuf[0:DEC, 4, :], bank[0:DEC, 2, 256:256 + ROPE]).then_inc(out_copied, 1)
        dve.wait_ge(keys_ready, 1)
        dve.wait_ge(cqn_ready, 1)
        for n in range(2):
            for a in range(2):
                last = v.tensor_copy(kcat[n][64:96, a, :], kpeA[64:96, :])
        last.then_inc(kcat_pe, 1)
        for h in range(HEADS):
            o = OUT_INDEX["uq", h]
            dve.wait_ge(proj_read[o % 2], o // 2 + 1)
            rotate(qT[:, h, :], ((qT[64:96, h, :], 0, TOK),), q_ready)

        def maximum(u):
            hp, i, a = UNITS[u]
            r, _, _, n = unit_shape(i)
            dve.wait_ge(scores_ready, u + 1)
            step(v.tensor_reduce(stat[0:r, 0, u:u + 1], bank[0:r, u % 2, 0:n], AX.X, ALU.max))
            step.settle()
            v.tensor_scalar(stat[0:r, 1, u:u + 1], stat[0:r, 0, u:u + 1], -ATT_SCALE, None, ALU.mult).then_inc(negmax_ready, 1)

        def normalise(u):
            hp, i, a = UNITS[u]
            r, _, _, n = unit_shape(i)
            dve.wait_ge(exp_done, u + 1)
            step(v.reciprocal(stat[0:r, 3, u:u + 1], stat[0:r, 2, u:u + 1]))
            step.settle()
            v.tensor_scalar(prob[u % 3][0:r, 0:n], prob[u % 3][0:r, 0:n], stat[0:r, 3, u:u + 1], None, ALU.mult)\
                .then_inc(prob_ready, 1)

        def copy_out(w):
            hp, i, _ = UNITS[2 * w]
            r, q0, _, _ = unit_shape(i)
            dve.wait_ge(pv_done, 2 * w + 2)
            src = bank[:, 3, 0:r]
            step(v.tensor_copy(oa_hi[:, hp, q0:q0 + r], src))
            step.settle()
            v.tensor_tensor(oa_lo[:, hp, q0:q0 + r], src, oa_hi[:, hp, q0:q0 + r].bitcast(F32), ALU.subtract).then_inc(oa_done, 1)

        NU = len(UNITS)
        for u in range(NU + 4):
            if u >= 5 and u % 2 == 1:
                copy_out((u - 5) // 2)
            if u < NU:
                maximum(u)
            if 1 <= u <= NU:
                normalise(u - 1)

        for c in range(NT):
            L = ROWS[c]
            dve.wait_ge(gate_done, c + 1)
            v.tensor_scalar(lmin[0:L, c, :], bank[0:L, c % 4, :], 0.0, None, ALU.min).then_inc(gate_min, 1)
        dve.wait_ge(gate_min, NT)
        dve.wait_ge(la_log, 1)
        v.tensor_tensor(la[:, 0:4, :], lmin[:, 0:4, :], la[:, 0:4, :], ALU.subtract).then_inc(la_ready, 1)
        v.tensor_tensor(la[0:DEC, 4, :], lmin[0:DEC, 4, :], la[0:DEC, 4, :], ALU.subtract).then_inc(la_ready, 1)
        for j in range(8):
            dve.wait_ge(gvT_done, j + 1)
            v.tensor_copy(vtok[:, 0:4, j * P:(j + 1) * P], bank[:, j % 2, :].rearrange("p (i l) -> p i l", i=4))
            v.tensor_copy(vtok[0:DEC, 4, j * P:(j + 1) * P], bank[0:DEC, 2 + j % 2, 0:P]).then_inc(vtok_ready, 1)

        for c in range(NT):
            L = ROWS[c]
            ns = L // SUB
            tok = slice(c * P, c * P + L)
            exK, exQ2, exKd, exQ1, exD = chunk_views(L)
            b = bS[:, :, 0:L]
            bs = b.rearrange("p h (s l) -> p h s l", l=SUB)
            mid = bs[:, :, :, SUB // 2 - 1:SUB // 2]
            q, k = gqk[:, 0:GH, tok], gqk[:, GH:2 * GH, tok]
            dve.wait_ge(bS_ready, c + 1)
            if c:
                dve.wait_ge(proj_done, OUT_INDEX["og", c - 1] + 1)
            for h in range(GH):
                step(v.tensor_tensor(exK[:, h], mid[:, h].to_broadcast([P, ns, L]),
                                     b[:, h].unsqueeze(1).to_broadcast([P, ns, L]), ALU.subtract))
            step.settle()
            step(v.tensor_scalar(ex[:, 0:GH * ns * L], ex[:, 0:GH * ns * L], EXP_CAP, None, ALU.min))
            step(v.tensor_tensor(exQ2, bs, mid.to_broadcast([P, GH, ns, SUB]), ALU.subtract))
            v.tensor_tensor(exKd, b[:, :, L - 1:L].to_broadcast([P, GH, L]), b, ALU.subtract).then_inc(ex_arg, 1)
            dve.wait_ge(ex_ready, c + 1)
            dve.wait_ge(ex_arg, c + 1)
            for h in range(GH):
                v.tensor_tensor(exK[:, h], exK[:, h], k[:, h].unsqueeze(1).to_broadcast([P, ns, L]), ALU.mult)
            v.tensor_tensor(exQ2, exQ2, q.rearrange("p h (s l) -> p h s l", l=SUB), ALU.mult)
            v.tensor_tensor(exQ1, exQ1, q, ALU.mult)
            v.tensor_tensor(exKd, exKd, k, ALU.mult).then_inc(kq_ready, 1)
            dve.wait_ge(att_done, c + 1)
            if c:
                dve.wait_ge(attT_done, c)
            v.tensor_tensor(att[0:L, :, 0:L], bank[0:L, 1, :].rearrange("p (h l) -> p h l", h=GH)[:, :, 0:L],
                            con("causal")[0:L, 0:L].unsqueeze(1).to_broadcast([L, GH, L]), ALU.mult).then_inc(att_masked, 1)
            o, _ = out_of("st", c)
            new = proj[:, o % 2, :, :].rearrange("p a (n v) -> p (a n) v", v=DV)
            state = S_smp if c == 4 else S_st
            if c == 0:
                step(v.tensor_copy(state[:, :, :], new))
                step.settle()
            else:
                if c == 4:
                    dve.wait_ge(state_loaded, 16)
                step.settle()
                for h in range(GH):
                    step(v.scalar_tensor_tensor(state[:, h, :], state[:, h, :], exD[:, h, :], new[:, h, :], ALU.mult, ALU.add))
                step.settle()
            v.nop().then_inc(S_ready, 1)
            step(v.nop())
            dve.wait_ge(S_ready, c + 1)
            dve.sem_inc(proj_read[o % 2], 1)

        for h in range(GH):
            o = OUT_INDEX["om", h]
            r2 = ors[h % 2]
            dve.wait_ge(proj_read[o % 2], o // 2 + 1)
            inverse(r2[:, :], r2[:, :])
            og = gqk[:, 2 * h:2 * h + 2, :]
            for n in range(2):
                step(v.scalar_tensor_tensor(og[:, n, :], og[:, n, :], g_gla[:, n:n + 1], r2[:, :], ALU.mult, ALU.mult))
            step.settle()
            step(v.tensor_tensor(og, og, grs[:, 2 * h:2 * h + 2, :], ALU.mult))
            step.settle()
            step(v.tensor_copy(ob_hi[:, 2 * h:2 * h + 2, :], og))
            step.settle()
            v.tensor_tensor(ob_lo[:, 2 * h:2 * h + 2, :], og, ob_hi[:, 2 * h:2 * h + 2, :].bitcast(F32), ALU.subtract)\
                .then_inc(ob_ready, 1)

        for j in range(8):
            for n, (gk_, wk_) in enumerate((("ga", "wa"), ("gb", "wb"))):
                g = OUT_INDEX[gk_, j]
                dve.wait_ge(proj_read[g % 2], g // 2 + 1)
                o, ps = out_of(wk_, j)
                dst = (msum[j % 2], mtmp)[n]
                v.tensor_tensor(halves(dst[:, :]), ps, halves(sg[n][:, :]), ALU.mult).then_inc(proj_read[o % 2], 1)
                dve.wait_ge(proj_read[o % 2], o // 2 + 1)
            step(v.tensor_tensor(mtmp[:, :], mtmp[:, :], msum[j % 2][:, :], ALU.add))
            step.settle()
            step(v.tensor_copy(mg_hi[:, j, :], mtmp[:, :]))
            step.settle()
            v.tensor_tensor(mg_lo[:, j, :], mtmp[:, :], mg_hi[:, j, :].bitcast(F32), ALU.subtract).then_inc(mg_ready, 1)
            dve.wait_ge(mg_ready, j + 1)

        dve.wait_ge(proj_done, OUT_INDEX["wo", 7] + 1)
        step(v.memset(LG[:, :, :], 0.0))
        step.settle()

        def logits(i):
            r = ROWS[i]
            o, _ = out_of("lg", i)
            v.tensor_tensor(LG[0:r, i, :], proj[0:r, o % 2, 0, 0:GROUPS + NE], b_rt[0:r, :], ALU.add).then_inc(proj_read[o % 2], 1)

        dve.wait_ge(sides_loaded, 128)
        for i in range(NT):
            r = ROWS[i]
            dve.wait_ge(yrow_done, i + 1)
            dve.wait_ge(x_loaded[i], 32)
            xi = X[0:r, i, :]
            v.tensor_tensor(xi.rearrange("p (a b) -> p a b", a=2), xi.rearrange("p (a b) -> p a b", a=2), bank[0:r, 0:2, :],
                            ALU.add).then_inc(x2_ready, 1)
            dve.wait_ge(x2_rms, i + 1)
            inverse(st_x[0:r, 4, i:i + 1], st_x[0:r, 1, i:i + 1])
            v.scalar_tensor_tensor(h2[0:r, i, :], xi, st_x[0:r, 4, i:i + 1], g_ffn[0:r, :], ALU.mult, ALU.mult).then_inc(h2_ready, 1)
            if i >= 1:
                logits(i - 1)
        logits(NT - 1)
        o = OUT_INDEX["lg", NT - 1]
        for o in (o, o - 1):
            dve.wait_ge(proj_read[o % 2], o // 2 + 1)

        def bc(ap, n):
            return ap.unsqueeze(2).to_broadcast([P, NT, n])

        def row(name, n):
            return con(name).unsqueeze(1).to_broadcast([P, NT, n])

        def run(ins):
            step(ins)
            step.settle()

        def first_max(out, val, m, iota, n):
            run(v.tensor_tensor(out, val, bc(m, n), ALU.is_equal))
            run(v.tensor_tensor(out, out, row(iota, n), ALU.mult))
            run(v.tensor_reduce(r5[2], out, AX.X, ALU.min))
            run(v.tensor_tensor(out, row(iota, n), bc(r5[2], n), ALU.is_equal))

        G_, E_l = LG[:, :, 0:GROUPS], LG[:, :, GROUPS:]
        run(v.tensor_reduce(r5[0], G_, AX.X, ALU.max))
        v.tensor_tensor(rG, G_, bc(r5[0], GROUPS), ALU.subtract).then_inc(rt_exp_in, 1)
        first_max(rOG, G_, r5[0], "iota4", GROUPS)
        run(v.tensor_scalar(rPen, rOG, 1.0, BIG, ALU.subtract, ALU.mult))
        for i in range(NT):
            em = rE[:, i, :].rearrange("p (g e) -> p g e", g=GROUPS)
            src = E_l[:, i, :].rearrange("p (g e) -> p g e", g=GROUPS)
            run(v.tensor_tensor(em, src, rOG[:, i, :].unsqueeze(2).to_broadcast([P, GROUPS, PER_GROUP]), ALU.mult))
            run(v.tensor_tensor(em, em, rPen[:, i, :].unsqueeze(2).to_broadcast([P, GROUPS, PER_GROUP]), ALU.add))
        run(v.tensor_reduce(r5[0], rE, AX.X, ALU.max))
        first_max(O1, rE, r5[0], "iota32", NE)
        run(v.tensor_scalar(rT, O1, -2.0 * BIG, None, ALU.mult))
        run(v.tensor_tensor(rE, rE, rT, ALU.add))
        run(v.tensor_reduce(r5[1], rE, AX.X, ALU.max))
        first_max(O2, rE, r5[1], "iota32", NE)
        v.tensor_tensor(rd, r5[1], r5[0], ALU.subtract).then_inc(rt_exp_in, 1)
        run(v.tensor_tensor(rT, O1, O2, ALU.add))
        v.tensor_tensor(picks[:, :, :], rT, bc(con("valid"), NE), ALU.mult).then_inc(chosen, 1)
        dve.wait_ge(rt_exp_out, 2)
        run(v.tensor_reduce(r5[2], rG, AX.X, ALU.add))
        run(v.tensor_scalar(r5[3], rd, 1.0, None, ALU.add))
        run(v.tensor_tensor(r5[3], r5[3], r5[2], ALU.mult))
        run(v.reciprocal(gate[:, 0, :], r5[3]))
        run(v.tensor_tensor(gate[:, 1, :], gate[:, 0, :], rd, ALU.mult))

        dve.wait_ge(ranks_done, 1)
        totals = bank[:, 1, 0:NT * NE].rearrange("p (i e) -> p i e", i=NT)
        run(v.memset(base[:, 0, :], 0.0))
        for i in range(NT):
            run(v.tensor_tensor(base[:, i + 1, :], base[:, i, :], totals[:, i, :], ALU.add))
        run(v.tensor_tensor(rank, bank[:, 0, 0:NT * NE].rearrange("p (i e) -> p i e", i=NT), base[:, 0:NT, :], ALU.add))
        run(v.tensor_tensor(nb8, base[:, NT, :].unsqueeze(2).to_broadcast([P, NE, 8]),
                            con("steps").unsqueeze(1).to_broadcast([P, NE, 8]), ALU.is_gt))
        run(v.tensor_reduce(cum[0], nb8, AX.X, ALU.add))
        run(v.tensor_copy(nb, cum[0]))
        for n, sh in enumerate((1, 2, 4, 8, 16)):
            a, b_ = cum[n % 2], cum[(n + 1) % 2]
            step(v.tensor_copy(b_[:, 0:sh], a[:, 0:sh]))
            run(v.tensor_tensor(b_[:, sh:], a[:, sh:], a[:, 0:NE - sh], ALU.add))
        end = cum[1]
        run(v.tensor_tensor(cum[0], end, nb, ALU.subtract))
        run(v.tensor_scalar(cum[0], cum[0], float(SLOTS), float(NMAIN - SLOTS), ALU.mult, ALU.add))
        run(v.tensor_tensor(cum[0], cum[0], con("base"), ALU.subtract))
        run(v.tensor_scalar(rT, rank, float(SLOTS), None, ALU.is_ge))
        run(v.tensor_tensor(rT, rT, cum[0].unsqueeze(1).to_broadcast([P, NT, NE]), ALU.mult))
        run(v.tensor_tensor(rank, rank, row("base", NE), ALU.add))
        run(v.tensor_tensor(rank, rank, rT, ALU.add))
        for c, O in enumerate((O1, O2)):
            run(v.tensor_tensor(rT, O, rank, ALU.mult))
            run(v.tensor_reduce(r5[c], rT, AX.X, ALU.add))
            run(v.tensor_copy(slotU[:, c * NT:(c + 1) * NT], r5[c]))
        run(v.tensor_tensor(nbe, end[0:1, :].unsqueeze(1).to_broadcast([1, NOVER, NE]),
                            con("blocks", 1).unsqueeze(2).to_broadcast([1, NOVER, NE]), ALU.is_le))
        run(v.tensor_reduce(bef, nbe, AX.X, ALU.add))
        run(v.tensor_scalar(bef, bef, float(NE - 1), None, ALU.min))
        run(v.tensor_copy(meta[0:1, 0:NOVER], bef))
        v.tensor_copy(meta[0:1, NOVER:NOVER + 1], end[0:1, NE - 1:NE]).then_inc(slots_ready, 1)

        def gated(s, done):
            v.tensor_tensor(hg[0:SLOTS, s, :], hg[0:SLOTS, s, :], proj[64:64 + SLOTS, s, 0, :], ALU.mult).then_inc(done, 1)

        def hidden_copy(s, done):
            v.tensor_copy(hT2[:, s, :, :], bank[:, 2 + s, 0:4 * SLOTS].rearrange("p (k l) -> p k l", k=4)).then_inc(done, 1)

        with dve.Fori(0, NE // 2) as q:
            for s in range(2):
                dve.wait_ge(silu_done[s], q + 1)
                gated(s, act_done[s])
            for s in range(2):
                dve.wait_ge(hT2_done[s], q + 1)
                hidden_copy(s, hT2_copied[s])
                dve.wait_ge(down_done[s], q + 1)
                dve.wait_ge(yo_free[s], q + 1)
                v.tensor_copy(yo[:, s, :], proj[:, s, 1, :]).then_inc(yo_ready[s], 1)
        dve.wait_ge(ys_stored[0], NE // 2 * 32)
        n_more = dve.value_load(meta[0:1, NOVER:NOVER + 1], min_val=0, max_val=NOVER)
        with dve.Fori(0, NOVER) as b:
            with dve.If(b < n_more):
                dve.wait_ge(more_silu, b + 1)
                gated(0, more_act)
                dve.wait_ge(more_hT, b + 1)
                hidden_copy(0, more_hT_copied)
                dve.wait_ge(more_down, b + 1)
                v.tensor_copy(yo[:, 0, :], proj[:, 0, 1, :]).then_inc(more_yo, 1)

        dve.wait_ge(more_free, n_more + 1)
        v.memset(st_x[:, 5, :], 0.0).then_inc(more_all, 1)
        dve.wait_ge(more_all, 1)

        for i in range(NT):
            r = ROWS[i]
            xi = X[0:r, i, :]
            dve.wait_ge(gathered[i % 2], 32 * (i // 2 + 1))
            step(v.scalar_tensor_tensor(xi, zg[2 * (i % 2)][0:r, :], gate[0:r, 0, i:i + 1], xi, ALU.mult, ALU.add))
            step.settle()
            v.scalar_tensor_tensor(xi, zg[2 * (i % 2) + 1][0:r, :], gate[0:r, 1, i:i + 1], xi, ALU.mult, ALU.add).then_inc(comb_done, 1)
            dve.wait_ge(comb_rms, i + 1)
            inverse(st_x[0:r, 5, i:i + 1], st_x[0:r, 2, i:i + 1])
            v.scalar_tensor_tensor(zo[i % 2][0:r, :], xi, st_x[0:r, 5, i:i + 1], g_fin[0:r, :], ALU.mult, ALU.mult).then_inc(y_ready, 1)


INS = ["x_prompt", "x_sample", "cache_ckv", "cache_krope", "state_gla", "w_in", "w_uq", "w_ukv", "w_gate2", "b_gate2",
       "w_branch_a", "w_branch_b", "w_out", "g_norm_ffn", "w_router_group", "b_router_group", "w_router_expert",
       "b_router_expert", "w_exp_gate", "w_exp_up", "w_exp_down", "g_norm_final"]
OUTS = [("y_prompt", (1, SEQ, D)), ("y_sample", (1, DEC, D)), ("ckv_prompt", (1, 1, SEQ, KV_LORA)),
        ("krope_prompt", (1, 1, SEQ, ROPE)), ("gla_prompt", (1, 1, GH, DK, DV)), ("ckv_sample", (1, 1, DEC, KV_LORA)),
        ("krope_sample", (1, 1, DEC, ROPE)), ("gla_sample", (1, 1, GH, DK, DV))]


def kernel(**inputs):
    import concourse.bacc as bacc
    from concourse.bass_utils import run_bass_kernel_spmd

    nc = bacc.Bacc("TRN2", target_bir_lowering=False, num_devices=1)
    arrays = {n: np.ascontiguousarray(inputs[n]) for n in INS}
    arrays["shape_constants"] = shape_constants()
    for n, src in (("g_mix_cols", "g_norm_mix"), ("g_q_cols", "g_qnorm"), ("g_kv_cols", "g_kvnorm"), ("g_gla_cols", "g_gla_norm")):
        arrays[n] = np.ascontiguousarray(np.asarray(inputs[src]).reshape(-1, P).T)
    t = {n: nc.dram_tensor(f"in_{n}", a.shape, mybir.dt.from_np(a.dtype), kind="ExternalInput").ap() for n, a in arrays.items()}
    for n, shape in OUTS:
        t[n] = nc.dram_tensor(f"out_{n}", shape, F32, kind="ExternalOutput").ap()
    build(nc, t)
    r = run_bass_kernel_spmd(nc, [{f"in_{n}": a for n, a in arrays.items()}], core_ids=[0])
    return tuple(r.results[0][f"out_{n}"] for n, _ in OUTS)
```

```python
from contextlib import ExitStack

import numpy as np

import concourse.bass as bass
from concourse import mybir

ALU = mybir.AluOpType
ACT = mybir.ActivationFunctionType
AX = mybir.AxisListType
F32 = mybir.dt.float32
F32R = mybir.dt.float32r
BF16 = mybir.dt.bfloat16
U32 = mybir.dt.uint32
I32 = mybir.dt.int32

P = 128
D = 1024
SEQ, DEC, PAST = 512, 32, 256
TOK = SEQ + DEC
HALF = TOK // 2
NT = 5
ROWS = [P, P, P, P, DEC]
KD = D // P
EPS = 1e-6
HEADS, Q_LORA, KV_LORA, NOPE, ROPE, VD = 8, 256, 128, 64, 32, 64
QK = NOPE + ROPE
ATT_SCALE = float(1.0 / np.sqrt(QK))
GH, DK, DV, RANK = 4, 128, 256, 16
SUB = 32
GROUPS, PER_GROUP, NE, FF = 4, 8, 32, 512
SLOTS = 64
NMAIN = NE * SLOTS
NOVER = (2 * TOK) // (SLOTS + 1)
NSLOT = NMAIN + NOVER * SLOTS
KEYS = SEQ + PAST + DEC
BIG = 1e30
EXP_CAP = 80.0

COLS = {}
_c = 0
for _name, _n in (("cq", Q_LORA), ("kv", KV_LORA), ("kr", ROPE), ("gq", GH * DK), ("gk", GH * DK), ("gv", GH * DV),
                  ("lr", RANK), ("gr", GH * DV), ("ga", D), ("gb", D)):
    COLS[_name] = _c
    _c += _n

CONST_AT = {}
_c = 0
for _name, _n in (("ident", P), ("tri16", P), ("causal", P), ("before", P), ("rope", TOK), ("iota4", GROUPS),
                  ("iota32", NE), ("base", NE), ("steps", 8), ("blocks", NOVER), ("valid", NT)):
    CONST_AT[_name] = (_c, _n)
    _c += _n
NCONST = _c


def shape_constants():
    c = np.zeros((P, NCONST), np.float32)

    def put(name, a):
        at, n = CONST_AT[name]
        c[:, at:at + n] = a

    r = np.arange(P)
    put("ident", np.eye(P))
    put("tri16", (r[:, None] <= r[None, :]) / 16.0)
    put("causal", r[None, :] <= r[:, None])
    put("before", r[:, None] < r[None, :])
    half = ROPE // 2
    inv = np.float32(10000.0) ** (-np.arange(half, dtype=np.float32) / np.float32(half))
    pos = np.concatenate([np.arange(SEQ), PAST + np.arange(DEC)]).astype(np.float32)
    ang = (pos[None, :] * inv[:, None].astype(np.float32)).astype(np.float32)
    rope = np.zeros((P, TOK), np.float32)
    rope[64:80] = rope[80:96] = np.cos(ang)
    rope[96:112], rope[112:128] = -np.sin(ang), np.sin(ang)
    put("rope", rope)
    put("iota4", np.arange(GROUPS) - 64.0)
    put("iota32", np.arange(NE) - 64.0)
    put("base", np.arange(NE) * float(SLOTS))
    put("steps", np.arange(1, 9) * float(SLOTS))
    put("blocks", np.arange(NOVER) * 1.0)
    valid = np.ones((P, NT), np.float32)
    valid[DEC:, NT - 1] = 0.0
    put("valid", valid)
    return c


EARLY_GR = 4


def weight_tiles():
    t = [("cq", 0), ("cq", 1), ("kv", 0), ("kr", 0)] + [("gr", j) for j in range(EARLY_GR)] + [("uq", 0), ("uq", 1)]
    t += [("gq", j) for j in range(4)] + [("gk", j) for j in range(4)] + [("gv", j) for j in range(8)]
    t += [("gr", j) for j in range(EARLY_GR, 8)]
    for j in range(8):
        t += [("ga", j), ("wa", j), ("gb", j), ("wb", j)]
    t += [("wo", j) for j in range(8)]
    return t


WT = weight_tiles()
WT_INDEX = {w: n for n, w in enumerate(WT)}
NRAW, NSPLIT = 3, 2
NPAIR = HEADS // 2


def outputs():
    o = []
    for n, (k, j) in enumerate(WT):
        if (k == "gr" and j >= EARLY_GR) or (k, j) in (("ga", 0), ("wa", 0)):
            continue
        o += [(k, 4 * j + m, n) for m in range(4)] if k == "uq" else [(k, j, n)]
        if (k, j) == ("uq", 1):
            o += [("V", b, None) for b in range(7)] + [("K", hp, None) for hp in range(NPAIR)]
        if (k, j) == ("gv", 7):
            for c in range(NT):
                if c < 4:
                    o.append(("gr", EARLY_GR + c, WT_INDEX["gr", EARLY_GR + c]))
                o += [("og", c, None), ("st", c, None)]
            o += [("ga", 0, WT_INDEX["ga", 0]), ("om", 0, None), ("om", 1, None), ("wa", 0, WT_INDEX["wa", 0]),
                  ("om", 2, None), ("om", 3, None)]
    return o + [("x2", i, None) for i in (1, 2, 4)]


OUT = outputs()
OUT_INDEX = {(k, j): n for n, (k, j, _) in enumerate(OUT)}
LAST_OUT = {}
for _o, (_k, _j, _w) in enumerate(OUT):
    if _w is not None:
        LAST_OUT[_w] = _o


def n_loads(w):
    return {"kr": 4, "uq": 6}.get(w[0], 1)


UNITS = [(hp, i, a) for hp in range(HEADS // 2) for i in range(NT) for a in range(2)]


def unit_shape(i):
    if i < 4:
        return P, i * P, 0, P * (i + 1)
    return DEC, SEQ, SEQ, PAST + DEC


def split_columns(n):
    return 4 * P if WT[n][0] == "wa" else D


class Steps:

    def __init__(self, eng, sem):
        self.eng, self.sem, self.n = eng, sem, 0

    def __call__(self, ins):
        ins.then_inc(self.sem, 1)
        self.n += 1

    def settle(self):
        self.eng.wait_ge(self.sem, self.n)


def hT_high(nc, act, i, hTf_ready, hT_hi, hT_f, hT_hi_ready):
    act.wait_ge(hTf_ready, i + 1)
    nc.scalar.copy(hT_hi[:, :, i * P:i * P + ROWS[i]], hT_f[i % 2][:, :, 0:ROWS[i]]).then_inc(hT_hi_ready, 1)


def build(nc, t):
    ctx = ExitStack()
    with ctx:
        _build(nc, t, ctx)


def _build(nc, t, ctx):
    def sem(name):
        return ctx.enter_context(nc.semaphore(name))

    def flat(name):
        return t[name].rearrange("a b c -> (a b) c")

    BASE = 16512

    class Region:
        def __init__(self, at):
            self.at = at

        def __call__(self, name, shape, dt=F32, after=None):
            n = 1
            for s in shape[1:]:
                n *= s
            size = n * mybir.dt.size(dt)
            h = nc.alloc_sbuf_tensor_at(name, shape, dt, offset=self.at)
            self.at += (size + 31) // 32 * 32
            return h

    R = Region(BASE)
    X = R("x_rows", [P, NT, D])
    cst = R("cst", [P, NCONST])
    mean256 = R("mean256", [P, P])
    mean128 = R("mean128", [P, P])
    ones = R("ones", [P, P])
    eps_col = R("eps_col", [P, 1])
    qlow = R("qlow", [1, P], BF16)
    khigh = R("khigh", [1, P], BF16)
    g_mix = R("g_mix", [P, KD])
    g_q = R("g_q", [P, 2])
    g_kv = R("g_kv", [P, 1])
    g_gla = R("g_gla", [P, 2])
    g_ffn = R("g_ffn", [P, KD])
    g_fin = R("g_fin", [P, D])
    w_rt = R("w_rt", [P, KD, 64])
    b_rt = R("b_rt", [P, GROUPS + NE])
    w_g2 = R("w_g2", [RANK + 1, GH * DK])
    st_x = R("st_x", [P, 6, NT])
    meta = R("meta", [1, NOVER + 1], I32)
    slotU = R("slotU", [P, 2 * NT], U32)
    gate = R("gate", [P, 2, NT])
    RING = R.at
    raw = [R(f"raw{n}", [P, D]) for n in range(NRAW)]
    whi = [R(f"whi{n}", [P, D], F32R) for n in range(NSPLIT)]
    wlo = [R(f"wlo{n}", [P, D], F32R) for n in range(NSPLIT)]
    HT = R.at
    hT_hi = R("hT_hi", [P, KD, TOK], F32R)
    hT_lo = R("hT_lo", [P, KD, TOK], F32R)
    ARENA = R.at
    LAST = 229344

    A0 = Region(ARENA)
    xn = [A0(f"xn{n}", [P, D]) for n in range(2)]
    hT_f = [A0(f"hT_f{n}", [P, KD, P]) for n in range(2)]

    A = Region(ARENA)
    oa_hi = A("oa_hi", [P, 4, TOK], F32R)
    oa_lo = A("oa_lo", [P, 4, TOK], F32R)
    glr = A("glr", [RANK + 1, TOK])
    AFTER_OA = A.at
    w_kv = A("w_kv", [P, D])
    ckvA = A("ckvA", [P, KEYS])
    kpeA = A("kpeA", [P, KEYS])
    V = A("V", [P, 7, HEADS * VD])
    qT = A("qT", [P, HEADS, TOK])
    KC = A.at
    kcat = [A(f"kcat{n}", [P, 2, KEYS]) for n in range(2)]
    rtmp = A("rtmp", [P, 2, TOK])
    caches = A("caches", [P, 2, 2, P])
    obuf = A("obuf", [P, NT, KV_LORA])
    kbuf = A("kbuf", [P, NT, ROPE])
    SM = A.at
    cqn_hi = A("cqn_hi", [P, 2, TOK], F32R)
    cqn_lo = A("cqn_lo", [P, 2, TOK], F32R)
    kr = A("kr", [P, TOK])
    kvr = A("kvr", [P, TOK])
    kvs = A("kvs", [P, TOK])
    rk = A("rk", [P, TOK])
    zero = nc.alloc_sbuf_tensor_at("zero", [P, D], F32, offset=LAST - 4096)
    assert A.at <= LAST - 4096, A.at
    Q_ = Region(KC)
    cq = Q_("cq", [P, 2, TOK])
    cqs = Q_("cqs", [P, 2, TOK])
    rq = Q_("rq", [P, TOK])
    S_ = Region(SM)
    prob = [S_(f"prob{n}", [P, SEQ]) for n in range(3)]
    probT = [S_(f"probT{n}", [P, SEQ]) for n in range(2)]
    stat = S_("stat", [P, 4, len(UNITS)])

    G = Region(AFTER_OA)
    OG = G.at
    gqk = G("gqk", [P, 2 * GH, TOK])
    AFTER_OG = G.at
    gvT = [G(f"gvT{n}", [P, TOK]) for n in range(2)]
    vtok = G("vtok", [P, NT, GH * DV])
    la = G("la", [P, NT, GH * DK])
    GS = G.at
    S_st = G("S_st", [P, GH, DV])
    bS = G("bS", [P, GH, P])
    ex = G("ex", [P, GH * 4 * P + 2 * GH * P])
    exq = [G(f"exq{n}", [P, GH * P + GH]) for n in range(2)]
    att = G("att", [P, GH, P])
    kdT = G("kdT", [P, GH, P])
    attT = G("attT", [P, GH, P])
    assert G.at <= LAST - 4096, G.at
    S_smp = nc.alloc_sbuf_tensor_at("S_smp", [P, GH, DV], F32, offset=LAST - 4096)
    grs = nc.alloc_sbuf_tensor_at("grs", [P, 8, TOK], F32, offset=BASE)
    G2 = Region(GS)
    lmin = G2("lmin", [P, NT, GH * DK])

    N_ = Region(AFTER_OG)
    ob_lo = nc.alloc_sbuf_tensor_at("ob_lo", [P, 8, TOK], F32R, offset=OG)
    ob_hi = N_("ob_hi", [P, 8, TOK], F32R)
    sg = [N_(f"sg{n}", [P, TOK]) for n in range(2)]
    mtmp = N_("mtmp", [P, TOK])
    msum = N_("msum", [P, TOK])
    osq = [N_(f"osq{n}", [P, 2, TOK]) for n in range(2)]
    MG0 = N_.at
    assert N_.at <= GS
    ors = [nc.alloc_sbuf_tensor_at(f"ors{n}", [P, TOK], F32, offset=at) for n, at in enumerate((BASE + 8 * TOK * 4, AFTER_OA - TOK * 4))]
    MG = (LAST - 2 * 8 * TOK * 4) // 32 * 32
    YT = MG - 8 * TOK * 4
    assert MG >= MG0
    E_ = Region(YT)
    yT = E_("yT", [P, 8, TOK])
    mg_hi = E_("mg_hi", [P, 8, TOK], F32R)
    mg_lo = E_("mg_lo", [P, 8, TOK], F32R)
    F_ = Region(MG)
    h2 = F_("h2", [P, NT, D])
    lgT = F_("lgT", [64, TOK])
    F_.at += 4096 - TOK * 4
    RT = F_.at
    W_ = Region(HT)
    we = [[W_(f"we{s}_{n}", [P, 4096]) for n in range(3)] for s in range(2)]
    assert W_.at - 16384 <= YT and W_.at <= MG
    K_ = Region(RING)
    xsb = K_("xsb", [P, D])
    xsT = K_("xsT", [P, KD, P])
    hg = K_("hg", [P, 2, FF])
    hT2 = K_("hT2", [P, 2, 4, SLOTS])
    yo = K_("yo", [P, 2, FF])
    assert K_.at <= HT
    Z_ = Region(MG)
    zg = [Z_(f"zg{n}", [P, D]) for n in range(4)]
    zo = [Z_(f"zo{n}", [P, D]) for n in range(2)]
    assert Z_.at <= RT

    def con(name, rows=P):
        at, n = CONST_AT[name]
        return cst[0:rows, at:at + n]

    proj = ctx.enter_context(nc.psum_tensor("proj", [P, 2, 2, 512], F32))
    bank = ctx.enter_context(nc.psum_tensor("bank", [P, 4, 512], F32))

    xs = nc.dram_tensor("expert_rows", (NSLOT, D), F32, kind="Internal").ap()
    ys = nc.dram_tensor("expert_out", (NSLOT, D), F32, kind="Internal").ap()
    w_in, w_uq, w_ukv = flat("w_in"), flat("w_uq"), flat("w_ukv")
    w_a, w_b, w_o = flat("w_branch_a"), flat("w_branch_b"), flat("w_out")
    w_eg = t["w_exp_gate"].rearrange("a e (k p) f -> (a e) p k f", p=P)
    w_eu = t["w_exp_up"].rearrange("a e (k p) f -> (a e) p k f", p=P)
    w_ed = t["w_exp_down"].rearrange("a e (k p) f -> (a e) p k f", p=P)

    def x_src(i):
        return flat("x_prompt")[i * P:(i + 1) * P, :] if i < 4 else flat("x_sample")

    x_loaded = [sem(f"x_loaded{i}") for i in range(NT)]
    w_loaded = [sem(f"w_loaded{n}") for n in range(NRAW)]
    proj_read = [sem(f"proj_read{n}") for n in range(2)]
    gathered = [sem(f"gathered{n}") for n in range(2)]
    y_stored = [sem(f"y_stored{n}") for n in range(2)]
    we_loaded = [[sem(f"we_loaded{s}_{n}") for n in range(3)] for s in range(2)]
    up_done = [sem(f"up_done{s}") for s in range(2)]
    silu_done = [sem(f"silu_done{s}") for s in range(2)]
    act_done = [sem(f"act_done{s}") for s in range(2)]
    hT2_done = [sem(f"hT2_done{s}") for s in range(2)]
    hT2_copied = [sem(f"hT2_copied{s}") for s in range(2)]
    down_done = [sem(f"down_done{s}") for s in range(2)]
    yo_ready = [sem(f"yo_ready{s}") for s in range(2)]
    ys_stored = [sem(f"ys_stored{s}") for s in range(2)]
    x_rms = sem("x_rms")
    xn_ready = sem("xn_ready")
    xT_ready = sem("xT_ready")
    hTf_ready = sem("hTf_ready")
    hT_hi_ready = sem("hT_hi_ready")
    hT_ready = sem("hT_ready")
    w_high = sem("w_high")
    w_split = sem("w_split")
    proj_done = sem("proj_done")
    lat_mean = sem("lat_mean")
    lat_rms = sem("lat_rms")
    cqn_ready = sem("cqn_ready")
    ckv_ready = sem("ckv_ready")
    kpe_ready = sem("kpe_ready")
    q_ready = sem("q_ready")
    cache_T = sem("cache_T")
    keys_ready = sem("keys_ready")
    out_T = sem("out_T")
    out_copied = sem("out_copied")
    kcat_pe = sem("kcat_pe")
    scores_ready = sem("scores_ready")
    negmax_ready = sem("negmax_ready")
    exp_done = sem("exp_done")
    prob_ready = sem("prob_ready")
    probT_done = sem("probT_done")
    probT_copied = sem("probT_copied")
    pv_done = sem("pv_done")
    oa_done = sem("oa_done")
    gvT_done = sem("gvT_done")
    vtok_ready = sem("vtok_ready")
    gate_done = sem("gate_done")
    gate_abs = sem("gate_abs")
    gate_min = sem("gate_min")
    la_log = sem("la_log")
    la_ready = sem("la_ready")
    cum_done = sem("cum_done")
    bS_ready = sem("bS_ready")
    ex_arg = sem("ex_arg")
    ex_ready = sem("ex_ready")
    kq_ready = sem("kq_ready")
    att_done = sem("att_done")
    att_masked = sem("att_masked")
    attT_done = sem("attT_done")
    attT_copied = sem("attT_copied")
    kdT_done = sem("kdT_done")
    kdT_copied = sem("kdT_copied")
    S_ready = sem("S_ready")
    S_stored = sem("S_stored")
    osq_ready = sem("osq_ready")
    og_ready = sem("og_ready")
    ob_high = sem("ob_high")
    ob_ready = sem("ob_ready")
    mg_ready = sem("mg_ready")
    w_rt_ready = sem("w_rt_ready")
    x2T_read = sem("x2T_read")
    logits_done = sem("logits_done")
    lgT_copied = sem("lgT_copied")
    lg_done = sem("lg_done")
    x2_turned = sem("x2_turned")
    x2_squared = sem("x2_squared")
    x2_ready = sem("x2_ready")
    x2_rms = sem("x2_rms")
    x2_inv = sem("x2_inv")
    h2_ready = sem("h2_ready")
    rt_exp_in = sem("rt_exp_in")
    rt_exp_out = sem("rt_exp_out")
    chosen = sem("chosen")
    ranks_done = sem("ranks_done")
    slots_ready = sem("slots_ready")
    meta_ready = sem("meta_ready")
    zero_set = sem("zero_set")
    xs_zeroed = sem("xs_zeroed")
    xs_written = sem("xs_written")
    xs_loaded = sem("xs_loaded")
    xsT_done = sem("xsT_done")
    xsT_copied = sem("xsT_copied")
    more_x = sem("more_x")
    more_w = sem("more_w")
    more_xT = sem("more_xT")
    more_xT_copied = sem("more_xT_copied")
    more_up = sem("more_up")
    more_silu = sem("more_silu")
    more_act = sem("more_act")
    more_hT = sem("more_hT")
    more_hT_copied = sem("more_hT_copied")
    more_down = sem("more_down")
    more_yo = sem("more_yo")
    more_stored = sem("more_stored")
    more_free = sem("more_free")
    yo_free = [sem(f"yo_free{s}") for s in range(2)]
    comb_done = sem("comb_done")
    comb_rms = sem("comb_rms")
    y_ready = sem("y_ready")
    lat_stored = sem("lat_stored")
    const_loaded = sem("const_loaded")
    sides_loaded = sem("sides_loaded")
    kv_loaded = sem("kv_loaded")
    caches_loaded = sem("caches_loaded")
    state_loaded = sem("state_loaded")
    consts_set = sem("consts_set")
    act_seq, dve_seq = sem("act_seq"), sem("dve_seq")

    def chunk_views(L, c):
        ns = L // SUB
        n0 = GH * ns * L
        n1 = GH * L

        def part(at, n):
            return ex[:, at:at + n]
        late = exq[c % 2]
        return (part(0, n0).rearrange("p (h s l) -> p h s l", h=GH, s=ns),
                part(n0, n1).rearrange("p (h s l) -> p h s l", h=GH, s=ns),
                part(n0 + n1, n1).rearrange("p (h l) -> p h l", h=GH),
                late[:, 0:n1].rearrange("p (h l) -> p h l", h=GH),
                late[:, GH * P:GH * P + GH].rearrange("p (h l) -> p h l", h=GH))

    T_ = Region(RT)
    LG = T_("LG", [P, NT, GROUPS + NE])
    r5 = [T_(f"r5_{n}", [P, NT])[:, :] for n in range(4)]
    rG = T_("rG", [P, NT, GROUPS])[:, :, :]
    rOG = T_("rOG", [P, NT, GROUPS])[:, :, :]
    rPen = T_("rPen", [P, NT, GROUPS])[:, :, :]
    rE = T_("rE", [P, NT, NE])[:, :, :]
    rT = T_("rT", [P, NT, NE])[:, :, :]
    O1 = T_("O1", [P, NT, NE])[:, :, :]
    O2 = T_("O2", [P, NT, NE])[:, :, :]
    picks = T_("picks", [P, NT, NE])
    rank = T_("rank", [P, NT, NE])[:, :, :]
    base = T_("tile_base", [P, NT + 1, NE])
    rd = T_("rd", [P, NT])[:, :]
    cum = [T_(f"cum{n}", [P, NE])[:, :] for n in range(2)]
    nb = T_("nb", [P, NE])[:, :]
    nb8 = T_("nb8", [P, NE, 8])[:, :, :]
    nbe = T_("nbe", [1, NOVER, NE])[:, :, :]
    bef = T_("bef", [1, NOVER])[:, :]
    assert T_.at <= LAST, T_.at

    def x2_source(i):
        return bank[:, 0:2, :] if i in (0, 3) else proj[:, OUT_INDEX["x2", i] % 2, :, :]

    block = ctx.enter_context(nc.Block())

    @block.sync
    def _(sp):
        def weight_source(n):
            kind, j = WT[n]
            dst = raw[n % NRAW]
            if kind == "kr":
                d3 = dst[:, :].rearrange("p (k c) -> p k c", k=KD)
                src = w_in.rearrange("(k p) c -> p k c", p=P)
                lr, k0 = COLS["lr"], COLS["kr"]
                return [(d3[:, :, 0:64], src[:, :, lr:lr + 64]), (d3[:, :, 64:96], src[:, :, k0:k0 + 32]),
                        (d3[:, :, 96:112], src[:, :, k0 + 16:k0 + 32]), (d3[:, :, 112:128], src[:, :, k0:k0 + 16])]
            if kind == "uq":
                d4 = dst[:, :].rearrange("p (k h c) -> p k h c", k=2, h=4)
                src = w_uq.rearrange("(k p) (h c) -> p k h c", p=P, c=QK)
                return [p for k in range(2) for p in (
                    (d4[:, k, :, 0:96], src[:, k, 4 * j:4 * j + 4, :]),
                    (d4[:, k, :, 96:112], src[:, k, 4 * j:4 * j + 4, 80:96]),
                    (d4[:, k, :, 112:128], src[:, k, 4 * j:4 * j + 4, 64:80]))]
            w = {"wa": w_a, "wb": w_b, "wo": w_o}.get(kind, w_in)
            k = {"wa": 4}.get(kind, KD)
            c0 = COLS.get(kind, 0) + j * P
            return [(dst[:, 0:k * P].rearrange("p (k c) -> p k c", k=k),
                     w.rearrange("(k p) c -> p k c", p=P)[:, :, c0:c0 + P])]

        def load_weights(n):
            if n >= NRAW:
                sp.wait_ge(w_split, n - NRAW + 1)
            for dst, src in weight_source(n):
                sp.dma_start(dst, src).then_inc(w_loaded[n % NRAW], 16)

        for i in range(NT):
            sp.dma_start(X[0:ROWS[i], i, :], x_src(i)).then_inc(x_loaded[i], 16)
            if i == 0:
                sp.dma_start(cst[:, :], t["shape_constants"]).then_inc(const_loaded, 16)
                sp.dma_start(g_mix[:, :], t["g_mix_cols"]).then_inc(const_loaded, 16)
                sp.dma_start(g_q[:, :], t["g_q_cols"]).then_inc(const_loaded, 16)
                sp.dma_start(g_kv[:, :], t["g_kv_cols"]).then_inc(const_loaded, 16)
                sp.dma_start(g_gla[:, :], t["g_gla_cols"]).then_inc(const_loaded, 16)
                sp.dma_start(g_ffn[:, :], t["g_ffn_cols"]).then_inc(const_loaded, 16)
        for n in range(NRAW):
            load_weights(n)
        for part in range(2):
            sp.dma_start(w_kv[:, part * FF:(part + 1) * FF].rearrange("p (h c) -> p h c", c=NOPE),
                         w_ukv.rearrange("p (h t c) -> p t h c", t=2, c=NOPE)[:, part]).then_inc(kv_loaded, 16)
        sp.dma_start(caches[:, 0, :, :], t["cache_ckv"].rearrange("a b (c p) d -> p (a b c) d", p=P)).then_inc(caches_loaded, 16)
        sp.dma_start(caches[:, 1, :, 64:96], t["cache_krope"].rearrange("a b (c p) d -> p (a b c) d", p=P)).then_inc(caches_loaded, 16)
        sp.dma_start(w_g2[0:RANK, :], flat("w_gate2")).then_inc(sides_loaded, 16)
        sp.dma_start(w_g2[RANK:RANK + 1, :], t["b_gate2"]).then_inc(sides_loaded, 16)
        sp.dma_start(g_fin[:, :], t["g_norm_final"].rearrange("(a d) -> a d", a=1).to_broadcast([P, D])).then_inc(sides_loaded, 16)
        sp.dma_start(b_rt[:, 0:GROUPS], t["b_router_group"].to_broadcast([P, GROUPS])).then_inc(sides_loaded, 16)
        sp.dma_start(b_rt[:, GROUPS:], t["b_router_expert"].to_broadcast([P, NE])).then_inc(sides_loaded, 16)
        sp.dma_start(w_rt[:, :, 0:GROUPS], flat("w_router_group").rearrange("(k p) c -> p k c", p=P)).then_inc(sides_loaded, 16)
        sp.dma_start(w_rt[:, :, GROUPS:GROUPS + NE], flat("w_router_expert").rearrange("(k p) c -> p k c", p=P)).then_inc(sides_loaded, 16)
        for n in range(NRAW, len(WT)):
            load_weights(n)
            if n == WT_INDEX["gq", 2]:
                sp.wait_ge(out_copied, 1)
                sp.dma_start(t["ckv_prompt"].rearrange("a b (c p) d -> p (a b c) d", p=P), obuf[:, 0:4, :]).then_inc(lat_stored, 16)
                sp.dma_start(t["ckv_sample"].rearrange("a b p d -> (a b p) d"), obuf[0:DEC, 4, :]).then_inc(lat_stored, 16)
                sp.dma_start(t["krope_prompt"].rearrange("a b (c p) d -> p (a b c) d", p=P), kbuf[:, 0:4, :]).then_inc(lat_stored, 16)
                sp.dma_start(t["krope_sample"].rearrange("a b p d -> (a b p) d"), kbuf[0:DEC, 4, :]).then_inc(lat_stored, 16)
            if n == WT_INDEX["gv", 5]:
                sp.wait_ge(xs_zeroed, 32)
                sp.dma_start(S_smp[:, :, :], t["state_gla"].rearrange("a b h p v -> p (a b h) v")).then_inc(state_loaded, 16)
            if n == WT_INDEX["wa", 0]:
                sp.wait_ge(S_ready, 4)
                sp.dma_start(t["gla_prompt"].rearrange("a b h p v -> p (a b h) v"), S_st[:, :, :]).then_inc(S_stored, 16)
                sp.wait_ge(S_ready, 5)
                sp.dma_start(t["gla_sample"].rearrange("a b h p v -> p (a b h) v"), S_smp[:, :, :]).then_inc(S_stored, 16)
            if n == WT_INDEX["gb", 1]:
                sp.wait_ge(ob_ready, GH)
                for i in range(NT):
                    sp.dma_start(X[0:ROWS[i], i, :], x_src(i)).then_inc(x_loaded[i], 16)

        def load_expert(s, part, e):
            w = (w_eg, w_eu, w_ed)[part]
            k = (KD, KD, 4)[part]
            sp.dma_start(we[s][part][:, :].rearrange("p (k f) -> p k f", k=k),
                         w[bass.ds(e, 1)].rearrange("o p k f -> (o p) k f")).then_inc(we_loaded[s][part], 16)

        sp.wait_ge(proj_done, OUT_INDEX["wb", 7] + 1)
        sp.wait_ge(mg_ready, 8)
        for s in range(2):
            for part in range(3):
                if (s, part) == (1, 2):
                    sp.wait_ge(x2_ready, NT)
                load_expert(s, part, s)
        sp.wait_ge(xs_written, 16 * 2 * NT)
        sp.wait_ge(proj_done, OUT_INDEX["wo", 7] + 1)
        sp.dma_start(xsb[:, :], xs[0:P, :]).then_inc(xs_loaded, 16)
        with sp.Fori(0, NE // 2 - 1) as q:
            sp.wait_ge(xsT_done, q + 1)
            sp.dma_start(xsb[:, :], xs[bass.ds(q * P + P, P), :]).then_inc(xs_loaded, 16)
            for s in range(2):
                sp.wait_ge(up_done[s], q + 1)
                load_expert(s, 0, q * 2 + 2 + s)
                load_expert(s, 1, q * 2 + 2 + s)
                sp.wait_ge(down_done[s], q + 1)
                load_expert(s, 2, q * 2 + 2 + s)

        sp.wait_ge(down_done[1], NE // 2)
        sp.wait_ge(meta_ready, 1)
        n_more = sp.value_load(meta[0:1, NOVER:NOVER + 1], min_val=0, max_val=NOVER)
        with sp.Fori(0, NOVER) as b:
            with sp.If(b < n_more):
                e = sp.value_load(meta[0:1, bass.ds(b, 1)], min_val=0, max_val=NE - 1)
                sp.wait_ge(more_free, b + 1)
                sp.dma_start(xsb[0:SLOTS, :], xs[bass.ds(b * SLOTS + NMAIN, SLOTS), :]).then_inc(more_x, 16)
                for part in range(3):
                    w = (w_eg, w_eu, w_ed)[part]
                    sp.dma_start(we[0][part][:, :].rearrange("p (k f) -> p k f", k=(KD, KD, 4)[part]),
                                 w[bass.ds(e, 1)].rearrange("o p k f -> (o p) k f")).then_inc(more_w, 16)

        for i in range(NT):
            sp.wait_ge(y_ready, i + 1)
            dst = flat("y_prompt")[i * P:(i + 1) * P, :] if i < 4 else flat("y_sample")
            sp.dma_start(dst, zo[i % 2][0:ROWS[i], :]).then_inc(y_stored[i % 2], 16)
        sp.wait_ge(y_stored[0], 48)
        sp.wait_ge(y_stored[1], 32)
        sp.wait_ge(S_stored, 32)
        sp.wait_ge(lat_stored, 64)

    @block.gpsimd
    def _(pool):
        def split(n):
            c = split_columns(n)
            pool.wait_ge(w_high, n + 1)
            hi, lo = whi[n % NSPLIT], wlo[n % NSPLIT]
            nc.gpsimd.tensor_tensor(lo[:, 0:c], raw[n % NRAW][:, 0:c], hi[:, 0:c].bitcast(F32),
                                    ALU.subtract).then_inc(w_split, 1)

        nc.gpsimd.memset(zero[:, :], 0.0).then_inc(zero_set, 1)
        for i in range(NT):
            pool.wait_ge(hT_hi_ready, i + 1)
            tok = slice(i * P, i * P + ROWS[i])
            nc.gpsimd.tensor_tensor(hT_lo[:, :, tok], hT_f[i % 2][:, :, 0:ROWS[i]], hT_hi[:, :, tok].bitcast(F32),
                                    ALU.subtract).then_inc(hT_ready, 1)
        for n in range(len(WT)):
            split(n)
            if n == WT_INDEX["gb", 0]:
                for h in range(GH):
                    two = slice(2 * h, 2 * h + 2)
                    pool.wait_ge(ob_high, h + 1)
                    nc.gpsimd.tensor_tensor(ob_lo[:, two, :], gqk[:, two, :], ob_hi[:, two, :].bitcast(F32),
                                            ALU.subtract).then_inc(ob_ready, 1)
            if n == WT_INDEX["uq", 1]:
                pool.wait_ge(zero_set, 1)
                pool.dma_start(xs.rearrange("(p r) d -> p r d", p=P), zero[:, :].unsqueeze(1).to_broadcast([P, NSLOT // P, D]))\
                    .then_inc(xs_zeroed, 16)
                more = ys[NMAIN:NSLOT, :].rearrange("(p r) d -> p r d", p=P)
                pool.dma_start(more, zero[:, :].unsqueeze(1).to_broadcast([P, (NSLOT - NMAIN) // P, D])).then_inc(xs_zeroed, 16)

        pool.wait_ge(xs_zeroed, 32)
        pool.wait_ge(h2_ready, NT)
        pool.wait_ge(slots_ready, 2)
        for i in range(NT):
            for c in range(2):
                pool.indirect_dma_start(
                    out=xs[:, :], out_offset=bass.IndirectOffsetOnAxis(ap=slotU[0:ROWS[i], c * NT + i:c * NT + i + 1], axis=0),
                    in_=h2[0:ROWS[i], i, :], in_offset=None).then_inc(xs_written, 16)

        def store(s, row, ready, n, done):
            pool.wait_ge(ready, n)
            for half in range(2):
                pool.dma_start(ys[bass.ds(row, SLOTS), half * FF:(half + 1) * FF],
                               yo[64 * half:64 * half + 64, s, :]).then_inc(done, 16)

        for s in range(2):
            pool.sem_inc(yo_free[s], 1)
        pool.sem_inc(more_free, 1)
        with pool.Fori(0, NE // 2) as q:
            for s in range(2):
                store(s, q * P + s * SLOTS, yo_ready[s], q + 1, ys_stored[s])
            for s in range(2):
                pool.wait_ge(ys_stored[s], q * 32 + 32)
                pool.sem_inc(yo_free[s], 1)
        pool.wait_ge(meta_ready, 1)
        n_more = pool.value_load(meta[0:1, NOVER:NOVER + 1], min_val=0, max_val=NOVER)
        with pool.Fori(0, NOVER) as b:
            with pool.If(b < n_more):
                store(0, b * SLOTS + NMAIN, more_yo, b + 1, more_stored)
                pool.wait_ge(more_stored, b * 32 + 32)
                pool.sem_inc(more_free, 1)

        pool.wait_ge(xs_written, 16 * 2 * NT)
        pool.wait_ge(ys_stored[0], 32 * NE // 2)
        pool.wait_ge(ys_stored[1], 32 * NE // 2)
        for i in range(NT):
            if i >= 2:
                pool.wait_ge(comb_done, i - 1)
            for c in range(2):
                pool.indirect_dma_start(
                    out=zg[2 * (i % 2) + c][0:ROWS[i], :], out_offset=None, in_=ys[:, :],
                    in_offset=bass.IndirectOffsetOnAxis(ap=slotU[0:ROWS[i], c * NT + i:c * NT + i + 1], axis=0))\
                    .then_inc(gathered[i % 2], 16)

    @block.tensor
    def _(pe):
        ident = con("ident")
        emitted = [0]

        def take(kind, j):
            o = emitted[0]
            assert OUT[o][:2] == (kind, j), (OUT[o], kind, j)
            emitted[0] += 1
            if o >= 2:
                pe.wait_ge(proj_read[o % 2], o // 2)
            return o, o % 2

        def add_x(slot, j):
            for i in range(NT):
                r = ROWS[i]
                for half in range(2):
                    a, b = max(i * P, half * HALF), min(i * P + r, (half + 1) * HALF)
                    if a < b:
                        pe.matmul(proj[:, slot, half, a - half * HALF:b - half * HALF], X[0:r, i, j * P:(j + 1) * P],
                                  ident[0:r, a - i * P:b - i * P], start=False, stop=False)

        def product(kind, j):
            o, slot = take(kind, j)
            n = OUT[o][2]
            hi, lo = whi[n % NSPLIT], wlo[n % NSPLIT]
            nk, rhi, rlo = {"uq": (2, cqn_hi, cqn_lo), "wa": (4, oa_hi, oa_lo), "wb": (8, ob_hi, ob_lo),
                            "wo": (8, mg_hi, mg_lo)}.get(kind, (KD, hT_hi, hT_lo))
            terms = [(k, w, r) for k in range(nk) for w, r in ((hi, rhi), (hi, rlo), (lo, rhi))]
            pe.wait_ge(w_split, n + 1)
            for m, (k, w, r) in enumerate(terms):
                at = (k * 4 + j % 4) * P if kind == "uq" else k * P
                for half in range(2):
                    mm = pe.matmul(proj[:, slot, half, 0:HALF], w[:, at:at + P], r[:, k, half * HALF:(half + 1) * HALF],
                                   start=(m == 0), stop=(m == len(terms) - 1))
                if kind == "wo" and m == 0:
                    add_x(slot, j)
            mm.then_inc(proj_done, 1)

        pe.wait_ge(const_loaded, 96)
        for i in range(NT):
            r = ROWS[i]
            pe.wait_ge(xn_ready, i + 1)
            if i >= 2:
                pe.wait_ge(hTf_ready, i - 1)
            for k in range(KD):
                at = (k % 4) * P
                mm = pe.transpose(bank[:, 2 * (i % 2) + k // 4, at:at + r], xn[i % 2][0:r, k * P:(k + 1) * P], ident[0:r, 0:r])
            mm.then_inc(xT_ready, 1)
        pe.wait_ge(hT_ready, NT)
        product("cq", 0)
        product("cq", 1)
        product("kv", 0)
        product("kr", 0)
        product("gr", 0)

        pe.wait_ge(consts_set, 1)
        pe.wait_ge(hTf_ready, NT)
        pe.wait_ge(proj_read[1], OUT_INDEX["cq", 1] // 2 + 1)
        pe.wait_ge(proj_read[0], OUT_INDEX["cq", 0] // 2 + 1)
        for half in range(2):
            for j in range(2):
                mm = pe.matmul(bank[:, half, 0:HALF], mean256[:, :], cqs[:, j, half * HALF:(half + 1) * HALF],
                               start=(j == 0), stop=(j == 1))
        mm.then_inc(lat_mean, 1)
        pe.wait_ge(proj_read[0], OUT_INDEX["kv", 0] // 2 + 1)
        for half in range(2):
            mm = pe.matmul(bank[:, 2 + half, 0:HALF], mean128[:, :], kvs[:, half * HALF:(half + 1) * HALF],
                           start=True, stop=True)
        mm.then_inc(lat_mean, 1)
        product("gr", 1)
        pe.wait_ge(caches_loaded, 32)
        pe.wait_ge(lat_rms, 2)
        for b in range(4):
            mm = pe.transpose(bank[:, 0, b * P:(b + 1) * P], caches[:, b // 2, b % 2, :], ident)
        mm.then_inc(cache_T, 1)
        pe.wait_ge(ckv_ready, 1)
        for i in range(4):
            pe.transpose(bank[:, 1, i * P:(i + 1) * P], ckvA[:, i * P:(i + 1) * P], ident)
        pe.transpose(bank[0:DEC, 2, 0:P], ckvA[:, SEQ + PAST:KEYS], ident)
        pe.wait_ge(kpe_ready, 1)
        for i in range(4):
            pe.transpose(bank[:, 2, P + i * ROPE:P + (i + 1) * ROPE], kpeA[64:96, i * P:(i + 1) * P], ident[64:96, 64:96])
        pe.transpose(bank[0:DEC, 2, 256:256 + ROPE], kpeA[64:96, SEQ + PAST:KEYS], ident[64:96, 64:96]).then_inc(out_T, 1)

        product("gr", 2)
        product("gr", 3)
        pe.wait_ge(cqn_ready, 1)
        for h in range(HEADS):
            product("uq", h)

        pe.wait_ge(kv_loaded, 32)
        pe.wait_ge(keys_ready, 1)
        for b in range(7):
            o, slot = take("V", b)
            r = P if b < 6 else DEC
            pe.matmul(proj[0:r, slot, 0, :], ckvA[:, b * P:b * P + r], w_kv[:, FF:2 * FF], start=True, stop=True)\
                .then_inc(proj_done, 1)

        def keys(hp):
            o, slot = take("K", hp)
            for half in range(2):
                mm = pe.matmul(proj[:, slot, half, 0:KEYS // 2], w_kv[:, hp * P:(hp + 1) * P],
                               ckvA[:, half * (KEYS // 2):(half + 1) * (KEYS // 2)], start=True, stop=True)
            mm.then_inc(proj_done, 1)

        def scores(u):
            hp, i, a = UNITS[u]
            h = 2 * hp + a
            r, q0, k0, n = unit_shape(i)
            if i == 0 and a == 0:
                ko = OUT_INDEX["K", hp]
                pe.wait_ge(proj_read[ko % 2], ko // 2 + 1)
                pe.wait_ge(q_ready, h + 2)
            if u == 0:
                pe.wait_ge(kcat_pe, 1)
                pe.wait_ge(out_copied, 1)
            if u >= 2:
                pe.wait_ge(exp_done, u - 1)
            mm = pe.matmul(bank[0:r, u % 2, 0:n], qT[0:QK, h, q0:q0 + r], kcat[hp % 2][0:QK, a, k0:k0 + n],
                           start=True, stop=(i == 4))
            if i < 4:
                mm = pe.matmul(bank[0:r, u % 2, n - P:n], qlow[0:1, :], khigh[0:1, :], start=False, stop=True)
            mm.then_inc(scores_ready, 1)

        def key_blocks(i):
            return [(b, P, b) for b in range(i + 1)] if i < 4 else [(0, P, 4), (1, P, 5), (2, DEC, 6)]

        def turn_probs(u):
            hp, i, a = UNITS[u]
            r = unit_shape(i)[0]
            pe.wait_ge(prob_ready, u + 1)
            if u >= 1:
                pe.wait_ge(probT_copied, u)
            for b, kr_, _ in key_blocks(i):
                mm = pe.transpose(bank[0:kr_, 2, b * r:(b + 1) * r], prob[u % 3][0:r, b * P:b * P + kr_], ident[0:r, 0:r])
            mm.then_inc(probT_done, 1)

        def pv(u):
            hp, i, a = UNITS[u]
            h = 2 * hp + a
            r = unit_shape(i)[0]
            v = u // 2
            pe.wait_ge(probT_copied, u + 1)
            if a == 0 and v >= 1:
                pe.wait_ge(oa_done, v)
            blocks = key_blocks(i)
            for b, kr_, vb in blocks:
                mm = pe.matmul(bank[64 * a:64 * a + 64, 3, 0:r],
                               V[0:kr_, vb, h * VD:(h + 1) * VD], probT[u % 2][0:kr_, b * r:(b + 1) * r],
                               start=(b == 0), stop=(b == len(blocks) - 1))
            mm.then_inc(pv_done, 1)

        keys(0)
        keys(1)
        NU = len(UNITS)
        for u in range(NU + 3):
            if u < NU:
                scores(u)
                if u % 10 == 0 and u // 10 in (1, 2):
                    keys(u // 10 + 1)
            if 2 <= u < NU + 2:
                turn_probs(u - 2)
            if u >= 3:
                pv(u - 3)

        for j in range(4):
            product("gq", j)
        for j in range(4):
            product("gk", j)
        pe.wait_ge(sides_loaded, 112)
        pe.wait_ge(oa_done, 20)
        for c in range(NT):
            L = ROWS[c]
            if c == 4:
                pe.wait_ge(gate_abs, 1)
                pe.wait_ge(gate_min, 1)
            pe.matmul(bank[0:L, c % 4, :], glr[0:RANK + 1, c * P:c * P + L], w_g2[0:RANK + 1, :], start=True, stop=True)\
                .then_inc(gate_done, 1)
        pe.wait_ge(gate_abs, NT)
        pe.wait_ge(gate_min, NT)
        def turn_values(j):
            o = OUT_INDEX["gv", j]
            pe.wait_ge(proj_read[o % 2], o // 2 + 1)
            if j >= 2:
                pe.wait_ge(vtok_ready, j - 1)
            for i in range(4):
                pe.transpose(bank[:, j % 2, i * P:(i + 1) * P], gvT[j % 2][:, i * P:(i + 1) * P], ident)
            pe.transpose(bank[0:DEC, 2 + j % 2, 0:P], gvT[j % 2][:, SEQ:TOK], ident).then_inc(gvT_done, 1)

        for j in range(8):
            product("gv", j)
            if j >= 1:
                turn_values(j - 1)
        turn_values(7)
        pe.wait_ge(vtok_ready, 8)

        def decays(c):
            L = ROWS[c]
            if c == 0:
                pe.wait_ge(la_ready, 2)
            else:
                pe.wait_ge(bS_ready, c)
            for h in range(GH):
                mm = pe.matmul(bank[:, 0, h * P:h * P + L], la[0:L, c, h * DK:(h + 1) * DK], con("tri16")[0:L, 0:L],
                               start=True, stop=True)
            mm.then_inc(cum_done, 1)

        decays(0)
        for c in range(NT):
            L = ROWS[c]
            exK, exQ2, exKd, exQ1, _ = chunk_views(L, c)
            pe.wait_ge(kq_ready, c + 1)
            if c >= 1:
                pe.wait_ge(att_masked, c)
                pe.wait_ge(kdT_copied, c)
            for h in range(GH):
                for s in range(L // SUB):
                    mm = pe.matmul(bank[32 * s:32 * s + 32, 1, h * P:h * P + L], exQ2[:, h, s, :], exK[:, h, s, :],
                                   start=True, stop=True)
            mm.then_inc(att_done, 1)
            for h in range(GH):
                mm = pe.transpose(bank[0:L, 3, h * P:(h + 1) * P], exKd[:, h, :], ident)
            mm.then_inc(kdT_done, 1)
            if c + 1 < NT:
                decays(c + 1)
            if c < 4:
                product("gr", EARLY_GR + c)
            pe.wait_ge(att_masked, c + 1)
            if c >= 1:
                pe.wait_ge(attT_copied, c)
            for h in range(GH):
                mm = pe.transpose(bank[0:L, 2, h * P:h * P + L], att[0:L, h, 0:L], ident[0:L, 0:L])
            mm.then_inc(attT_done, 1)
            o, slot = take("og", c)
            pe.wait_ge(attT_copied, c + 1)
            state = None
            if c == 4:
                pe.wait_ge(state_loaded, 16)
                state = S_smp
            elif c:
                pe.wait_ge(S_ready, c)
                state = S_st
            for n in range(8):
                h = n // 2
                out = proj[:, slot, n // 4, (n % 4) * P:(n % 4) * P + L]
                mm = pe.matmul(out, vtok[0:L, c, n * P:(n + 1) * P], attT[0:L, h, 0:L], start=True, stop=state is None)
                if state is not None:
                    mm = pe.matmul(out, state[:, h, (n % 2) * P:(n % 2 + 1) * P], exQ1[:, h, :], start=False, stop=True)
            mm.then_inc(proj_done, 1)
            o, slot = take("st", c)
            pe.wait_ge(kdT_copied, c + 1)
            for h in range(GH):
                mm = pe.matmul(proj[:, slot, h // 2, (h % 2) * DV:(h % 2 + 1) * DV], kdT[0:L, h, :],
                               vtok[0:L, c, h * DV:(h + 1) * DV], start=True, stop=True)
            mm.then_inc(proj_done, 1)

        def o_mean(h):
            o, slot = take("om", h)
            pe.wait_ge(osq_ready, h + 1)
            for half in range(2):
                for j in range(2):
                    mm = pe.matmul(proj[:, slot, half, 0:HALF], mean256[:, :], osq[h % 2][:, j, half * HALF:(half + 1) * HALF],
                                   start=(j == 0), stop=(j == 1))
            mm.then_inc(proj_done, 1)

        for j in range(8):
            product("ga", j)
            if j == 0:
                o_mean(0)
                o_mean(1)
            product("wa", j)
            if j == 0:
                o_mean(2)
                o_mean(3)
            product("gb", j)
            if j == 0:
                pe.wait_ge(ob_ready, GH)
            product("wb", j)
        pe.wait_ge(mg_ready, 8)
        for i in range(NT):
            pe.wait_ge(x_loaded[i], 32)
        pe.wait_ge(w_rt_ready, 1)

        def logits(j):
            pe.wait_ge(x2T_read, j + 1)
            for half in range(2):
                mm = pe.matmul(bank[0:64, 2 + half, 0:HALF], w_rt[:, j, :], yT[:, j, half * HALF:(half + 1) * HALF],
                               start=(j == 0), stop=(j == KD - 1))
            if j == KD - 1:
                mm.then_inc(logits_done, 1)

        for j in range(8):
            product("wo", j)
            if j >= 1:
                logits(j - 1)
        logits(7)

        def x2_rows(i):
            r = ROWS[i]
            if i in (0, 3):
                if i:
                    pe.wait_ge(x2_ready, 1)
                out = bank[:, 0:2, :]
            else:
                _, slot = take("x2", i)
                out = proj[:, slot, :, :]
            for j in range(8):
                mm = pe.transpose(out[0:r, j // 4, (j % 4) * P:(j % 4 + 1) * P], yT[:, j, i * P:i * P + r], ident)
            mm.then_inc(x2_turned, 1)

        for i in range(3):
            x2_rows(i)
        pe.wait_ge(lgT_copied, 1)
        for i in range(NT):
            r = ROWS[i]
            mm = pe.transpose(bank[0:r, 2, i * 64:(i + 1) * 64], lgT[:, i * P:i * P + r], ident[0:64, 0:64])
        mm.then_inc(lg_done, 1)
        for i in range(3, NT):
            x2_rows(i)
        pe.wait_ge(chosen, 1)
        pe.wait_ge(x2_ready, NT)
        Mf = picks[:, :, :].rearrange("p i e -> p (i e)")
        pe.matmul(bank[:, 0, 0:NT * NE], con("before"), Mf, start=True, stop=True)
        pe.matmul(bank[:, 1, 0:NT * NE], ones[:, :], Mf, start=True, stop=True).then_inc(ranks_done, 1)

        pe.wait_ge(proj_read[0], len([o for o in range(len(OUT)) if o % 2 == 0]))
        pe.wait_ge(proj_read[1], len([o for o in range(len(OUT)) if o % 2 == 1]))
        pe.wait_ge(slots_ready, 2)

        def up(s, cols, wg, wu, done):
            for k in range(KD):
                pe.matmul(proj[0:SLOTS, s, 0, :], xsT[:, k, cols], wg[:, k * FF:(k + 1) * FF],
                          start=(k == 0), stop=(k == KD - 1))
                mm = pe.matmul(proj[64:64 + SLOTS, s, 0, :], xsT[:, k, cols], wu[:, k * FF:(k + 1) * FF],
                               start=(k == 0), stop=(k == KD - 1))
            mm.then_inc(done, 1)

        def turn_hidden(s, done):
            for k in range(4):
                mm = pe.transpose(bank[:, 2 + s, k * SLOTS:(k + 1) * SLOTS], hg[0:SLOTS, s, k * P:(k + 1) * P],
                                  ident[0:SLOTS, 0:SLOTS])
            mm.then_inc(done, 1)

        def down(s, wd, done):
            for k in range(4):
                pe.matmul(proj[0:SLOTS, s, 1, :], hT2[:, s, k, :], wd[:, k * D:k * D + FF], start=(k == 0), stop=(k == 3))
                mm = pe.matmul(proj[64:64 + SLOTS, s, 1, :], hT2[:, s, k, :], wd[:, k * D + FF:(k + 1) * D],
                               start=(k == 0), stop=(k == 3))
            mm.then_inc(done, 1)

        with pe.Fori(0, NE // 2) as q:
            pe.wait_ge(xs_loaded, q * 16 + 16)
            for k in range(KD):
                mm = pe.transpose(bank[:, k // 4, (k % 4) * P:(k % 4 + 1) * P], xsb[:, k * P:(k + 1) * P], ident)
            mm.then_inc(xsT_done, 1)
            pe.wait_ge(xsT_copied, q + 1)
            for s in range(2):
                pe.wait_ge(we_loaded[s][0], q * 16 + 16)
                pe.wait_ge(we_loaded[s][1], q * 16 + 16)
                up(s, slice(s * SLOTS, (s + 1) * SLOTS), we[s][0], we[s][1], up_done[s])
            for s in range(2):
                pe.wait_ge(consts_set, 1)
                pe.wait_ge(act_done[s], q + 1)
                turn_hidden(s, hT2_done[s])
                pe.wait_ge(hT2_copied[s], q + 1)
                pe.wait_ge(we_loaded[s][2], q * 16 + 16)
                down(s, we[s][2], down_done[s])

        pe.wait_ge(yo_ready[0], NE // 2)
        pe.wait_ge(meta_ready, 1)
        n_more = pe.value_load(meta[0:1, NOVER:NOVER + 1], min_val=0, max_val=NOVER)
        with pe.Fori(0, NOVER) as b:
            with pe.If(b < n_more):
                pe.wait_ge(more_x, b * 16 + 16)
                for k in range(KD):
                    mm = pe.transpose(bank[:, k // 4, (k % 4) * P:(k % 4 + 1) * P], xsb[:, k * P:(k + 1) * P], ident)
                mm.then_inc(more_xT, 1)
                pe.wait_ge(more_xT_copied, b + 1)
                pe.wait_ge(more_w, b * 48 + 48)
                up(0, slice(0, SLOTS), we[0][0], we[0][1], more_up)
                pe.wait_ge(consts_set, 1)
                pe.wait_ge(more_act, b + 1)
                turn_hidden(0, more_hT)
                pe.wait_ge(more_hT_copied, b + 1)
                down(0, we[0][2], more_down)

    @block.scalar
    def _(act):
        step = Steps(act, act_seq)
        need = [0] * NRAW

        def high(n):
            c = split_columns(n)
            need[n % NRAW] += 16 * n_loads(WT[n])
            act.wait_ge(w_loaded[n % NRAW], need[n % NRAW])
            nc.scalar.copy(whi[n % NSPLIT][:, 0:c], raw[n % NRAW][:, 0:c]).then_inc(w_high, 1)

        def out_of(kind, j):
            o = OUT_INDEX[kind, j]
            act.wait_ge(proj_done, o + 1)
            w = OUT[o][2]
            if w is not None and LAST_OUT[w] == o and w + NSPLIT < len(WT):
                high(w + NSPLIT)
            return o, proj[:, o % 2, :, 0:HALF]

        def halves(ap):
            return ap.rearrange("p (a b) -> p a b", a=2)

        def root_mean_square(junk, src, out, done):
            step(nc.scalar.activation(junk, src, ACT.Square, accum_out=out))
            step.settle()
            nc.scalar.activation(out, out, ACT.Sqrt, scale=1.0 / D, bias=eps_col[0:out.shape[0], :]).then_inc(done, 1)

        act.wait_ge(consts_set, 1)
        for i in range(NT):
            r = ROWS[i]
            act.wait_ge(x_loaded[i], 16)
            if i >= 2:
                act.wait_ge(xT_ready, i - 1)
            root_mean_square(xn[i % 2][0:r, :], X[0:r, i, :], st_x[0:r, 0, i:i + 1], x_rms)
            if i >= 1:
                hT_high(nc, act, i - 1, hTf_ready, hT_hi, hT_f, hT_hi_ready)
        hT_high(nc, act, NT - 1, hTf_ready, hT_hi, hT_f, hT_hi_ready)
        for n in range(NSPLIT):
            high(n)

        def output_gate(j):
            o, ps = out_of("gr", j)
            nc.scalar.activation(halves(grs[:, j, :]), ps, ACT.Silu).then_inc(proj_read[o % 2], 1)

        for j in range(2):
            o, ps = out_of("cq", j)
            nc.scalar.copy(halves(cq[:, j, :]), ps)
            nc.scalar.activation(halves(cqs[:, j, :]), ps, ACT.Square).then_inc(proj_read[o % 2], 1)
        o, ps = out_of("kv", 0)
        nc.scalar.copy(halves(kvr[:, :]), ps)
        nc.scalar.activation(halves(kvs[:, :]), ps, ACT.Square).then_inc(proj_read[o % 2], 1)
        o, ps = out_of("kr", 0)
        act.wait_ge(consts_set, 1)
        nc.scalar.copy(halves(kr[:, :]), ps)
        nc.scalar.copy(halves(glr[0:RANK, :]), ps[0:RANK]).then_inc(proj_read[o % 2], 1)
        act.wait_ge(xn_ready, NT)
        output_gate(0)
        for n, root in enumerate((rq, rk)):
            act.wait_ge(lat_mean, n + 1)
            nc.scalar.activation(halves(root[:, :]), bank[:, 2 * n:2 * n + 2, 0:HALF], ACT.Sqrt, bias=eps_col[:, :]).then_inc(lat_rms, 1)
        for j in range(1, EARLY_GR):
            output_gate(j)
        for h in range(HEADS):
            o, ps = out_of("uq", h)
            nc.scalar.copy(halves(qT[:, h, :]), ps).then_inc(proj_read[o % 2], 1)
        for b in range(7):
            o, _ = out_of("V", b)
            r = P if b < 6 else DEC
            nc.scalar.copy(V[0:r, b, :], proj[0:r, o % 2, 0, :]).then_inc(proj_read[o % 2], 1)

        def keys(hp):
            o, _ = out_of("K", hp)
            if hp >= 2:
                act.wait_ge(scores_ready, 10 * (hp - 1))
            if hp == 0:
                act.wait_ge(cqn_ready, 1)
            for a in range(2):
                last = nc.scalar.copy(kcat[hp % 2][0:NOPE, a, :].rearrange("p (c k) -> p c k", c=2),
                                      proj[64 * a:64 * a + 64, o % 2, :, 0:KEYS // 2])
            last.then_inc(proj_read[o % 2], 1)

        keys(0)
        keys(1)

        def exps(u):
            hp, i, a = UNITS[u]
            r, _, _, n = unit_shape(i)
            act.wait_ge(negmax_ready, u + 1)
            if u >= 3:
                act.wait_ge(probT_done, u - 2)
            nc.scalar.activation(prob[u % 3][0:r, 0:n], bank[0:r, u % 2, 0:n], ACT.Exp, bias=stat[0:r, 1, u:u + 1],
                                 scale=ATT_SCALE, accum_out=stat[0:r, 2, u:u + 1]).then_inc(exp_done, 1)

        def copy_turned(u):
            _, i, _ = UNITS[u]
            n = unit_shape(i)[3]
            act.wait_ge(probT_done, u + 1)
            if u >= 2:
                act.wait_ge(pv_done, u - 1)
            if i < 4:
                nc.scalar.copy(probT[u % 2][:, 0:n], bank[:, 2, 0:n]).then_inc(probT_copied, 1)
            else:
                nc.scalar.copy(probT[u % 2][:, 0:2 * DEC], bank[:, 2, 0:2 * DEC])
                nc.scalar.copy(probT[u % 2][0:DEC, 2 * DEC:3 * DEC], bank[0:DEC, 2, 2 * DEC:3 * DEC]).then_inc(probT_copied, 1)

        NU = len(UNITS)
        for u in range(NU + 2):
            if u < NU:
                exps(u)
                if u % 10 == 0 and u // 10 in (1, 2):
                    keys(u // 10 + 1)
            if u >= 2:
                copy_turned(u - 2)

        act.wait_ge(pv_done, NU)
        act.wait_ge(oa_done, NU // 2)
        act.wait_ge(lat_stored, 64)
        for j in range(4):
            o, ps = out_of("gq", j)
            nc.scalar.mul(halves(gqk[:, j, :]), ps, float(DK) ** -0.5).then_inc(proj_read[o % 2], 1)
        for j in range(4):
            o, ps = out_of("gk", j)
            nc.scalar.copy(halves(gqk[:, 4 + j, :]), ps).then_inc(proj_read[o % 2], 1)
        for c in range(NT):
            L = ROWS[c]
            act.wait_ge(gate_min, c + 1)
            nc.scalar.activation(la[0:L, c, :], bank[0:L, c % 4, :], ACT.Abs).then_inc(gate_abs, 1)
        act.wait_ge(gate_abs, NT)
        for func, scale, bias in ((ACT.Exp, -1.0, 0.0), (ACT.Ln, 1.0, 1.0)):
            step(nc.scalar.activation(la[:, 0:4, :], la[:, 0:4, :], func, bias=bias, scale=scale))
            step(nc.scalar.activation(la[0:DEC, 4, :], la[0:DEC, 4, :], func, bias=bias, scale=scale))
            step.settle()
        nc.scalar.nop().then_inc(la_log, 1)
        for j in range(8):
            o, ps = out_of("gv", j)
            if j >= 2:
                act.wait_ge(gvT_done, j - 1)
            nc.scalar.copy(halves(gvT[j % 2][:, :]), ps).then_inc(proj_read[o % 2], 1)

        def copy_decays(c):
            L = ROWS[c]
            act.wait_ge(cum_done, c + 1)
            if c == 0:
                act.wait_ge(la_ready, 2)
            else:
                act.wait_ge(ex_ready, c)
            nc.scalar.copy(bS[:, :, 0:L], bank[:, 0, :].rearrange("p (h l) -> p h l", h=GH)[:, :, 0:L]).then_inc(bS_ready, 1)

        def exponentials(c):
            L = ROWS[c]
            _, _, _, exQ1, exD = chunk_views(L, c)
            act.wait_ge(bS_ready, c + 1)
            act.wait_ge(ex_arg, c + 1)
            if c >= 2:
                act.wait_ge(S_ready, c - 1)
            n = GH * (L // SUB) * L + 2 * GH * L
            nc.scalar.activation(ex[:, 0:n], ex[:, 0:n], ACT.Exp)
            nc.scalar.activation(exQ1, bS[:, :, 0:L], ACT.Exp)
            nc.scalar.activation(exD, bS[:, :, L - 1:L], ACT.Exp).then_inc(ex_ready, 1)

        copy_decays(0)
        exponentials(0)
        for c in range(NT):
            L = ROWS[c]
            act.wait_ge(kdT_done, c + 1)
            if c:
                act.wait_ge(proj_done, OUT_INDEX["st", c - 1] + 1)
            nc.scalar.copy(kdT[0:L, :, :], bank[0:L, 3, :].rearrange("p (h l) -> p h l", h=GH)).then_inc(kdT_copied, 1)
            if c + 1 < NT:
                copy_decays(c + 1)
            if c < 4:
                output_gate(EARLY_GR + c)
            act.wait_ge(attT_done, c + 1)
            nc.scalar.copy(attT[0:L, :, 0:L], bank[0:L, 2, :].rearrange("p (h l) -> p h l", h=GH)[:, :, 0:L])\
                .then_inc(attT_copied, 1)
            if c + 1 < NT:
                exponentials(c + 1)
            o, _ = out_of("og", c)
            src = proj[:, o % 2, :, :].rearrange("p a (n l) -> p (a n) l", n=4)[:, :, 0:L]
            nc.scalar.copy(gqk[:, :, c * P:c * P + L], src).then_inc(proj_read[o % 2], 1)

        def o_squares(h):
            if h >= 2:
                act.wait_ge(proj_done, OUT_INDEX["om", h - 2] + 1)
            nc.scalar.activation(osq[h % 2][:, :, :], gqk[:, 2 * h:2 * h + 2, :], ACT.Square).then_inc(osq_ready, 1)

        def o_root(h):
            o, ps = out_of("om", h)
            if h >= 2:
                act.wait_ge(og_ready, h - 1)
            nc.scalar.activation(halves(ors[h % 2][:, :]), ps, ACT.Sqrt, bias=eps_col[:, :]).then_inc(proj_read[o % 2], 1)

        def o_high(h):
            act.wait_ge(og_ready, h + 1)
            nc.scalar.copy(ob_hi[:, 2 * h:2 * h + 2, :], gqk[:, 2 * h:2 * h + 2, :]).then_inc(ob_high, 1)

        def gate_value(n, kind, j):
            o, ps = out_of(kind, j)
            if j >= 1:
                u = OUT_INDEX[("wa", "wb")[n], j - 1]
                act.wait_ge(proj_read[u % 2], u // 2 + 1)
            nc.scalar.activation(halves(sg[n][:, :]), ps, ACT.Sigmoid).then_inc(proj_read[o % 2], 1)

        ogo = OUT_INDEX["og", 4]
        act.wait_ge(proj_read[ogo % 2], ogo // 2 + 1)
        o_squares(0)
        o_squares(1)
        gate_value(0, "ga", 0)
        o_root(0)
        o_squares(2)
        o_root(1)
        o_squares(3)
        out_of("wa", 0)
        o_high(0)
        o_root(2)
        o_high(1)
        o_root(3)
        o_high(2)
        o_high(3)
        for j in range(8):
            if j:
                gate_value(0, "ga", j)
                out_of("wa", j)
            gate_value(1, "gb", j)
            out_of("wb", j)

        for j in range(8):
            o, ps = out_of("wo", j)
            nc.scalar.copy(halves(yT[:, j, :]), ps).then_inc(x2T_read, 1)
            act.wait_ge(x2T_read, j + 1)
            act.sem_inc(proj_read[o % 2], 1)
        act.wait_ge(logits_done, 1)
        nc.scalar.copy(halves(lgT[:, :]), bank[0:64, 2:4, 0:HALF]).then_inc(lgT_copied, 1)

        for i in range(NT):
            r = ROWS[i]
            act.wait_ge(x2_turned, i + 1)
            step(nc.scalar.activation(h2[0:r, i, :].rearrange("p (a b) -> p a b", a=2), x2_source(i)[0:r], ACT.Square,
                                      accum_out=st_x[0:r, 1, i:i + 1]))
            step.settle()
            act.sem_inc(x2_squared, 1)
        nc.scalar.activation(st_x[:, 1, :], st_x[:, 1, :], ACT.Sqrt, scale=1.0 / D, bias=eps_col[:, :]).then_inc(x2_rms, 1)
        act.wait_ge(x2_inv, 1)
        for i in range(NT):
            r = ROWS[i]
            act.wait_ge(x2_ready, i + 1)
            nc.scalar.mul(h2[0:r, i, :], X[0:r, i, :], st_x[0:r, 4, i:i + 1]).then_inc(h2_ready, 1)
        for n in range(2):
            act.wait_ge(rt_exp_in, n + 1)
            v = (rG, rd)[n]
            nc.scalar.activation(v, v, ACT.Exp).then_inc(rt_exp_out, 1)

        with act.Fori(0, NE // 2) as q:
            for s in range(2):
                act.wait_ge(up_done[s], q + 1)
                nc.scalar.activation(hg[0:SLOTS, s, :], proj[0:SLOTS, s, 0, :], ACT.Silu).then_inc(silu_done[s], 1)
        act.wait_ge(hT2_done[0], NE // 2)
        act.wait_ge(meta_ready, 1)
        n_more = act.value_load(meta[0:1, NOVER:NOVER + 1], min_val=0, max_val=NOVER)
        with act.Fori(0, NOVER) as b:
            with act.If(b < n_more):
                act.wait_ge(more_up, b + 1)
                nc.scalar.activation(hg[0:SLOTS, 0, :], proj[0:SLOTS, 0, 0, :], ACT.Silu).then_inc(more_silu, 1)

        for i in range(NT):
            r = ROWS[i]
            act.wait_ge(comb_done, i + 1)
            if i >= 2:
                act.wait_ge(y_stored[i % 2], 16 * (i // 2))
            root_mean_square(zo[i % 2][0:r, :], X[0:r, i, :], st_x[0:r, 2, i:i + 1], comb_rms)

    @block.vector
    def _(dve):
        step = Steps(dve, dve_seq)
        v = nc.vector

        def out_of(kind, j):
            o = OUT_INDEX[kind, j]
            dve.wait_ge(proj_done, o + 1)
            return o, proj[:, o % 2, :, 0:HALF]

        def halves(ap):
            return ap.rearrange("p (a b) -> p a b", a=2)

        def inverse(out, root):
            step(v.reciprocal(out, root))
            step.settle()

        v.memset(eps_col[:, :], EPS)
        v.memset(mean256[:, :], 1.0 / 256)
        v.memset(mean128[:, :], 1.0 / 128)
        v.memset(ones[:, :], 1.0)
        v.memset(qlow[0:1, 0:64], 1.0)
        v.memset(qlow[0:1, 64:P], 0.0)
        v.memset(khigh[0:1, 0:64], 0.0)
        v.memset(khigh[0:1, 64:P], -BIG)
        v.memset(w_rt[:, :, GROUPS + NE:], 0.0)
        v.memset(st_x[:, 1, :], 1.0)
        v.memset(caches[:, 1, :, 0:64], 0.0)
        v.memset(caches[:, 1, :, 96:P], 0.0)
        v.memset(glr[0:RANK + 1, :], 1.0).then_inc(consts_set, 1)

        for i in range(NT):
            r = ROWS[i]
            dve.wait_ge(x_rms, i + 1)
            inverse(st_x[0:r, 3, i:i + 1], st_x[0:r, 0, i:i + 1])
            v.tensor_scalar(xn[i % 2][0:r, :], X[0:r, i, :], st_x[0:r, 3, i:i + 1], None, ALU.mult).then_inc(xn_ready, 1)
            dve.wait_ge(xT_ready, i + 1)
            dve.wait_ge(const_loaded, 96)
            if i >= 2:
                dve.wait_ge(hT_ready, i - 1)
            for b in range(2):
                src = bank[:, 2 * (i % 2) + b, :].rearrange("p (k c) -> p k c", k=4)[:, :, 0:r]
                last = v.tensor_tensor(hT_f[i % 2][:, 4 * b:4 * b + 4, 0:r], src,
                                       g_mix[:, 4 * b:4 * b + 4].unsqueeze(2).to_broadcast([P, 4, r]), ALU.mult)
            last.then_inc(hTf_ready, 1)

        dve.wait_ge(lat_rms, 1)
        inverse(rq[:, :], rq[:, :])
        for j in range(2):
            step(v.scalar_tensor_tensor(cq[:, j, :], cq[:, j, :], g_q[:, j:j + 1], rq[:, :], ALU.mult, ALU.mult))
        step.settle()
        step(v.tensor_copy(cqn_hi[:, :, :], cq[:, :, :]))
        step.settle()
        v.tensor_tensor(cqn_lo[:, :, :], cq[:, :, :], cqn_hi[:, :, :].bitcast(F32), ALU.subtract).then_inc(cqn_ready, 1)
        dve.wait_ge(lat_rms, 2)
        inverse(rk[:, :], rk[:, :])
        for dst, c0, n in ((0, 0, SEQ), (SEQ + PAST, SEQ, DEC)):
            last = v.scalar_tensor_tensor(ckvA[:, dst:dst + n], kvr[:, c0:c0 + n], g_kv[:, 0:1], rk[:, c0:c0 + n],
                                          ALU.mult, ALU.mult)
        last.then_inc(ckv_ready, 1)
        o = OUT_INDEX["kr", 0]
        dve.wait_ge(proj_read[o % 2], o // 2 + 1)

        def rotate(src, outs, done):
            step.settle()
            step(v.tensor_tensor(rtmp[64:96, 0, :], src[64:96], con("rope")[64:96], ALU.mult))
            step(v.tensor_tensor(rtmp[64:96, 1, :], src[96:128], con("rope")[96:128], ALU.mult))
            step.settle()
            for dst, c0, n in outs:
                last = v.tensor_tensor(dst, rtmp[64:96, 0, c0:c0 + n], rtmp[64:96, 1, c0:c0 + n], ALU.add)
            last.then_inc(done, 1)
            dve.wait_ge(done, rotated[done.name])
            rotated[done.name] += 1

        rotated = {kpe_ready.name: 1, q_ready.name: 1}
        rotate(kr[:, :], ((kpeA[64:96, 0:SEQ], 0, SEQ), (kpeA[64:96, SEQ + PAST:KEYS], SEQ, DEC)), kpe_ready)
        dve.wait_ge(cache_T, 1)
        v.tensor_copy(ckvA[:, SEQ:SEQ + PAST], bank[:, 0, 0:2 * P])
        v.tensor_copy(kpeA[64:96, SEQ:SEQ + PAST], bank[64:96, 0, 2 * P:4 * P]).then_inc(keys_ready, 1)
        dve.wait_ge(out_T, 1)
        v.tensor_copy(obuf[:, 0:4, :], bank[:, 1, :].rearrange("p (c d) -> p c d", c=4))
        v.tensor_copy(obuf[0:DEC, 4, :], bank[0:DEC, 2, 0:P])
        v.tensor_copy(kbuf[:, 0:4, :], bank[:, 2, P:2 * P].rearrange("p (c d) -> p c d", c=4))
        v.tensor_copy(kbuf[0:DEC, 4, :], bank[0:DEC, 2, 256:256 + ROPE]).then_inc(out_copied, 1)
        dve.wait_ge(keys_ready, 1)
        dve.wait_ge(cqn_ready, 1)
        for n in range(2):
            for a in range(2):
                last = v.tensor_copy(kcat[n][64:96, a, :], kpeA[64:96, :])
        last.then_inc(kcat_pe, 1)
        for h in range(HEADS):
            o = OUT_INDEX["uq", h]
            dve.wait_ge(proj_read[o % 2], o // 2 + 1)
            rotate(qT[:, h, :], ((qT[64:96, h, :], 0, TOK),), q_ready)

        def maximum(u):
            hp, i, a = UNITS[u]
            r, _, _, n = unit_shape(i)
            dve.wait_ge(scores_ready, u + 1)
            step(v.tensor_reduce(stat[0:r, 0, u:u + 1], bank[0:r, u % 2, 0:n], AX.X, ALU.max))
            step.settle()
            v.tensor_scalar(stat[0:r, 1, u:u + 1], stat[0:r, 0, u:u + 1], -ATT_SCALE, None, ALU.mult).then_inc(negmax_ready, 1)

        def normalise(u):
            hp, i, a = UNITS[u]
            r, _, _, n = unit_shape(i)
            dve.wait_ge(exp_done, u + 1)
            step(v.reciprocal(stat[0:r, 3, u:u + 1], stat[0:r, 2, u:u + 1]))
            step.settle()
            v.tensor_scalar(prob[u % 3][0:r, 0:n], prob[u % 3][0:r, 0:n], stat[0:r, 3, u:u + 1], None, ALU.mult)\
                .then_inc(prob_ready, 1)

        def copy_out(w):
            hp, i, _ = UNITS[2 * w]
            r, q0, _, _ = unit_shape(i)
            dve.wait_ge(pv_done, 2 * w + 2)
            src = bank[:, 3, 0:r]
            step(v.tensor_copy(oa_hi[:, hp, q0:q0 + r], src))
            step.settle()
            v.tensor_tensor(oa_lo[:, hp, q0:q0 + r], src, oa_hi[:, hp, q0:q0 + r].bitcast(F32), ALU.subtract).then_inc(oa_done, 1)

        NU = len(UNITS)
        for u in range(NU + 4):
            if u >= 5 and u % 2 == 1:
                copy_out((u - 5) // 2)
            if u < NU:
                maximum(u)
            if 1 <= u <= NU:
                normalise(u - 1)

        for c in range(NT):
            L = ROWS[c]
            dve.wait_ge(gate_done, c + 1)
            v.tensor_scalar(lmin[0:L, c, :], bank[0:L, c % 4, :], 0.0, None, ALU.min).then_inc(gate_min, 1)
        dve.wait_ge(gate_min, NT)
        dve.wait_ge(la_log, 1)
        v.tensor_tensor(la[:, 0:4, :], lmin[:, 0:4, :], la[:, 0:4, :], ALU.subtract).then_inc(la_ready, 1)
        v.tensor_tensor(la[0:DEC, 4, :], lmin[0:DEC, 4, :], la[0:DEC, 4, :], ALU.subtract).then_inc(la_ready, 1)
        for j in range(8):
            dve.wait_ge(gvT_done, j + 1)
            v.tensor_copy(vtok[:, 0:4, j * P:(j + 1) * P], bank[:, j % 2, :].rearrange("p (i l) -> p i l", i=4))
            v.tensor_copy(vtok[0:DEC, 4, j * P:(j + 1) * P], bank[0:DEC, 2 + j % 2, 0:P]).then_inc(vtok_ready, 1)

        def exponents(c):
            L = ROWS[c]
            ns = L // SUB
            exK, exQ2, exKd, _, _ = chunk_views(L, c)
            b = bS[:, :, 0:L]
            bs = b.rearrange("p h (s l) -> p h s l", l=SUB)
            mid = bs[:, :, :, SUB // 2 - 1:SUB // 2]
            dve.wait_ge(bS_ready, c + 1)
            if c:
                dve.wait_ge(att_done, c)
                dve.wait_ge(kdT_done, c)
            for h in range(GH):
                step(v.tensor_tensor(exK[:, h], mid[:, h].to_broadcast([P, ns, L]),
                                     b[:, h].unsqueeze(1).to_broadcast([P, ns, L]), ALU.subtract))
            step.settle()
            step(v.tensor_scalar(ex[:, 0:GH * ns * L], ex[:, 0:GH * ns * L], EXP_CAP, None, ALU.min))
            step(v.tensor_tensor(exQ2, bs, mid.to_broadcast([P, GH, ns, SUB]), ALU.subtract))
            v.tensor_tensor(exKd, b[:, :, L - 1:L].to_broadcast([P, GH, L]), b, ALU.subtract).then_inc(ex_arg, 1)

        def decayed(c):
            L = ROWS[c]
            ns = L // SUB
            tok = slice(c * P, c * P + L)
            exK, exQ2, exKd, exQ1, _ = chunk_views(L, c)
            q, k = gqk[:, 0:GH, tok], gqk[:, GH:2 * GH, tok]
            dve.wait_ge(ex_ready, c + 1)
            dve.wait_ge(ex_arg, c + 1)
            for h in range(GH):
                v.tensor_tensor(exK[:, h], exK[:, h], k[:, h].unsqueeze(1).to_broadcast([P, ns, L]), ALU.mult)
            v.tensor_tensor(exQ2, exQ2, q.rearrange("p h (s l) -> p h s l", l=SUB), ALU.mult)
            v.tensor_tensor(exQ1, exQ1, q, ALU.mult)
            v.tensor_tensor(exKd, exKd, k, ALU.mult).then_inc(kq_ready, 1)

        def new_state(c):
            _, _, _, _, exD = chunk_views(ROWS[c], c)
            o, _ = out_of("st", c)
            new = proj[:, o % 2, :, :].rearrange("p a (n v) -> p (a n) v", v=DV)
            state = S_smp if c == 4 else S_st
            if c == 0:
                step(v.tensor_copy(state[:, :, :], new))
            else:
                if c == 4:
                    dve.wait_ge(state_loaded, 16)
                for h in range(GH):
                    step(v.scalar_tensor_tensor(state[:, h, :], state[:, h, :], exD[:, h, :], new[:, h, :], ALU.mult, ALU.add))
            step.settle()
            v.nop().then_inc(S_ready, 1)
            dve.sem_inc(proj_read[o % 2], 1)

        dve.wait_ge(sides_loaded, 112)
        v.tensor_tensor(w_rt[:, :, :], w_rt[:, :, :], g_ffn[:, :].unsqueeze(2).to_broadcast([P, KD, 64]), ALU.mult)\
            .then_inc(w_rt_ready, 1)

        exponents(0)
        decayed(0)
        for c in range(NT):
            L = ROWS[c]
            dve.wait_ge(att_done, c + 1)
            if c:
                dve.wait_ge(attT_done, c)
            v.tensor_tensor(att[0:L, :, 0:L], bank[0:L, 1, :].rearrange("p (h l) -> p h l", h=GH)[:, :, 0:L],
                            con("causal")[0:L, 0:L].unsqueeze(1).to_broadcast([L, GH, L]), ALU.mult).then_inc(att_masked, 1)
            if c + 1 < NT:
                exponents(c + 1)
                decayed(c + 1)
            new_state(c)

        def gated_output(h):
            o = OUT_INDEX["om", h]
            r2 = ors[h % 2]
            dve.wait_ge(proj_read[o % 2], o // 2 + 1)
            inverse(r2[:, :], r2[:, :])
            og = gqk[:, 2 * h:2 * h + 2, :]
            for n in range(2):
                step(v.scalar_tensor_tensor(og[:, n, :], og[:, n, :], g_gla[:, n:n + 1], r2[:, :], ALU.mult, ALU.mult))
            step.settle()
            v.tensor_tensor(og, og, grs[:, 2 * h:2 * h + 2, :], ALU.mult).then_inc(og_ready, 1)

        def branch(n, j):
            g = OUT_INDEX[("ga", "gb")[n], j]
            dve.wait_ge(proj_read[g % 2], g // 2 + 1)
            o, ps = out_of(("wa", "wb")[n], j)
            dst = (msum, mtmp)[n]
            v.tensor_tensor(halves(dst[:, :]), ps, halves(sg[n][:, :]), ALU.mult).then_inc(proj_read[o % 2], 1)
            dve.wait_ge(proj_read[o % 2], o // 2 + 1)

        gated_output(0)
        gated_output(1)
        branch(0, 0)
        gated_output(2)
        gated_output(3)
        dve.wait_ge(S_stored, 32)
        for j in range(8):
            if j:
                branch(0, j)
            branch(1, j)
            step(v.tensor_tensor(mtmp[:, :], mtmp[:, :], msum[:, :], ALU.add))
            step.settle()
            step(v.tensor_copy(mg_hi[:, j, :], mtmp[:, :]))
            step.settle()
            v.tensor_tensor(mg_lo[:, j, :], mtmp[:, :], mg_hi[:, j, :].bitcast(F32), ALU.subtract).then_inc(mg_ready, 1)
            dve.wait_ge(mg_ready, j + 1)

        dve.wait_ge(proj_done, OUT_INDEX["wo", 7] + 1)
        step(v.memset(LG[:, :, :], 0.0))
        for i in range(NT):
            r = ROWS[i]
            dve.wait_ge(x2_squared, i + 1)
            v.tensor_copy(X[0:r, i, :].rearrange("p (a b) -> p a b", a=2), x2_source(i)[0:r]).then_inc(x2_ready, 1)
            if i not in (0, 3):
                dve.wait_ge(x2_ready, i + 1)
                dve.sem_inc(proj_read[OUT_INDEX["x2", i] % 2], 1)
        dve.wait_ge(x2_rms, 1)
        v.reciprocal(st_x[:, 4, :], st_x[:, 1, :]).then_inc(x2_inv, 1)
        dve.wait_ge(x2_inv, 1)
        dve.wait_ge(lg_done, 1)
        raw_logits = bank[:, 2, 0:NT * 64].rearrange("p (i c) -> p i c", i=NT)[:, :, 0:GROUPS + NE]
        for r, a, b in ((P, 0, 4), (DEC, 4, 5)):
            step(v.tensor_tensor(LG[0:r, a:b, :], raw_logits[0:r, a:b], st_x[0:r, 4, a:b].unsqueeze(2).to_broadcast([r, b - a, GROUPS + NE]),
                                 ALU.mult))
        step.settle()
        for r, a, b in ((P, 0, 4), (DEC, 4, 5)):
            step(v.tensor_tensor(LG[0:r, a:b, :], LG[0:r, a:b, :], b_rt[0:r, :].unsqueeze(1).to_broadcast([r, b - a, GROUPS + NE]),
                                 ALU.add))
        step.settle()

        def bc(ap, n):
            return ap.unsqueeze(2).to_broadcast([P, NT, n])

        def row(name, n):
            return con(name).unsqueeze(1).to_broadcast([P, NT, n])

        def run(ins):
            step(ins)
            step.settle()

        def first_max(out, val, m, iota, n):
            run(v.tensor_tensor(out, val, bc(m, n), ALU.is_equal))
            run(v.tensor_tensor(out, out, row(iota, n), ALU.mult))
            run(v.tensor_reduce(r5[2], out, AX.X, ALU.min))
            run(v.tensor_tensor(out, row(iota, n), bc(r5[2], n), ALU.is_equal))

        G_, E_l = LG[:, :, 0:GROUPS], LG[:, :, GROUPS:]
        run(v.tensor_reduce(r5[0], G_, AX.X, ALU.max))
        v.tensor_tensor(rG, G_, bc(r5[0], GROUPS), ALU.subtract).then_inc(rt_exp_in, 1)
        first_max(rOG, G_, r5[0], "iota4", GROUPS)
        run(v.tensor_scalar(rPen, rOG, 1.0, BIG, ALU.subtract, ALU.mult))
        em = rE.rearrange("p i (g e) -> p i g e", g=GROUPS)
        run(v.tensor_tensor(em, E_l.rearrange("p i (g e) -> p i g e", g=GROUPS),
                            rOG.unsqueeze(3).to_broadcast([P, NT, GROUPS, PER_GROUP]), ALU.mult))
        run(v.tensor_tensor(em, em, rPen.unsqueeze(3).to_broadcast([P, NT, GROUPS, PER_GROUP]), ALU.add))
        run(v.tensor_reduce(r5[0], rE, AX.X, ALU.max))
        first_max(O1, rE, r5[0], "iota32", NE)
        run(v.tensor_scalar(rT, O1, -2.0 * BIG, None, ALU.mult))
        run(v.tensor_tensor(rE, rE, rT, ALU.add))
        run(v.tensor_reduce(r5[1], rE, AX.X, ALU.max))
        first_max(O2, rE, r5[1], "iota32", NE)
        v.tensor_tensor(rd, r5[1], r5[0], ALU.subtract).then_inc(rt_exp_in, 1)
        run(v.tensor_tensor(rT, O1, O2, ALU.add))
        v.tensor_tensor(picks[:, :, :], rT, bc(con("valid"), NE), ALU.mult).then_inc(chosen, 1)
        dve.wait_ge(rt_exp_out, 2)
        run(v.tensor_reduce(r5[2], rG, AX.X, ALU.add))
        run(v.tensor_scalar(r5[3], rd, 1.0, None, ALU.add))
        run(v.tensor_tensor(r5[3], r5[3], r5[2], ALU.mult))
        run(v.reciprocal(gate[:, 0, :], r5[3]))
        run(v.tensor_tensor(gate[:, 1, :], gate[:, 0, :], rd, ALU.mult))

        dve.wait_ge(ranks_done, 1)
        totals = bank[:, 1, 0:NT * NE].rearrange("p (i e) -> p i e", i=NT)
        run(v.memset(base[:, 0, :], 0.0))
        for i in range(NT):
            run(v.tensor_tensor(base[:, i + 1, :], base[:, i, :], totals[:, i, :], ALU.add))
        run(v.tensor_tensor(rank, bank[:, 0, 0:NT * NE].rearrange("p (i e) -> p i e", i=NT), base[:, 0:NT, :], ALU.add))
        run(v.tensor_tensor(nb8, base[:, NT, :].unsqueeze(2).to_broadcast([P, NE, 8]),
                            con("steps").unsqueeze(1).to_broadcast([P, NE, 8]), ALU.is_gt))
        run(v.tensor_reduce(cum[0], nb8, AX.X, ALU.add))
        run(v.tensor_copy(nb, cum[0]))
        for n, sh in enumerate((1, 2, 4, 8, 16)):
            a, b_ = cum[n % 2], cum[(n + 1) % 2]
            step(v.tensor_copy(b_[:, 0:sh], a[:, 0:sh]))
            run(v.tensor_tensor(b_[:, sh:], a[:, sh:], a[:, 0:NE - sh], ALU.add))
        end = cum[1]
        run(v.tensor_tensor(cum[0], end, nb, ALU.subtract))
        run(v.tensor_scalar(cum[0], cum[0], float(SLOTS), float(NMAIN - SLOTS), ALU.mult, ALU.add))
        run(v.tensor_tensor(cum[0], cum[0], con("base"), ALU.subtract))
        run(v.tensor_scalar(rT, rank, float(SLOTS), None, ALU.is_ge))
        run(v.tensor_tensor(rT, rT, cum[0].unsqueeze(1).to_broadcast([P, NT, NE]), ALU.mult))
        run(v.tensor_tensor(rank, rank, row("base", NE), ALU.add))
        run(v.tensor_tensor(rank, rank, rT, ALU.add))
        for c, O in enumerate((O1, O2)):
            run(v.tensor_tensor(rT, O, rank, ALU.mult))
            run(v.tensor_reduce(r5[c], rT, AX.X, ALU.add))
            v.tensor_copy(slotU[:, c * NT:(c + 1) * NT], r5[c]).then_inc(slots_ready, 1)
        run(v.tensor_tensor(nbe, end[0:1, :].unsqueeze(1).to_broadcast([1, NOVER, NE]),
                            con("blocks", 1).unsqueeze(2).to_broadcast([1, NOVER, NE]), ALU.is_le))
        run(v.tensor_reduce(bef, nbe, AX.X, ALU.add))
        run(v.tensor_scalar(bef, bef, float(NE - 1), None, ALU.min))
        run(v.tensor_copy(meta[0:1, 0:NOVER], bef))
        v.tensor_copy(meta[0:1, NOVER:NOVER + 1], end[0:1, NE - 1:NE]).then_inc(meta_ready, 1)

        def gated(s, done):
            v.tensor_tensor(hg[0:SLOTS, s, :], hg[0:SLOTS, s, :], proj[64:64 + SLOTS, s, 0, :], ALU.mult).then_inc(done, 1)

        def hidden_copy(s, done):
            v.tensor_copy(hT2[:, s, :, :], bank[:, 2 + s, 0:4 * SLOTS].rearrange("p (k l) -> p k l", k=4)).then_inc(done, 1)

        def turned_rows(done):
            for b in range(2):
                last = v.tensor_tensor(xsT[:, 4 * b:4 * b + 4, :], bank[:, b, :].rearrange("p (k l) -> p k l", k=4),
                                       g_ffn[:, 4 * b:4 * b + 4].unsqueeze(2).to_broadcast([P, 4, P]), ALU.mult)
            last.then_inc(done, 1)

        with dve.Fori(0, NE // 2) as q:
            dve.wait_ge(xsT_done, q + 1)
            turned_rows(xsT_copied)
            for s in range(2):
                dve.wait_ge(silu_done[s], q + 1)
                gated(s, act_done[s])
            for s in range(2):
                dve.wait_ge(hT2_done[s], q + 1)
                hidden_copy(s, hT2_copied[s])
                dve.wait_ge(down_done[s], q + 1)
                dve.wait_ge(yo_free[s], q + 1)
                v.tensor_copy(yo[:, s, :], proj[:, s, 1, :]).then_inc(yo_ready[s], 1)
        dve.wait_ge(ys_stored[0], NE // 2 * 32)
        dve.wait_ge(meta_ready, 1)
        n_more = dve.value_load(meta[0:1, NOVER:NOVER + 1], min_val=0, max_val=NOVER)
        with dve.Fori(0, NOVER) as b:
            with dve.If(b < n_more):
                dve.wait_ge(more_xT, b + 1)
                turned_rows(more_xT_copied)
                dve.wait_ge(more_silu, b + 1)
                gated(0, more_act)
                dve.wait_ge(more_hT, b + 1)
                hidden_copy(0, more_hT_copied)
                dve.wait_ge(more_down, b + 1)
                v.tensor_copy(yo[:, 0, :], proj[:, 0, 1, :]).then_inc(more_yo, 1)

        for i in range(NT):
            r = ROWS[i]
            xi = X[0:r, i, :]
            dve.wait_ge(gathered[i % 2], 32 * (i // 2 + 1))
            step(v.scalar_tensor_tensor(xi, zg[2 * (i % 2)][0:r, :], gate[0:r, 0, i:i + 1], xi, ALU.mult, ALU.add))
            step.settle()
            v.scalar_tensor_tensor(xi, zg[2 * (i % 2) + 1][0:r, :], gate[0:r, 1, i:i + 1], xi, ALU.mult, ALU.add).then_inc(comb_done, 1)
            dve.wait_ge(comb_rms, i + 1)
            inverse(st_x[0:r, 5, i:i + 1], st_x[0:r, 2, i:i + 1])
            v.scalar_tensor_tensor(zo[i % 2][0:r, :], xi, st_x[0:r, 5, i:i + 1], g_fin[0:r, :], ALU.mult, ALU.mult).then_inc(y_ready, 1)


INS = ["x_prompt", "x_sample", "cache_ckv", "cache_krope", "state_gla", "w_in", "w_uq", "w_ukv", "w_gate2", "b_gate2",
       "w_branch_a", "w_branch_b", "w_out", "w_router_group", "b_router_group", "w_router_expert",
       "b_router_expert", "w_exp_gate", "w_exp_up", "w_exp_down", "g_norm_final"]
OUTS = [("y_prompt", (1, SEQ, D)), ("y_sample", (1, DEC, D)), ("ckv_prompt", (1, 1, SEQ, KV_LORA)),
        ("krope_prompt", (1, 1, SEQ, ROPE)), ("gla_prompt", (1, 1, GH, DK, DV)), ("ckv_sample", (1, 1, DEC, KV_LORA)),
        ("krope_sample", (1, 1, DEC, ROPE)), ("gla_sample", (1, 1, GH, DK, DV))]


def kernel(**inputs):
    import concourse.bacc as bacc
    from concourse.bass_utils import run_bass_kernel_spmd

    nc = bacc.Bacc("TRN2", target_bir_lowering=False, num_devices=1)
    arrays = {n: np.ascontiguousarray(inputs[n]) for n in INS}
    arrays["shape_constants"] = shape_constants()
    for n, src in (("g_mix_cols", "g_norm_mix"), ("g_q_cols", "g_qnorm"), ("g_kv_cols", "g_kvnorm"), ("g_gla_cols", "g_gla_norm"),
                   ("g_ffn_cols", "g_norm_ffn")):
        arrays[n] = np.ascontiguousarray(np.asarray(inputs[src]).reshape(-1, P).T)
    t = {n: nc.dram_tensor(f"in_{n}", a.shape, mybir.dt.from_np(a.dtype), kind="ExternalInput").ap() for n, a in arrays.items()}
    for n, shape in OUTS:
        t[n] = nc.dram_tensor(f"out_{n}", shape, F32, kind="ExternalOutput").ap()
    build(nc, t)
    r = run_bass_kernel_spmd(nc, [{f"in_{n}": a for n, a in arrays.items()}], core_ids=[0])
    return tuple(r.results[0][f"out_{n}"] for n, _ in OUTS)
```

```python
from contextlib import ExitStack

import numpy as np

import concourse.bass as bass
from concourse import mybir

ALU = mybir.AluOpType
ACT = mybir.ActivationFunctionType
AX = mybir.AxisListType
F32 = mybir.dt.float32
F32R = mybir.dt.float32r
BF16 = mybir.dt.bfloat16
U32 = mybir.dt.uint32
I32 = mybir.dt.int32

P = 128
D = 1024
SEQ, DEC, PAST = 512, 32, 256
TOK = SEQ + DEC
HALF = TOK // 2
NT = 5
ROWS = [P, P, P, P, DEC]
KD = D // P
EPS = 1e-6
HEADS, Q_LORA, KV_LORA, NOPE, ROPE, VD = 8, 256, 128, 64, 32, 64
QK = NOPE + ROPE
ATT_SCALE = float(1.0 / np.sqrt(QK))
GH, DK, DV, RANK = 4, 128, 256, 16
SUB = 32
GROUPS, PER_GROUP, NE, FF = 4, 8, 32, 512
SLOTS = 64
NMAIN = NE * SLOTS
NOVER = (2 * TOK) // (SLOTS + 1)
NBLK = NE + NOVER
PAIRS = NE // 2
NSETS = 3
ROUNDS = (PAIRS - 1) // NSETS
assert ROUNDS * NSETS + 1 == PAIRS
KEYS = SEQ + PAST + DEC
BIG = 1e30
EXP_CAP = 80.0

COLS = {}
_c = 0
for _name, _n in (("cq", Q_LORA), ("kv", KV_LORA), ("kr", ROPE), ("gq", GH * DK), ("gk", GH * DK), ("gv", GH * DV),
                  ("lr", RANK), ("gr", GH * DV), ("ga", D), ("gb", D)):
    COLS[_name] = _c
    _c += _n

CONST_AT = {}
_c = 0
for _name, _n in (("ident", P), ("tri16", P), ("causal", P), ("before", P), ("rope", TOK), ("iota4", GROUPS),
                  ("iota32", NE), ("base", NE), ("steps", 8), ("blocks", NOVER), ("valid", NT), ("lane", P), ("iota_blk", NBLK), ("blk_start", NBLK - 1), ("tok_p", NT), ("tok_i", NT),
                  ("half", 1)):
    CONST_AT[_name] = (_c, _n)
    _c += _n
NCONST = _c


def shape_constants():
    c = np.zeros((P, NCONST), np.float32)

    def put(name, a):
        at, n = CONST_AT[name]
        c[:, at:at + n] = a

    r = np.arange(P)
    put("ident", np.eye(P))
    put("tri16", (r[:, None] <= r[None, :]) / 16.0)
    put("causal", r[None, :] <= r[:, None])
    put("before", r[:, None] < r[None, :])
    half = ROPE // 2
    inv = np.float32(10000.0) ** (-np.arange(half, dtype=np.float32) / np.float32(half))
    pos = np.concatenate([np.arange(SEQ), PAST + np.arange(DEC)]).astype(np.float32)
    ang = (pos[None, :] * inv[:, None].astype(np.float32)).astype(np.float32)
    rope = np.zeros((P, TOK), np.float32)
    rope[64:80] = rope[80:96] = np.cos(ang)
    rope[96:112], rope[112:128] = -np.sin(ang), np.sin(ang)
    put("rope", rope)
    put("iota4", np.arange(GROUPS) - 64.0)
    put("iota32", np.arange(NE) - 64.0)
    put("base", np.arange(NE) * float(SLOTS))
    put("steps", np.arange(1, 9) * float(SLOTS))
    put("blocks", np.arange(NOVER) * 1.0)
    valid = np.ones((P, NT), np.float32)
    valid[DEC:, NT - 1] = 0.0
    put("valid", valid)
    put("lane", r[None, :] % SLOTS)
    put("iota_blk", np.arange(NBLK) * 1.0)
    put("blk_start", np.arange(1, NBLK) * float(SLOTS))
    put("tok_p", (r[:, None] + 1) * valid)
    put("tok_i", np.arange(NT) * float(P) * valid)
    put("half", (r[:, None] >= SLOTS) - 4.0)
    return c


EARLY_GR = 4


EARLY_CUM = 4


def cum_bank(c):
    return 0 if c else 2 + EARLY_CUM % 2


def weight_tiles():
    t = [("cq", 0), ("cq", 1), ("kv", 0), ("kr", 0)] + [("gr", j) for j in range(EARLY_GR)] + [("uq", 0), ("uq", 1)]
    t += [("gq", j) for j in range(4)] + [("gk", j) for j in range(4)] + [("gv", j) for j in range(8)]
    t += [("gr", j) for j in range(EARLY_GR, 8)]
    for j in (0, 1):
        t += [("ga", j), ("wa", j)]
    for j in (0, 1):
        t += [("gb", j), ("wb", j)]
    for j in range(2, 8):
        t += [("ga", j), ("wa", j), ("gb", j), ("wb", j)]
    t += [("wo", j) for j in range(8)]
    return t


WT = weight_tiles()
WT_INDEX = {w: n for n, w in enumerate(WT)}
NRAW, NHIGH, NSPLIT = 3, 3, 2
NPAIR = HEADS // 2


def outputs():
    o = []
    for n, (k, j) in enumerate(WT):
        if (k == "gr" and j >= EARLY_GR) or (k, j) in (("ga", 0), ("wa", 0)):
            continue
        o += [(k, 4 * j + m, n) for m in range(4)] if k == "uq" else [(k, j, n)]
        if (k, j) == ("uq", 1):
            o += [("V", b, None) for b in range(7)] + [("K", hp, None) for hp in range(NPAIR)]
        if (k, j) == ("gv", 7):
            for c in range(NT):
                if c < 4:
                    o.append(("gr", EARLY_GR + c, WT_INDEX["gr", EARLY_GR + c]))
                o += [("og", c, None), ("st", c, None)]
            o += [("ga", 0, WT_INDEX["ga", 0]), ("om", 0, None), ("om", 1, None), ("wa", 0, WT_INDEX["wa", 0]),
                  ("om", 2, None), ("om", 3, None)]
    return o + [("x2", i, None) for i in (1, 2, 4)]


OUT = outputs()
OUT_INDEX = {(k, j): n for n, (k, j, _) in enumerate(OUT)}
LAST_OUT = {}
for _o, (_k, _j, _w) in enumerate(OUT):
    if _w is not None:
        LAST_OUT[_w] = _o


def n_loads(w):
    return {"kr": 4, "uq": 6}.get(w[0], 1)


UNITS = [(hp, i, a) for hp in range(HEADS // 2) for i in range(NT) for a in range(2)]


def unit_shape(i):
    if i < 4:
        return P, i * P, 0, P * (i + 1)
    return DEC, SEQ, SEQ, PAST + DEC


def split_columns(n):
    return 4 * P if WT[n][0] == "wa" else D


class Steps:

    def __init__(self, eng, sem):
        self.eng, self.sem, self.n = eng, sem, 0

    def __call__(self, ins):
        ins.then_inc(self.sem, 1)
        self.n += 1

    def settle(self):
        self.eng.wait_ge(self.sem, self.n)


def hT_high(nc, act, i, hTf_ready, hT_hi, hT_f, hT_hi_ready):
    act.wait_ge(hTf_ready, i + 1)
    nc.scalar.copy(hT_hi[:, :, i * P:i * P + ROWS[i]], hT_f[i][:, :, 0:ROWS[i]]).then_inc(hT_hi_ready, 1)


def run_pairs(eng, pair):
    pair(0, 0)
    with eng.Fori(0, ROUNDS) as it:
        for m in range(1, NSETS + 1):
            pair(it, m)


DVE_LOW = (1, 3)


def hT_low(engine, eng, i, hT_hi_ready, hT_hi, hT_lo, hT_f, hT_ready):
    eng.wait_ge(hT_hi_ready, i + 1)
    tok = slice(i * P, i * P + ROWS[i])
    engine.tensor_tensor(hT_lo[:, :, tok], hT_f[i][:, :, 0:ROWS[i]], hT_hi[:, :, tok].bitcast(F32),
                         ALU.subtract).then_inc(hT_ready, 1)


def build(nc, t):
    ctx = ExitStack()
    with ctx:
        _build(nc, t, ctx)


def _build(nc, t, ctx):
    def sem(name):
        return ctx.enter_context(nc.semaphore(name))

    def flat(name):
        return t[name].rearrange("a b c -> (a b) c")

    BASE = 16512

    class Region:
        def __init__(self, at):
            self.at = at

        def __call__(self, name, shape, dt=F32, after=None):
            n = 1
            for s in shape[1:]:
                n *= s
            size = n * mybir.dt.size(dt)
            h = nc.alloc_sbuf_tensor_at(name, shape, dt, offset=self.at)
            self.at += (size + 31) // 32 * 32
            return h

    R = Region(BASE)
    X = R("x_rows", [P, NT, D])
    cst = R("cst", [P, NCONST])
    mean256 = R("mean256", [P, P])
    mean128 = R("mean128", [P, P])
    ones = R("ones", [P, P])
    eps_col = R("eps_col", [P, 1])
    qlow = R("qlow", [1, P], BF16)
    khigh = R("khigh", [1, P], BF16)
    g_mix = R("g_mix", [P, KD])
    g_q = R("g_q", [P, 2])
    g_kv = R("g_kv", [P, 1])
    g_gla = R("g_gla", [P, 2])
    g_ffn = R("g_ffn", [P, KD])
    g_fin = R("g_fin", [P, D])
    w_rt = R("w_rt", [P, KD, 64])
    b_rt = R("b_rt", [P, GROUPS + NE])
    w_g2 = R("w_g2", [RANK + 1, GH * DK])
    st_x = R("st_x", [P, 6, NT])
    meta = R("meta", [1, NOVER + 1], I32)
    G1 = R("gather_at", [P, NBLK])
    S1 = R("scatter_at", [P, NBLK])
    gidx = R("gidx", [P, 1], U32)
    sidx = [R(f"sidx{n}", [P, 1], U32) for n in range(2)]
    gate = R("gate", [P, 2, NT])
    RING = R.at
    raw = [R(f"raw{n}", [P, D]) for n in range(NRAW)]
    whi = [R(f"whi{n}", [P, D], F32R) for n in range(NHIGH)]
    wlo = [R(f"wlo{n}", [P, D], F32R) for n in range(NSPLIT)]
    HT = R.at
    hT_hi = R("hT_hi", [P, KD, TOK], F32R)
    hT_lo = R("hT_lo", [P, KD, TOK], F32R)
    ARENA = R.at
    LAST = 229344

    A = Region(ARENA)
    oa_hi = A("oa_hi", [P, 4, TOK], F32R)
    oa_lo = A("oa_lo", [P, 4, TOK], F32R)
    glr = A("glr", [RANK + 1, TOK])
    AFTER_OA = A.at
    w_kv = A("w_kv", [P, D])
    ckvA = A("ckvA", [P, KEYS])
    kpeA = A("kpeA", [P, KEYS])
    VALUES = A.at
    V = A("V", [P, 7, HEADS * VD])
    qT = A("qT", [P, HEADS, TOK])
    KC = A.at
    kcat = [A(f"kcat{n}", [P, 2, KEYS]) for n in range(2)]
    rtmp = A("rtmp", [P, 2, TOK])
    caches = A("caches", [P, 2, 2, P])
    obuf = A("obuf", [P, NT, KV_LORA])
    kbuf = A("kbuf", [P, NT, ROPE])
    SM = A.at
    cqn_hi = A("cqn_hi", [P, 2, TOK], F32R)
    cqn_lo = A("cqn_lo", [P, 2, TOK], F32R)
    kr = A("kr", [P, TOK])
    kvr = A("kvr", [P, TOK])
    kvs = A("kvs", [P, TOK])
    rk = A("rk", [P, TOK])
    assert A.at <= LAST - 4096, A.at
    Q_ = Region(KC)
    cq = Q_("cq", [P, 2, TOK])
    cqs = Q_("cqs", [P, 2, TOK])
    rq = Q_("rq", [P, TOK])
    S_ = Region(SM)
    prob = [S_(f"prob{n}", [P, SEQ]) for n in range(3)]
    probT = [S_(f"probT{n}", [P, SEQ]) for n in range(2)]
    stat = S_("stat", [P, 4, len(UNITS)])

    A0 = Region(VALUES)
    xn = [A0(f"xn{n}", [P, D]) for n in range(2)]
    hT_f = [A0(f"hT_f{n}", [P, KD, P]) for n in range(NT)]
    squares = A0("squares", [P, D])

    G = Region(AFTER_OA)
    OG = G.at
    gqk = G("gqk", [P, 2 * GH, TOK])
    AFTER_OG = G.at
    gvT = [G(f"gvT{n}", [P, TOK]) for n in range(2)]
    vtok = G("vtok", [P, NT, GH * DV])
    la = G("la", [P, NT, GH * DK])
    GS = G.at
    S_st = G("S_st", [P, GH, DV])
    bS = G("bS", [P, GH, P])
    ex = G("ex", [P, GH * 4 * P + 2 * GH * P])
    exq = [G(f"exq{n}", [P, GH * P + GH]) for n in range(2)]
    att = G("att", [P, GH, P])
    kdT = G("kdT", [P, GH, P])
    attT = G("attT", [P, GH, P])
    assert G.at <= LAST - 4096, G.at
    S_smp = nc.alloc_sbuf_tensor_at("S_smp", [P, GH, DV], F32, offset=LAST - 4096)
    grs = nc.alloc_sbuf_tensor_at("grs", [P, 8, TOK], F32, offset=BASE)
    G2 = Region(GS)
    lmin = G2("lmin", [P, NT, GH * DK])

    N_ = Region(AFTER_OG)
    ob_lo = nc.alloc_sbuf_tensor_at("ob_lo", [P, 8, TOK], F32R, offset=OG)
    ob_hi = N_("ob_hi", [P, 8, TOK], F32R)
    sg = [N_(f"sg{n}", [P, TOK]) for n in range(2)]
    mtmp = N_("mtmp", [P, TOK])
    msum = N_("msum", [P, TOK])
    osq = [N_(f"osq{n}", [P, 2, TOK]) for n in range(2)]
    MG0 = N_.at
    assert N_.at <= GS
    ors = [nc.alloc_sbuf_tensor_at(f"ors{n}", [P, TOK], F32, offset=at) for n, at in enumerate((BASE + 8 * TOK * 4, AFTER_OA - TOK * 4))]
    MG = (LAST - 2 * 8 * TOK * 4) // 32 * 32
    YT = MG - 8 * TOK * 4
    assert MG >= MG0
    E_ = Region(YT)
    yT = E_("yT", [P, 8, TOK])
    mg_hi = E_("mg_hi", [P, 8, TOK], F32R)
    mg_lo = E_("mg_lo", [P, 8, TOK], F32R)
    msum1 = nc.alloc_sbuf_tensor_at("msum1", [P, TOK], F32, offset=E_.at - TOK * 4)
    F_ = Region(MG)
    h2 = F_("h2", [P, NT, D])
    lgT = F_("lgT", [64, TOK])
    K_ = Region(RING)
    xsb = K_("xsb", [P, D])
    xsT = K_("xsT", [P, KD, P])
    hg = K_("hg", [P, 2, FF])
    hT2 = K_("hT2", [P, 2, 4, SLOTS])
    yo = K_("yo", [P, 2, FF])
    W_ = Region(K_.at)
    parts = [W_(f"we{n}", [P, 4096]) for n in range(3 * NSETS)]
    we = [parts[1:4], parts[4:7], [parts[0], parts[7], parts[8]]]
    PART = 16384
    assert K_.at + PART >= HT and K_.at + 6 * PART <= YT and K_.at + 7 * PART <= MG and W_.at >= F_.at
    RT = W_.at
    M_ = Region(RING + 4096)
    slotF = M_("slotF", [P, 2, NT])
    blkF = M_("blkF", [P, 2, NT])
    over_blk = M_("over_blk", [P, 2 * NT, NBLK - 1])
    is_blk = M_("is_blk", [P, 2 * NT, NBLK])
    q_p = M_("q_p", [P, 2 * NT, NBLK], BF16)
    q_i = M_("q_i", [P, 2 * NT, NBLK], BF16)
    q_c = M_("q_c", [P, NT, NBLK], BF16)
    lanes = M_("lanes", [P, 2 * NT, P], BF16)
    vacant = M_("vacant", [P, NBLK])
    assert M_.at <= K_.at
    Z_ = Region(K_.at + PART)
    zc = [Z_(f"zc{n}", [P, 2, D]) for n in range(NT)]
    zo = [Z_(f"zo{n}", [P, D]) for n in range(NT)]

    def con(name, rows=P):
        at, n = CONST_AT[name]
        return cst[0:rows, at:at + n]

    proj = ctx.enter_context(nc.psum_tensor("proj", [P, 2, 2, 512], F32))
    bank = ctx.enter_context(nc.psum_tensor("bank", [P, 4, 512], F32))

    rows = nc.dram_tensor("token_rows", (TOK, D), F32, kind="Internal").ap()
    ys = nc.dram_tensor("expert_out", (4 * TOK, FF), F32, kind="Internal").ap()
    w_in, w_uq, w_ukv = flat("w_in"), flat("w_uq"), flat("w_ukv")
    w_a, w_b, w_o = flat("w_branch_a"), flat("w_branch_b"), flat("w_out")
    w_eg = t["w_exp_gate"].rearrange("a e (k p) f -> (a e) p k f", p=P)
    w_eu = t["w_exp_up"].rearrange("a e (k p) f -> (a e) p k f", p=P)
    w_ed = t["w_exp_down"].rearrange("a e (k p) f -> (a e) p k f", p=P)

    def x_src(i):
        return flat("x_prompt")[i * P:(i + 1) * P, :] if i < 4 else flat("x_sample")

    x_loaded = [sem(f"x_loaded{i}") for i in range(NT)]
    w_loaded = [sem(f"w_loaded{n}") for n in range(NRAW)]
    proj_read = [sem(f"proj_read{n}") for n in range(2)]
    y_stored = sem("y_stored")
    we_loaded = [[sem(f"we_loaded{s}_{n}") for n in range(3)] for s in range(NSETS)]
    up_done = sem("up_done")
    silu_done = sem("silu_done")
    act_done = [sem(f"act_done{s}") for s in range(2)]
    hT2_done = sem("hT2_done")
    hT2_copied = [sem(f"hT2_copied{s}") for s in range(2)]
    down_done = sem("down_done")
    yo_ready = sem("yo_ready")
    combined_loaded = [sem(f"combined_loaded{n}") for n in range(NT)]
    ys_stored = [sem(f"ys_stored{s}") for s in range(2)]
    x_rms = sem("x_rms")
    xn_ready = sem("xn_ready")
    xT_ready = sem("xT_ready")
    hTf_ready = sem("hTf_ready")
    hT_hi_ready = sem("hT_hi_ready")
    hT_ready = sem("hT_ready")
    w_high = sem("w_high")
    w_split = sem("w_split")
    proj_done = sem("proj_done")
    lat_mean = sem("lat_mean")
    lat_rms = sem("lat_rms")
    cqn_ready = sem("cqn_ready")
    ckv_ready = sem("ckv_ready")
    kpe_ready = sem("kpe_ready")
    q_ready = sem("q_ready")
    cache_T = sem("cache_T")
    keys_ready = sem("keys_ready")
    out_T = sem("out_T")
    out_copied = sem("out_copied")
    kcat_pe = sem("kcat_pe")
    scores_ready = sem("scores_ready")
    negmax_ready = sem("negmax_ready")
    exp_done = sem("exp_done")
    prob_ready = sem("prob_ready")
    probT_done = sem("probT_done")
    probT_copied = sem("probT_copied")
    pv_done = sem("pv_done")
    oa_done = sem("oa_done")
    gvT_done = sem("gvT_done")
    vtok_ready = sem("vtok_ready")
    gate_done = sem("gate_done")
    gate_abs = sem("gate_abs")
    gate_min = sem("gate_min")
    la_log = sem("la_log")
    la_ready = sem("la_ready")
    cum_done = sem("cum_done")
    bS_ready = sem("bS_ready")
    ex_arg = sem("ex_arg")
    ex_ready = sem("ex_ready")
    kq_ready = sem("kq_ready")
    att_done = sem("att_done")
    att_masked = sem("att_masked")
    attT_done = sem("attT_done")
    attT_copied = sem("attT_copied")
    kdT_done = sem("kdT_done")
    kdT_copied = sem("kdT_copied")
    S_ready = sem("S_ready")
    S_stored = sem("S_stored")
    osq_ready = sem("osq_ready")
    og_gated = sem("og_gated")
    og_ready = sem("og_ready")
    ob_high = sem("ob_high")
    ob_ready = sem("ob_ready")
    mg_ready = sem("mg_ready")
    w_rt_ready = sem("w_rt_ready")
    x2T_read = sem("x2T_read")
    logits_done = sem("logits_done")
    lgT_copied = sem("lgT_copied")
    lg_done = sem("lg_done")
    x2_turned = sem("x2_turned")
    x2_squared = sem("x2_squared")
    x2_ready = sem("x2_ready")
    x2_rms = sem("x2_rms")
    x2_inv = sem("x2_inv")
    h2_ready = sem("h2_ready")
    rt_exp_in = sem("rt_exp_in")
    rt_exp_out = sem("rt_exp_out")
    chosen = sem("chosen")
    ranks_done = sem("ranks_done")
    rows_stored = sem("rows_stored")
    blk_ready = sem("blk_ready")
    onehots_i_ready = sem("onehots_i_ready")
    onehots_ready = sem("onehots_ready")
    maps_done = sem("maps_done")
    gidx_ready = sem("gidx_ready")
    xsb_set = sem("xsb_set")
    dispatched = sem("dispatched")
    all_stored = sem("all_stored")
    more_idx = sem("more_idx")
    meta_ready = sem("meta_ready")
    xs_loaded = sem("xs_loaded")
    xsT_done = sem("xsT_done")
    xsT_copied = sem("xsT_copied")
    more_x = sem("more_x")
    more_w = sem("more_w")
    more_xT = sem("more_xT")
    more_xT_copied = sem("more_xT_copied")
    more_up = sem("more_up")
    more_silu = sem("more_silu")
    more_act = sem("more_act")
    more_hT = sem("more_hT")
    more_hT_copied = sem("more_hT_copied")
    more_down = sem("more_down")
    more_yo = sem("more_yo")
    more_stored = sem("more_stored")
    more_free = sem("more_free")
    comb_done = sem("comb_done")
    comb_rms = sem("comb_rms")
    comb_inv = sem("comb_inv")
    y_scaled = sem("y_scaled")
    y_ready = sem("y_ready")
    y_last = sem("y_last")
    lat_stored = sem("lat_stored")
    const_loaded = sem("const_loaded")
    sides_loaded = sem("sides_loaded")
    kv_loaded = sem("kv_loaded")
    caches_loaded = sem("caches_loaded")
    state_loaded = sem("state_loaded")
    consts_set = sem("consts_set")
    act_seq, dve_seq = sem("act_seq"), sem("dve_seq")

    def chunk_views(L, c):
        ns = L // SUB
        n0 = GH * ns * L
        n1 = GH * L

        def part(at, n):
            return ex[:, at:at + n]
        late = exq[c % 2]
        return (part(0, n0).rearrange("p (h s l) -> p h s l", h=GH, s=ns),
                part(n0, n1).rearrange("p (h s l) -> p h s l", h=GH, s=ns),
                part(n0 + n1, n1).rearrange("p (h l) -> p h l", h=GH),
                late[:, 0:n1].rearrange("p (h l) -> p h l", h=GH),
                late[:, GH * P:GH * P + GH].rearrange("p (h l) -> p h l", h=GH))

    T_ = Region(RT)
    LG = T_("LG", [P, NT, GROUPS + NE])
    r5 = [T_(f"r5_{n}", [P, NT])[:, :] for n in range(4)]
    rG = T_("rG", [P, NT, GROUPS])[:, :, :]
    rOG = T_("rOG", [P, NT, GROUPS])[:, :, :]
    rPen = T_("rPen", [P, NT, GROUPS])[:, :, :]
    rE = T_("rE", [P, NT, NE])[:, :, :]
    rT = T_("rT", [P, NT, NE])[:, :, :]
    O1 = T_("O1", [P, NT, NE])[:, :, :]
    O2 = T_("O2", [P, NT, NE])[:, :, :]
    picks = T_("picks", [P, NT, NE])
    rank = T_("rank", [P, NT, NE])[:, :, :]
    base = T_("tile_base", [P, NT + 1, NE])
    rd = T_("rd", [P, NT])[:, :]
    cum = [T_(f"cum{n}", [P, NE])[:, :] for n in range(2)]
    nb = T_("nb", [P, NE])[:, :]
    nb8 = T_("nb8", [P, NE, 8])[:, :, :]
    nbe = T_("nbe", [1, NOVER, NE])[:, :, :]
    bef = T_("bef", [1, NOVER])[:, :]
    assert T_.at <= LAST, T_.at

    def x2_source(i):
        return bank[:, 0:2, :] if i in (0, 3) else proj[:, OUT_INDEX["x2", i] % 2, :, :]

    block = ctx.enter_context(nc.Block())

    @block.sync
    def _(sp):
        def weight_source(n):
            kind, j = WT[n]
            dst = raw[n % NRAW]
            if kind == "kr":
                d3 = dst[:, :].rearrange("p (k c) -> p k c", k=KD)
                src = w_in.rearrange("(k p) c -> p k c", p=P)
                lr, k0 = COLS["lr"], COLS["kr"]
                return [(d3[:, :, 0:64], src[:, :, lr:lr + 64]), (d3[:, :, 64:96], src[:, :, k0:k0 + 32]),
                        (d3[:, :, 96:112], src[:, :, k0 + 16:k0 + 32]), (d3[:, :, 112:128], src[:, :, k0:k0 + 16])]
            if kind == "uq":
                d4 = dst[:, :].rearrange("p (k h c) -> p k h c", k=2, h=4)
                src = w_uq.rearrange("(k p) (h c) -> p k h c", p=P, c=QK)
                return [p for k in range(2) for p in (
                    (d4[:, k, :, 0:96], src[:, k, 4 * j:4 * j + 4, :]),
                    (d4[:, k, :, 96:112], src[:, k, 4 * j:4 * j + 4, 80:96]),
                    (d4[:, k, :, 112:128], src[:, k, 4 * j:4 * j + 4, 64:80]))]
            w = {"wa": w_a, "wb": w_b, "wo": w_o}.get(kind, w_in)
            k = {"wa": 4}.get(kind, KD)
            c0 = COLS.get(kind, 0) + j * P
            return [(dst[:, 0:k * P].rearrange("p (k c) -> p k c", k=k),
                     w.rearrange("(k p) c -> p k c", p=P)[:, :, c0:c0 + P])]

        def load_weights(n):
            if n >= NRAW:
                sp.wait_ge(w_split, n - NRAW + 1)
            for dst, src in weight_source(n):
                sp.dma_start(dst, src).then_inc(w_loaded[n % NRAW], 16)

        for i in range(NT):
            sp.dma_start(X[0:ROWS[i], i, :], x_src(i)).then_inc(x_loaded[i], 16)
            if i == 0:
                sp.dma_start(cst[:, :], t["shape_constants"]).then_inc(const_loaded, 16)
                sp.dma_start(g_mix[:, :], t["g_mix_cols"]).then_inc(const_loaded, 16)
                sp.dma_start(g_q[:, :], t["g_q_cols"]).then_inc(const_loaded, 16)
                sp.dma_start(g_kv[:, :], t["g_kv_cols"]).then_inc(const_loaded, 16)
                sp.dma_start(g_gla[:, :], t["g_gla_cols"]).then_inc(const_loaded, 16)
                sp.dma_start(g_ffn[:, :], t["g_ffn_cols"]).then_inc(const_loaded, 16)
        for n in range(NRAW):
            load_weights(n)
        for part in range(2):
            sp.dma_start(w_kv[:, part * FF:(part + 1) * FF].rearrange("p (h c) -> p h c", c=NOPE),
                         w_ukv.rearrange("p (h t c) -> p t h c", t=2, c=NOPE)[:, part]).then_inc(kv_loaded, 16)
        sp.dma_start(caches[:, 0, :, :], t["cache_ckv"].rearrange("a b (c p) d -> p (a b c) d", p=P)).then_inc(caches_loaded, 16)
        sp.dma_start(caches[:, 1, :, 64:96], t["cache_krope"].rearrange("a b (c p) d -> p (a b c) d", p=P)).then_inc(caches_loaded, 16)
        sp.dma_start(w_g2[0:RANK, :], flat("w_gate2")).then_inc(sides_loaded, 16)
        sp.dma_start(w_g2[RANK:RANK + 1, :], t["b_gate2"]).then_inc(sides_loaded, 16)
        sp.dma_start(g_fin[:, :], t["g_norm_final"].rearrange("(a d) -> a d", a=1).to_broadcast([P, D])).then_inc(sides_loaded, 16)
        sp.dma_start(b_rt[:, 0:GROUPS], t["b_router_group"].to_broadcast([P, GROUPS])).then_inc(sides_loaded, 16)
        sp.dma_start(b_rt[:, GROUPS:], t["b_router_expert"].to_broadcast([P, NE])).then_inc(sides_loaded, 16)
        sp.dma_start(w_rt[:, :, 0:GROUPS], flat("w_router_group").rearrange("(k p) c -> p k c", p=P)).then_inc(sides_loaded, 16)
        sp.dma_start(w_rt[:, :, GROUPS:GROUPS + NE], flat("w_router_expert").rearrange("(k p) c -> p k c", p=P)).then_inc(sides_loaded, 16)
        for n in range(NRAW, len(WT)):
            load_weights(n)
            if n == WT_INDEX["gq", 2]:
                sp.wait_ge(out_copied, 1)
                sp.dma_start(t["ckv_prompt"].rearrange("a b (c p) d -> p (a b c) d", p=P), obuf[:, 0:4, :]).then_inc(lat_stored, 16)
                sp.dma_start(t["ckv_sample"].rearrange("a b p d -> (a b p) d"), obuf[0:DEC, 4, :]).then_inc(lat_stored, 16)
                sp.dma_start(t["krope_prompt"].rearrange("a b (c p) d -> p (a b c) d", p=P), kbuf[:, 0:4, :]).then_inc(lat_stored, 16)
                sp.dma_start(t["krope_sample"].rearrange("a b p d -> (a b p) d"), kbuf[0:DEC, 4, :]).then_inc(lat_stored, 16)
            if n == WT_INDEX["gv", 5]:
                sp.dma_start(S_smp[:, :, :], t["state_gla"].rearrange("a b h p v -> p (a b h) v")).then_inc(state_loaded, 16)
            if n == WT_INDEX["ga", 1]:
                sp.wait_ge(S_ready, 4)
                sp.dma_start(t["gla_prompt"].rearrange("a b h p v -> p (a b h) v"), S_st[:, :, :]).then_inc(S_stored, 16)
                sp.wait_ge(S_ready, 5)
                sp.dma_start(t["gla_sample"].rearrange("a b h p v -> p (a b h) v"), S_smp[:, :, :]).then_inc(S_stored, 16)
            if 0 <= n - WT_INDEX["ga", 3] < NT:
                i = n - WT_INDEX["ga", 3]
                sp.wait_ge(ob_ready, GH)
                sp.dma_start(X[0:ROWS[i], i, :], x_src(i)).then_inc(x_loaded[i], 16)

        def load_expert(s, part, e):
            w = (w_eg, w_eu, w_ed)[part]
            k = (KD, KD, 4)[part]
            src = w[e:e + 1] if isinstance(e, int) else w[bass.ds(e, 1)]
            sp.dma_start(we[s][part][:, :].rearrange("p (k f) -> p k f", k=k),
                         src.rearrange("o p k f -> (o p) k f")).then_inc(we_loaded[s][part], 16)

        sp.wait_ge(proj_done, OUT_INDEX["wb", 7] + 1)
        sp.wait_ge(mg_ready, 8)
        for s, part in ((0, 0), (0, 1), (0, 2), (1, 0), (1, 1)):
            load_expert(s, part, s)
        sp.wait_ge(proj_done, OUT_INDEX["wo", 7] + 1)
        load_expert(2, 0, 2)
        for i in range(NT):
            sp.wait_ge(h2_ready, i + 1)
            sp.dma_start(rows[i * P:i * P + ROWS[i], :], h2[0:ROWS[i], i, :]).then_inc(rows_stored, 16)
        sp.wait_ge(x2_turned, NT)
        load_expert(1, 2, 1)
        sp.wait_ge(rows_stored, 16 * NT)
        load_expert(2, 1, 2)
        load_expert(2, 2, 2)

        def next_weights(it, u):
            s = u % NSETS
            sp.wait_ge(up_done, it * (2 * NSETS) + u + 1)
            load_expert(s, 0, it * (2 * NSETS) + u + NSETS)
            load_expert(s, 1, it * (2 * NSETS) + u + NSETS)
            sp.wait_ge(down_done, it * (2 * NSETS) + u + 1)
            load_expert(s, 2, it * (2 * NSETS) + u + NSETS)

        full, rest = divmod(NE - NSETS, 2 * NSETS)
        with sp.Fori(0, full) as it:
            for u in range(2 * NSETS):
                next_weights(it, u)
        for u in range(rest):
            next_weights(full, u)

        sp.wait_ge(down_done, NE)
        sp.wait_ge(meta_ready, 1)
        n_more = sp.value_load(meta[0:1, NOVER:NOVER + 1], min_val=0, max_val=NOVER)
        with sp.If(n_more > 0):
            with sp.Fori(0, NOVER) as b:
                with sp.If(b < n_more):
                    e = sp.value_load(meta[0:1, bass.ds(b, 1)], min_val=0, max_val=NE - 1)
                    sp.wait_ge(more_free, b + 1)
                    for part in range(3):
                        w = (w_eg, w_eu, w_ed)[part]
                        sp.dma_start(we[0][part][:, :].rearrange("p (k f) -> p k f", k=(KD, KD, 4)[part]),
                                     w[bass.ds(e, 1)].rearrange("o p k f -> (o p) k f")).then_inc(more_w, 16)

        sp.wait_ge(all_stored, 1)
        pair_rows = ys.rearrange("(t x) d -> t (x d)", x=4)
        for i in range(NT):
            sp.dma_start(zc[i][0:ROWS[i], :, :].rearrange("p c d -> p (c d)"), pair_rows[i * P:i * P + ROWS[i], :])\
                .then_inc(combined_loaded[i], 16)
        for i in range(NT):
            if i < NT - 1:
                sp.wait_ge(y_ready, i + 1)
            else:
                sp.wait_ge(y_last, 1)
            dst = flat("y_prompt")[i * P:(i + 1) * P, :] if i < 4 else flat("y_sample")
            sp.dma_start(dst, zo[i][0:ROWS[i], :]).then_inc(y_stored, 16)
        sp.wait_ge(y_stored, 16 * NT)
        sp.wait_ge(S_stored, 32)
        sp.wait_ge(lat_stored, 64)

    @block.gpsimd
    def _(pool):
        def split(n):
            c = split_columns(n)
            pool.wait_ge(w_high, n + 1)
            if n >= NSPLIT:
                pool.wait_ge(proj_done, LAST_OUT[n - NSPLIT] + 1)
            hi, lo = whi[n % NHIGH], wlo[n % NSPLIT]
            nc.gpsimd.tensor_tensor(lo[:, 0:c], raw[n % NRAW][:, 0:c], hi[:, 0:c].bitcast(F32),
                                    ALU.subtract).then_inc(w_split, 1)

        for i in range(NT - 1):
            if i not in DVE_LOW:
                hT_low(nc.gpsimd, pool, i, hT_hi_ready, hT_hi, hT_lo, hT_f, hT_ready)
        def low_output(h):
            two = slice(2 * h, 2 * h + 2)
            pool.wait_ge(ob_high, h + 1)
            nc.gpsimd.tensor_tensor(ob_lo[:, two, :], gqk[:, two, :], ob_hi[:, two, :].bitcast(F32),
                                    ALU.subtract).then_inc(ob_ready, 1)

        def gate_output(h):
            two = slice(2 * h, 2 * h + 2)
            pool.wait_ge(osq_ready, h + 1)
            nc.gpsimd.tensor_tensor(gqk[:, two, :], gqk[:, two, :], grs[:, two, :], ALU.mult).then_inc(og_gated, 1)

        gates_after = {("wa", 0): (0, 1), ("ga", 1): (2, 3)}
        low_outputs_after = {("ga", 1): (0,), ("wa", 1): (1,), ("gb", 0): (2,), ("wb", 0): (3,)}
        for n in range(len(WT)):
            split(n)
            for h in gates_after.get(WT[n], ()):
                gate_output(h)
            for h in low_outputs_after.get(WT[n], ()):
                low_output(h)

        pool.wait_ge(w_split, len(WT))
        nc.gpsimd.memset(xsb[:, :], 0.0).then_inc(xsb_set, 1)
        pool.wait_ge(xsb_set, 1)

        def gather(n, done):
            pool.indirect_dma_start(out=xsb[0:n, :], out_offset=None, in_=rows[:, :],
                                    in_offset=bass.IndirectOffsetOnAxis(ap=gidx[0:n, 0:1], axis=0),
                                    bounds_check=TOK - 1, oob_is_err=False).then_inc(done, 16)

        def scatter(s, done):
            pool.indirect_dma_start(out=ys[:, :], out_offset=bass.IndirectOffsetOnAxis(ap=sidx[s][:, 0:1], axis=0),
                                    in_=yo[:, s, :], in_offset=None, bounds_check=4 * TOK - 1, oob_is_err=False)\
                .then_inc(done, 16)

        pool.sem_inc(more_free, 1)
        pool.wait_ge(blk_ready, 1)
        for c in range(2):
            nc.gpsimd.tensor_tensor(q_i[:, c * NT:(c + 1) * NT, :], is_blk[:, c * NT:(c + 1) * NT, :],
                                    con("tok_i").unsqueeze(2).to_broadcast([P, NT, NBLK]), ALU.mult)
        nc.gpsimd.tensor_tensor(q_c[:, :, :], is_blk[:, NT:, :], con("valid").unsqueeze(2).to_broadcast([P, NT, NBLK]),
                                ALU.mult).then_inc(onehots_i_ready, 1)
        pool.wait_ge(rows_stored, 16 * NT)
        pool.wait_ge(gidx_ready, 1)
        gather(P, xs_loaded)

        def pair(it, m):
            pool.wait_ge(gidx_ready, it * NSETS + m + 2)
            pool.sem_inc(dispatched, 1)
            gather(P, xs_loaded)
            for s in range(2):
                pool.wait_ge(yo_ready, it * (2 * NSETS) + 2 * m + s + 1)
                pool.sem_inc(dispatched, 1)
                scatter(s, ys_stored[s])

        run_pairs(pool, pair)
        pool.wait_ge(xs_loaded, 16 * (PAIRS + 1))
        pool.wait_ge(meta_ready, 1)
        n_more = pool.value_load(meta[0:1, NOVER:NOVER + 1], min_val=0, max_val=NOVER)
        with pool.If(n_more > 0):
            with pool.Fori(0, NOVER) as b:
                with pool.If(b < n_more):
                    pool.wait_ge(more_idx, b + 1)
                    pool.sem_inc(dispatched, 1)
                    gather(SLOTS, more_x)
                    pool.wait_ge(more_yo, b + 1)
                    pool.sem_inc(dispatched, 1)
                    scatter(0, more_stored)
                    pool.wait_ge(more_stored, b * 16 + 16)
                    pool.sem_inc(more_free, 1)
        for s in range(2):
            pool.wait_ge(ys_stored[s], 16 * PAIRS)
        pool.sem_inc(all_stored, 1)

        for i in range(NT - 1):
            r = ROWS[i]
            pool.wait_ge(y_scaled, i + 1)
            nc.gpsimd.tensor_tensor(zo[i][0:r, :], zo[i][0:r, :], g_fin[0:r, :], ALU.mult).then_inc(y_ready, 1)

    @block.tensor
    def _(pe):
        ident = con("ident")
        emitted = [0]

        def take(kind, j):
            o = emitted[0]
            assert OUT[o][:2] == (kind, j), (OUT[o], kind, j)
            emitted[0] += 1
            if o >= 2:
                pe.wait_ge(proj_read[o % 2], o // 2)
            return o, o % 2

        def add_x(slot, j):
            for i in range(NT):
                r = ROWS[i]
                for half in range(2):
                    a, b = max(i * P, half * HALF), min(i * P + r, (half + 1) * HALF)
                    if a < b:
                        pe.matmul(proj[:, slot, half, a - half * HALF:b - half * HALF], X[0:r, i, j * P:(j + 1) * P],
                                  ident[0:r, a - i * P:b - i * P], start=False, stop=False)

        def product(kind, j):
            o, slot = take(kind, j)
            n = OUT[o][2]
            hi, lo = whi[n % NHIGH], wlo[n % NSPLIT]
            nk, rhi, rlo = {"uq": (2, cqn_hi, cqn_lo), "wa": (4, oa_hi, oa_lo), "wb": (8, ob_hi, ob_lo),
                            "wo": (8, mg_hi, mg_lo)}.get(kind, (KD, hT_hi, hT_lo))
            terms = [(k, w, r) for k in range(nk) for w, r in ((hi, rhi), (hi, rlo), (lo, rhi))]
            pe.wait_ge(w_split, n + 1)
            for m, (k, w, r) in enumerate(terms):
                if (kind, j) == ("wo", 0) and m % 3 == 0:
                    pe.wait_ge(mg_ready, k + 1)
                if (kind, j) == ("wb", 0) and m % 6 == 0:
                    pe.wait_ge(ob_ready, k // 2 + 1)
                at = (k * 4 + j % 4) * P if kind == "uq" else k * P
                for half in range(2):
                    mm = pe.matmul(proj[:, slot, half, 0:HALF], w[:, at:at + P], r[:, k, half * HALF:(half + 1) * HALF],
                                   start=(m == 0), stop=(m == len(terms) - 1))
                if kind == "wo" and m == 0:
                    add_x(slot, j)
            mm.then_inc(proj_done, 1)

        pe.wait_ge(const_loaded, 96)
        for i in range(NT):
            r = ROWS[i]
            pe.wait_ge(xn_ready, i + 1)
            if i >= 2:
                pe.wait_ge(hTf_ready, i - 1)
            for k in range(KD):
                at = (k % 4) * P
                mm = pe.transpose(bank[:, 2 * (i % 2) + k // 4, at:at + r], xn[i % 2][0:r, k * P:(k + 1) * P], ident[0:r, 0:r])
            mm.then_inc(xT_ready, 1)
        pe.wait_ge(hT_ready, NT)
        product("cq", 0)
        product("cq", 1)
        product("kv", 0)
        product("kr", 0)
        product("gr", 0)

        pe.wait_ge(consts_set, 1)
        pe.wait_ge(hTf_ready, NT)
        pe.wait_ge(proj_read[1], OUT_INDEX["cq", 1] // 2 + 1)
        pe.wait_ge(proj_read[0], OUT_INDEX["cq", 0] // 2 + 1)
        for half in range(2):
            for j in range(2):
                mm = pe.matmul(bank[:, half, 0:HALF], mean256[:, :], cqs[:, j, half * HALF:(half + 1) * HALF],
                               start=(j == 0), stop=(j == 1))
        mm.then_inc(lat_mean, 1)
        pe.wait_ge(proj_read[0], OUT_INDEX["kv", 0] // 2 + 1)
        for half in range(2):
            mm = pe.matmul(bank[:, 2 + half, 0:HALF], mean128[:, :], kvs[:, half * HALF:(half + 1) * HALF],
                           start=True, stop=True)
        mm.then_inc(lat_mean, 1)
        product("gr", 1)
        pe.wait_ge(caches_loaded, 32)
        pe.wait_ge(lat_rms, 2)
        for b in range(4):
            mm = pe.transpose(bank[:, 0, b * P:(b + 1) * P], caches[:, b // 2, b % 2, :], ident)
        mm.then_inc(cache_T, 1)
        product("gr", 2)
        pe.wait_ge(ckv_ready, 1)
        for i in range(4):
            pe.transpose(bank[:, 1, i * P:(i + 1) * P], ckvA[:, i * P:(i + 1) * P], ident)
        pe.transpose(bank[0:DEC, 2, 0:P], ckvA[:, SEQ + PAST:KEYS], ident)
        pe.wait_ge(kpe_ready, 1)
        for i in range(4):
            pe.transpose(bank[:, 2, P + i * ROPE:P + (i + 1) * ROPE], kpeA[64:96, i * P:(i + 1) * P], ident[64:96, 64:96])
        pe.transpose(bank[0:DEC, 2, 256:256 + ROPE], kpeA[64:96, SEQ + PAST:KEYS], ident[64:96, 64:96]).then_inc(out_T, 1)

        product("gr", 3)
        pe.wait_ge(cqn_ready, 1)
        for h in range(HEADS):
            product("uq", h)

        pe.wait_ge(kv_loaded, 32)
        pe.wait_ge(keys_ready, 1)
        for b in range(7):
            o, slot = take("V", b)
            r = P if b < 6 else DEC
            pe.matmul(proj[0:r, slot, 0, :], ckvA[:, b * P:b * P + r], w_kv[:, FF:2 * FF], start=True, stop=True)\
                .then_inc(proj_done, 1)

        def keys(hp):
            o, slot = take("K", hp)
            for half in range(2):
                mm = pe.matmul(proj[:, slot, half, 0:KEYS // 2], w_kv[:, hp * P:(hp + 1) * P],
                               ckvA[:, half * (KEYS // 2):(half + 1) * (KEYS // 2)], start=True, stop=True)
            mm.then_inc(proj_done, 1)

        def scores(u):
            hp, i, a = UNITS[u]
            h = 2 * hp + a
            r, q0, k0, n = unit_shape(i)
            if i == 0 and a == 0:
                ko = OUT_INDEX["K", hp]
                pe.wait_ge(proj_read[ko % 2], ko // 2 + 1)
                pe.wait_ge(q_ready, h + 2)
            if u == 0:
                pe.wait_ge(kcat_pe, 1)
                pe.wait_ge(out_copied, 1)
            if u >= 2:
                pe.wait_ge(exp_done, u - 1)
            mm = pe.matmul(bank[0:r, u % 2, 0:n], qT[0:QK, h, q0:q0 + r], kcat[hp % 2][0:QK, a, k0:k0 + n],
                           start=True, stop=(i == 4))
            if i < 4:
                mm = pe.matmul(bank[0:r, u % 2, n - P:n], qlow[0:1, :], khigh[0:1, :], start=False, stop=True)
            mm.then_inc(scores_ready, 1)

        def key_blocks(i):
            return [(b, P, b) for b in range(i + 1)] if i < 4 else [(0, P, 4), (1, P, 5), (2, DEC, 6)]

        def turn_probs(u):
            hp, i, a = UNITS[u]
            r = unit_shape(i)[0]
            pe.wait_ge(prob_ready, u + 1)
            if u >= 1:
                pe.wait_ge(probT_copied, u)
            for b, kr_, _ in key_blocks(i):
                mm = pe.transpose(bank[0:kr_, 2, b * r:(b + 1) * r], prob[u % 3][0:r, b * P:b * P + kr_], ident[0:r, 0:r])
            mm.then_inc(probT_done, 1)

        def pv(u):
            hp, i, a = UNITS[u]
            h = 2 * hp + a
            r = unit_shape(i)[0]
            v = u // 2
            pe.wait_ge(probT_copied, u + 1)
            if a == 0 and v >= 1:
                pe.wait_ge(oa_done, v)
            blocks = key_blocks(i)
            for b, kr_, vb in blocks:
                mm = pe.matmul(bank[64 * a:64 * a + 64, 3, 0:r],
                               V[0:kr_, vb, h * VD:(h + 1) * VD], probT[u % 2][0:kr_, b * r:(b + 1) * r],
                               start=(b == 0), stop=(b == len(blocks) - 1))
            mm.then_inc(pv_done, 1)

        keys(0)
        keys(1)
        NU = len(UNITS)
        for u in range(NU + 3):
            if u < NU:
                scores(u)
                if u % 10 == 0 and u // 10 in (1, 2):
                    keys(u // 10 + 1)
            if 2 <= u < NU + 2:
                turn_probs(u - 2)
            if u >= 3:
                pv(u - 3)

        for j in range(4):
            product("gq", j)
        for j in range(4):
            product("gk", j)
        pe.wait_ge(sides_loaded, 112)
        pe.wait_ge(oa_done, 20)
        for c in range(NT):
            L = ROWS[c]
            if c == 4:
                pe.wait_ge(gate_abs, 1)
                pe.wait_ge(gate_min, 1)
            pe.matmul(bank[0:L, c % 4, :], glr[0:RANK + 1, c * P:c * P + L], w_g2[0:RANK + 1, :], start=True, stop=True)\
                .then_inc(gate_done, 1)
        pe.wait_ge(gate_abs, NT)
        pe.wait_ge(gate_min, NT)
        def decays(c):
            L = ROWS[c]
            if c == 0:
                pe.wait_ge(la_ready, 2)
            else:
                pe.wait_ge(bS_ready, c)
            for h in range(GH):
                mm = pe.matmul(bank[:, cum_bank(c), h * P:h * P + L], la[0:L, c, h * DK:(h + 1) * DK], con("tri16")[0:L, 0:L],
                               start=True, stop=True)
            mm.then_inc(cum_done, 1)

        def turn_values(j):
            o = OUT_INDEX["gv", j]
            pe.wait_ge(proj_read[o % 2], o // 2 + 1)
            if j >= 2:
                pe.wait_ge(vtok_ready, j - 1)
            if j == EARLY_CUM:
                pe.wait_ge(bS_ready, 1)
            for i in range(4):
                pe.transpose(bank[:, j % 2, i * P:(i + 1) * P], gvT[j % 2][:, i * P:(i + 1) * P], ident)
            pe.transpose(bank[0:DEC, 2 + j % 2, 0:P], gvT[j % 2][:, SEQ:TOK], ident).then_inc(gvT_done, 1)

        for j in range(8):
            product("gv", j)
            if j >= 1:
                turn_values(j - 1)
            if j == EARLY_CUM:
                pe.wait_ge(vtok_ready, j - 1)
                decays(0)
        turn_values(7)
        pe.wait_ge(vtok_ready, 8)

        for c in range(NT):
            L = ROWS[c]
            exK, exQ2, exKd, exQ1, _ = chunk_views(L, c)
            if c + 1 < NT:
                decays(c + 1)
            pe.wait_ge(kq_ready, c + 1)
            if c >= 1:
                pe.wait_ge(att_masked, c)
                pe.wait_ge(kdT_copied, c)
            for h in range(GH):
                for s in range(L // SUB):
                    mm = pe.matmul(bank[32 * s:32 * s + 32, 1, h * P:h * P + L], exQ2[:, h, s, :], exK[:, h, s, :],
                                   start=True, stop=True)
            mm.then_inc(att_done, 1)
            for h in range(GH):
                mm = pe.transpose(bank[0:L, 3, h * P:(h + 1) * P], exKd[:, h, :], ident)
            mm.then_inc(kdT_done, 1)
            pe.wait_ge(att_masked, c + 1)
            if c >= 1:
                pe.wait_ge(attT_copied, c)
            for h in range(GH):
                mm = pe.transpose(bank[0:L, 2, h * P:h * P + L], att[0:L, h, 0:L], ident[0:L, 0:L])
            mm.then_inc(attT_done, 1)
            if c < 4:
                product("gr", EARLY_GR + c)
            o, slot = take("og", c)
            pe.wait_ge(attT_copied, c + 1)
            state = None
            if c == 4:
                pe.wait_ge(state_loaded, 16)
                state = S_smp
            elif c:
                pe.wait_ge(S_ready, c)
                state = S_st
            for n in range(8):
                h = n // 2
                out = proj[:, slot, n // 4, (n % 4) * P:(n % 4) * P + L]
                mm = pe.matmul(out, vtok[0:L, c, n * P:(n + 1) * P], attT[0:L, h, 0:L], start=True, stop=state is None)
                if state is not None:
                    mm = pe.matmul(out, state[:, h, (n % 2) * P:(n % 2 + 1) * P], exQ1[:, h, :], start=False, stop=True)
            mm.then_inc(proj_done, 1)
            o, slot = take("st", c)
            pe.wait_ge(kdT_copied, c + 1)
            for h in range(GH):
                mm = pe.matmul(proj[:, slot, h // 2, (h % 2) * DV:(h % 2 + 1) * DV], kdT[0:L, h, :],
                               vtok[0:L, c, h * DV:(h + 1) * DV], start=True, stop=True)
            mm.then_inc(proj_done, 1)

        def o_mean(h):
            o, slot = take("om", h)
            pe.wait_ge(osq_ready, h + 1)
            for half in range(2):
                for j in range(2):
                    mm = pe.matmul(proj[:, slot, half, 0:HALF], mean256[:, :], osq[h % 2][:, j, half * HALF:(half + 1) * HALF],
                                   start=(j == 0), stop=(j == 1))
            mm.then_inc(proj_done, 1)

        product("ga", 0)
        o_mean(0)
        o_mean(1)
        product("wa", 0)
        o_mean(2)
        o_mean(3)
        product("ga", 1)
        product("wa", 1)
        product("gb", 0)
        product("wb", 0)
        product("gb", 1)
        product("wb", 1)
        for j in range(2, 8):
            for kind in ("ga", "wa", "gb", "wb"):
                product(kind, j)
        for i in range(NT):
            pe.wait_ge(x_loaded[i], 32)
        pe.wait_ge(w_rt_ready, 1)

        def logits(j):
            pe.wait_ge(x2T_read, j + 1)
            for half in range(2):
                mm = pe.matmul(bank[0:64, 2 + half, 0:HALF], w_rt[:, j, :], yT[:, j, half * HALF:(half + 1) * HALF],
                               start=(j == 0), stop=(j == KD - 1))
            if j == KD - 1:
                mm.then_inc(logits_done, 1)

        for j in range(8):
            product("wo", j)
            if j >= 1:
                logits(j - 1)
        logits(7)

        def x2_rows(i):
            r = ROWS[i]
            if i in (0, 3):
                if i:
                    pe.wait_ge(x2_ready, 1)
                out = bank[:, 0:2, :]
            else:
                _, slot = take("x2", i)
                out = proj[:, slot, :, :]
            for j in range(8):
                mm = pe.transpose(out[0:r, j // 4, (j % 4) * P:(j % 4 + 1) * P], yT[:, j, i * P:i * P + r], ident)
            mm.then_inc(x2_turned, 1)

        for i in range(3):
            x2_rows(i)
        pe.wait_ge(lgT_copied, 1)
        for i in range(NT):
            r = ROWS[i]
            mm = pe.transpose(bank[0:r, 2, i * 64:(i + 1) * 64], lgT[:, i * P:i * P + r], ident[0:64, 0:64])
        mm.then_inc(lg_done, 1)
        for i in range(3, NT):
            x2_rows(i)
        pe.wait_ge(chosen, 1)
        pe.wait_ge(x2_ready, NT)
        Mf = picks[:, :, :].rearrange("p i e -> p (i e)")
        pe.matmul(bank[:, 0, 0:NT * NE], con("before"), Mf, start=True, stop=True)
        pe.matmul(bank[:, 1, 0:NT * NE], ones[:, :], Mf, start=True, stop=True).then_inc(ranks_done, 1)

        pe.wait_ge(onehots_ready, 2)
        pe.wait_ge(onehots_i_ready, 1)
        at = bank[:, 3, 0:NBLK]
        for n in range(2 * NT):
            pe.matmul(at, lanes[:, n, :], q_p[:, n, :], start=(n == 0), stop=False)
            mm = pe.matmul(at, lanes[:, n, :], q_i[:, n, :], start=False, stop=(n == 2 * NT - 1))
        for i in range(NT):
            mm = pe.matmul(bank[:, 2, 0:NBLK], lanes[:, NT + i, :], q_c[:, i, :], start=(i == 0), stop=(i == NT - 1))
        mm.then_inc(maps_done, 1)

        pe.wait_ge(proj_read[0], len([o for o in range(len(OUT)) if o % 2 == 0]))
        pe.wait_ge(proj_read[1], len([o for o in range(len(OUT)) if o % 2 == 1]))
        pe.wait_ge(gidx_ready, 1)

        def up(s, cols, wg, wu, done):
            for k in range(KD):
                pe.matmul(proj[0:SLOTS, s, 0, :], xsT[:, k, cols], wg[:, k * FF:(k + 1) * FF],
                          start=(k == 0), stop=(k == KD - 1))
                mm = pe.matmul(proj[64:64 + SLOTS, s, 0, :], xsT[:, k, cols], wu[:, k * FF:(k + 1) * FF],
                               start=(k == 0), stop=(k == KD - 1))
            mm.then_inc(done, 1)

        def turn_hidden(s, done):
            for k in range(4):
                mm = pe.transpose(bank[:, 2 + s, k * SLOTS:(k + 1) * SLOTS], hg[0:SLOTS, s, k * P:(k + 1) * P],
                                  ident[0:SLOTS, 0:SLOTS])
            mm.then_inc(done, 1)

        def down(s, wd, done):
            for k in range(4):
                pe.matmul(proj[0:SLOTS, s, 1, :], hT2[:, s, k, :], wd[:, k * D:k * D + FF], start=(k == 0), stop=(k == 3))
                mm = pe.matmul(proj[64:64 + SLOTS, s, 1, :], hT2[:, s, k, :], wd[:, k * D + FF:(k + 1) * D],
                               start=(k == 0), stop=(k == 3))
            mm.then_inc(done, 1)

        def pair(it, m):
            pe.wait_ge(xs_loaded, it * (16 * NSETS) + 16 * m + 16)
            for k in range(KD):
                mm = pe.transpose(bank[:, k // 4, (k % 4) * P:(k % 4 + 1) * P], xsb[:, k * P:(k + 1) * P], ident)
            mm.then_inc(xsT_done, 1)
            pe.wait_ge(xsT_copied, it * NSETS + m + 1)
            for s in range(2):
                u = 2 * m + s
                w = we[u % NSETS]
                for part in range(2):
                    pe.wait_ge(we_loaded[u % NSETS][part], it * 32 + 16 * (u // NSETS) + 16)
                up(s, slice(s * SLOTS, (s + 1) * SLOTS), w[0], w[1], up_done)
            for s in range(2):
                u = 2 * m + s
                pe.wait_ge(consts_set, 1)
                pe.wait_ge(act_done[s], it * NSETS + m + 1)
                turn_hidden(s, hT2_done)
                pe.wait_ge(hT2_copied[s], it * NSETS + m + 1)
                pe.wait_ge(we_loaded[u % NSETS][2], it * 32 + 16 * (u // NSETS) + 16)
                down(s, we[u % NSETS][2], down_done)

        run_pairs(pe, pair)
        pe.wait_ge(yo_ready, NE)
        pe.wait_ge(meta_ready, 1)
        n_more = pe.value_load(meta[0:1, NOVER:NOVER + 1], min_val=0, max_val=NOVER)
        with pe.If(n_more > 0):
            with pe.Fori(0, NOVER) as b:
                with pe.If(b < n_more):
                    pe.wait_ge(more_x, b * 16 + 16)
                    for k in range(KD):
                        mm = pe.transpose(bank[:, k // 4, (k % 4) * P:(k % 4 + 1) * P], xsb[:, k * P:(k + 1) * P], ident)
                    mm.then_inc(more_xT, 1)
                    pe.wait_ge(more_xT_copied, b + 1)
                    pe.wait_ge(more_w, b * 48 + 48)
                    up(0, slice(0, SLOTS), we[0][0], we[0][1], more_up)
                    pe.wait_ge(consts_set, 1)
                    pe.wait_ge(more_act, b + 1)
                    turn_hidden(0, more_hT)
                    pe.wait_ge(more_hT_copied, b + 1)
                    down(0, we[0][2], more_down)

    @block.scalar
    def _(act):
        step = Steps(act, act_seq)
        need = [0] * NRAW

        def high(n):
            c = split_columns(n)
            need[n % NRAW] += 16 * n_loads(WT[n])
            act.wait_ge(w_loaded[n % NRAW], need[n % NRAW])
            nc.scalar.copy(whi[n % NHIGH][:, 0:c], raw[n % NRAW][:, 0:c]).then_inc(w_high, 1)

        def out_of(kind, j):
            o = OUT_INDEX[kind, j]
            act.wait_ge(proj_done, o + 1)
            w = OUT[o][2]
            if w is not None and LAST_OUT[w] == o and w + NHIGH < len(WT):
                high(w + NHIGH)
            return o, proj[:, o % 2, :, 0:HALF]

        def halves(ap):
            return ap.rearrange("p (a b) -> p a b", a=2)

        def root_mean_square(junk, src, out, done):
            step(nc.scalar.activation(junk, src, ACT.Square, accum_out=out))
            step.settle()
            nc.scalar.activation(out, out, ACT.Sqrt, scale=1.0 / D, bias=eps_col[0:out.shape[0], :]).then_inc(done, 1)

        act.wait_ge(consts_set, 1)

        def x_root(i):
            r = ROWS[i]
            act.wait_ge(x_loaded[i], 16)
            root_mean_square(squares[0:r, :], X[0:r, i, :], st_x[0:r, 0, i:i + 1], x_rms)

        for i in range(3):
            x_root(i)
        for i in range(NT):
            hT_high(nc, act, i, hTf_ready, hT_hi, hT_f, hT_hi_ready)
            if i + 3 < NT:
                x_root(i + 3)
            if 1 <= i <= NHIGH:
                high(i - 1)

        def output_gate(j):
            o, ps = out_of("gr", j)
            nc.scalar.activation(halves(grs[:, j, :]), ps, ACT.Silu).then_inc(proj_read[o % 2], 1)

        for j in range(2):
            o, ps = out_of("cq", j)
            nc.scalar.copy(halves(cq[:, j, :]), ps)
            nc.scalar.activation(halves(cqs[:, j, :]), ps, ACT.Square).then_inc(proj_read[o % 2], 1)
        o, ps = out_of("kv", 0)
        nc.scalar.copy(halves(kvr[:, :]), ps)
        nc.scalar.activation(halves(kvs[:, :]), ps, ACT.Square).then_inc(proj_read[o % 2], 1)
        o, ps = out_of("kr", 0)
        act.wait_ge(consts_set, 1)
        nc.scalar.copy(halves(kr[:, :]), ps)
        nc.scalar.copy(halves(glr[0:RANK, :]), ps[0:RANK]).then_inc(proj_read[o % 2], 1)
        act.wait_ge(xn_ready, NT)
        output_gate(0)
        for n, root in enumerate((rq, rk)):
            act.wait_ge(lat_mean, n + 1)
            nc.scalar.activation(halves(root[:, :]), bank[:, 2 * n:2 * n + 2, 0:HALF], ACT.Sqrt, bias=eps_col[:, :]).then_inc(lat_rms, 1)
        for j in range(1, EARLY_GR):
            output_gate(j)
        for h in range(HEADS):
            o, ps = out_of("uq", h)
            nc.scalar.mul(halves(qT[:, h, :]), ps, -ATT_SCALE).then_inc(proj_read[o % 2], 1)
        for b in range(7):
            o, _ = out_of("V", b)
            r = P if b < 6 else DEC
            nc.scalar.copy(V[0:r, b, :], proj[0:r, o % 2, 0, :]).then_inc(proj_read[o % 2], 1)

        def keys(hp):
            o, _ = out_of("K", hp)
            if hp >= 2:
                act.wait_ge(scores_ready, 10 * (hp - 1))
            if hp == 0:
                act.wait_ge(cqn_ready, 1)
            for a in range(2):
                last = nc.scalar.copy(kcat[hp % 2][0:NOPE, a, :].rearrange("p (c k) -> p c k", c=2),
                                      proj[64 * a:64 * a + 64, o % 2, :, 0:KEYS // 2])
            last.then_inc(proj_read[o % 2], 1)

        keys(0)
        keys(1)

        def exps(u):
            hp, i, a = UNITS[u]
            r, _, _, n = unit_shape(i)
            act.wait_ge(negmax_ready, u + 1)
            if u >= 3:
                act.wait_ge(probT_done, u - 2)
            nc.scalar.activation(prob[u % 3][0:r, 0:n], bank[0:r, u % 2, 0:n], ACT.Exp, bias=stat[0:r, 1, u:u + 1],
                                 scale=-1.0, accum_out=stat[0:r, 2, u:u + 1]).then_inc(exp_done, 1)

        def copy_turned(u):
            _, i, _ = UNITS[u]
            n = unit_shape(i)[3]
            act.wait_ge(probT_done, u + 1)
            if u >= 2:
                act.wait_ge(pv_done, u - 1)
            if i < 4:
                nc.scalar.copy(probT[u % 2][:, 0:n], bank[:, 2, 0:n]).then_inc(probT_copied, 1)
            else:
                nc.scalar.copy(probT[u % 2][:, 0:2 * DEC], bank[:, 2, 0:2 * DEC])
                nc.scalar.copy(probT[u % 2][0:DEC, 2 * DEC:3 * DEC], bank[0:DEC, 2, 2 * DEC:3 * DEC]).then_inc(probT_copied, 1)

        NU = len(UNITS)
        for u in range(NU + 2):
            if u < NU:
                exps(u)
                if u % 10 == 0 and u // 10 in (1, 2):
                    keys(u // 10 + 1)
            if u >= 2:
                copy_turned(u - 2)

        act.wait_ge(pv_done, NU)
        act.wait_ge(oa_done, NU // 2)
        act.wait_ge(lat_stored, 64)
        for j in range(4):
            o, ps = out_of("gq", j)
            nc.scalar.mul(halves(gqk[:, j, :]), ps, float(DK) ** -0.5).then_inc(proj_read[o % 2], 1)
        for j in range(4):
            o, ps = out_of("gk", j)
            nc.scalar.copy(halves(gqk[:, 4 + j, :]), ps).then_inc(proj_read[o % 2], 1)
        for c in range(NT):
            L = ROWS[c]
            act.wait_ge(gate_min, c + 1)
            nc.scalar.activation(la[0:L, c, :], bank[0:L, c % 4, :], ACT.Abs).then_inc(gate_abs, 1)
        act.wait_ge(gate_abs, NT)
        for func, scale, bias in ((ACT.Exp, -1.0, 0.0), (ACT.Ln, 1.0, 1.0)):
            step(nc.scalar.activation(la[:, 0:4, :], la[:, 0:4, :], func, bias=bias, scale=scale))
            step(nc.scalar.activation(la[0:DEC, 4, :], la[0:DEC, 4, :], func, bias=bias, scale=scale))
            step.settle()
        nc.scalar.nop().then_inc(la_log, 1)
        def copy_decays(c):
            L = ROWS[c]
            act.wait_ge(cum_done, c + 1)
            if c == 0:
                act.wait_ge(la_ready, 2)
            else:
                act.wait_ge(ex_ready, c)
            nc.scalar.copy(bS[:, :, 0:L], bank[:, cum_bank(c), :].rearrange("p (h l) -> p h l", h=GH)[:, :, 0:L]).then_inc(bS_ready, 1)

        def exponentials(c):
            L = ROWS[c]
            _, _, _, exQ1, exD = chunk_views(L, c)
            act.wait_ge(bS_ready, c + 1)
            act.wait_ge(ex_arg, c + 1)
            if c >= 2:
                act.wait_ge(S_ready, c - 1)
            n = GH * (L // SUB) * L + 2 * GH * L
            nc.scalar.activation(ex[:, 0:n], ex[:, 0:n], ACT.Exp)
            nc.scalar.activation(exQ1, bS[:, :, 0:L], ACT.Exp)
            nc.scalar.activation(exD, bS[:, :, L - 1:L], ACT.Exp).then_inc(ex_ready, 1)

        for j in range(8):
            o, ps = out_of("gv", j)
            if j >= 2:
                act.wait_ge(gvT_done, j - 1)
            nc.scalar.copy(halves(gvT[j % 2][:, :]), ps).then_inc(proj_read[o % 2], 1)
            if j == EARLY_CUM:
                copy_decays(0)
            if j == EARLY_CUM + 1:
                exponentials(0)

        for c in range(NT):
            L = ROWS[c]
            if c + 1 < NT:
                copy_decays(c + 1)
            act.wait_ge(kdT_done, c + 1)
            if c:
                act.wait_ge(proj_done, OUT_INDEX["st", c - 1] + 1)
            nc.scalar.copy(kdT[0:L, :, :], bank[0:L, 3, :].rearrange("p (h l) -> p h l", h=GH)).then_inc(kdT_copied, 1)
            act.wait_ge(attT_done, c + 1)
            nc.scalar.copy(attT[0:L, :, 0:L], bank[0:L, 2, :].rearrange("p (h l) -> p h l", h=GH)[:, :, 0:L])\
                .then_inc(attT_copied, 1)
            if c + 1 < NT:
                exponentials(c + 1)
            if c < 4:
                output_gate(EARLY_GR + c)
            o, _ = out_of("og", c)
            src = proj[:, o % 2, :, :].rearrange("p a (n l) -> p (a n) l", n=4)[:, :, 0:L]
            nc.scalar.copy(gqk[:, :, c * P:c * P + L], src).then_inc(proj_read[o % 2], 1)

        def o_squares(h):
            if h >= 2:
                act.wait_ge(proj_done, OUT_INDEX["om", h - 2] + 1)
            nc.scalar.activation(osq[h % 2][:, :, :], gqk[:, 2 * h:2 * h + 2, :], ACT.Square).then_inc(osq_ready, 1)

        def o_root(h):
            o, ps = out_of("om", h)
            if h >= 2:
                act.wait_ge(og_ready, h - 1)
            nc.scalar.activation(halves(ors[h % 2][:, :]), ps, ACT.Sqrt, bias=eps_col[:, :]).then_inc(proj_read[o % 2], 1)

        def o_high(h):
            act.wait_ge(og_ready, h + 1)
            nc.scalar.copy(ob_hi[:, 2 * h:2 * h + 2, :], gqk[:, 2 * h:2 * h + 2, :]).then_inc(ob_high, 1)

        def gate_value(n, kind, j):
            o, ps = out_of(kind, j)
            if j >= 1:
                u = OUT_INDEX[("wa", "wb")[n], j - 1]
                act.wait_ge(proj_read[u % 2], u // 2 + 1)
            nc.scalar.activation(halves(sg[n][:, :]), ps, ACT.Sigmoid).then_inc(proj_read[o % 2], 1)

        ogo = OUT_INDEX["og", 4]
        act.wait_ge(proj_read[ogo % 2], ogo // 2 + 1)
        o_squares(0)
        o_squares(1)
        gate_value(0, "ga", 0)
        o_root(0)
        o_squares(2)
        o_root(1)
        o_squares(3)
        out_of("wa", 0)
        o_high(0)
        o_root(2)
        o_high(1)
        o_root(3)
        gate_value(0, "ga", 1)
        o_high(2)
        out_of("wa", 1)
        o_high(3)
        for j in range(8):
            if j >= 2:
                gate_value(0, "ga", j)
                out_of("wa", j)
            gate_value(1, "gb", j)
            out_of("wb", j)

        for j in range(8):
            o, ps = out_of("wo", j)
            nc.scalar.copy(halves(yT[:, j, :]), ps).then_inc(x2T_read, 1)
            act.wait_ge(x2T_read, j + 1)
            act.sem_inc(proj_read[o % 2], 1)
        act.wait_ge(logits_done, 1)
        nc.scalar.copy(halves(lgT[:, :]), bank[0:64, 2:4, 0:HALF]).then_inc(lgT_copied, 1)

        for i in range(NT):
            r = ROWS[i]
            act.wait_ge(x2_turned, i + 1)
            step(nc.scalar.activation(h2[0:r, i, :].rearrange("p (a b) -> p a b", a=2), x2_source(i)[0:r], ACT.Square,
                                      accum_out=st_x[0:r, 1, i:i + 1]))
            step.settle()
            act.sem_inc(x2_squared, 1)
        nc.scalar.activation(st_x[:, 1, :], st_x[:, 1, :], ACT.Sqrt, scale=1.0 / D, bias=eps_col[:, :]).then_inc(x2_rms, 1)
        act.wait_ge(x2_inv, 1)
        for i in range(NT):
            r = ROWS[i]
            act.wait_ge(x2_ready, i + 1)
            nc.scalar.mul(h2[0:r, i, :], X[0:r, i, :], st_x[0:r, 4, i:i + 1]).then_inc(h2_ready, 1)
        for n in range(2):
            act.wait_ge(rt_exp_in, n + 1)
            v = (rG, rd)[n]
            nc.scalar.activation(v, v, ACT.Exp).then_inc(rt_exp_out, 1)

        def pair(it, m):
            for s in range(2):
                act.wait_ge(up_done, it * (2 * NSETS) + 2 * m + s + 1)
                nc.scalar.activation(hg[0:SLOTS, s, :], proj[0:SLOTS, s, 0, :], ACT.Silu).then_inc(silu_done, 1)

        run_pairs(act, pair)
        act.wait_ge(hT2_done, NE)
        act.wait_ge(meta_ready, 1)
        n_more = act.value_load(meta[0:1, NOVER:NOVER + 1], min_val=0, max_val=NOVER)
        with act.If(n_more > 0):
            with act.Fori(0, NOVER) as b:
                with act.If(b < n_more):
                    act.wait_ge(more_up, b + 1)
                    nc.scalar.activation(hg[0:SLOTS, 0, :], proj[0:SLOTS, 0, 0, :], ACT.Silu).then_inc(more_silu, 1)

        def last_scale(i):
            r = ROWS[i]
            act.wait_ge(comb_inv, i + 1)
            nc.scalar.mul(zo[i][0:r, :], X[0:r, i, :], st_x[0:r, 5, i:i + 1]).then_inc(y_scaled, 1)

        for i in range(NT):
            r = ROWS[i]
            act.wait_ge(comb_done, i + 1)
            root_mean_square(zo[i][0:r, :], X[0:r, i, :], st_x[0:r, 2, i:i + 1], comb_rms)
            if i:
                last_scale(i - 1)

    @block.vector
    def _(dve):
        step = Steps(dve, dve_seq)
        v = nc.vector

        def out_of(kind, j):
            o = OUT_INDEX[kind, j]
            dve.wait_ge(proj_done, o + 1)
            return o, proj[:, o % 2, :, 0:HALF]

        def halves(ap):
            return ap.rearrange("p (a b) -> p a b", a=2)

        def inverse(out, root):
            step(v.reciprocal(out, root))
            step.settle()

        v.memset(eps_col[:, :], EPS)
        v.memset(mean256[:, :], 1.0 / 256)
        v.memset(mean128[:, :], 1.0 / 128)
        v.memset(ones[:, :], 1.0)
        v.memset(qlow[0:1, 0:64], 1.0)
        v.memset(qlow[0:1, 64:P], 0.0)
        v.memset(khigh[0:1, 0:64], 0.0)
        v.memset(khigh[0:1, 64:P], BIG)
        v.memset(w_rt[:, :, GROUPS + NE:], 0.0)
        v.memset(st_x[:, 1, :], 1.0)
        v.memset(caches[:, 1, :, 0:64], 0.0)
        v.memset(caches[:, 1, :, 96:P], 0.0)
        v.memset(glr[0:RANK + 1, :], 1.0).then_inc(consts_set, 1)

        def normed(i):
            r = ROWS[i]
            dve.wait_ge(x_rms, i + 1)
            inverse(st_x[0:r, 3, i:i + 1], st_x[0:r, 0, i:i + 1])
            v.tensor_scalar(xn[i % 2][0:r, :], X[0:r, i, :], st_x[0:r, 3, i:i + 1], None, ALU.mult).then_inc(xn_ready, 1)

        normed(0)
        normed(1)
        dve.wait_ge(const_loaded, 96)
        for i in range(NT):
            r = ROWS[i]
            dve.wait_ge(xT_ready, i + 1)
            for b in range(2):
                src = bank[:, 2 * (i % 2) + b, :].rearrange("p (k c) -> p k c", k=4)[:, :, 0:r]
                last = v.tensor_tensor(hT_f[i][:, 4 * b:4 * b + 4, 0:r], src,
                                       g_mix[:, 4 * b:4 * b + 4].unsqueeze(2).to_broadcast([P, 4, r]), ALU.mult)
            last.then_inc(hTf_ready, 1)
            if i + 2 < NT:
                normed(i + 2)
            if i - 1 in DVE_LOW:
                hT_low(nc.vector, dve, i - 1, hT_hi_ready, hT_hi, hT_lo, hT_f, hT_ready)
        hT_low(nc.vector, dve, NT - 1, hT_hi_ready, hT_hi, hT_lo, hT_f, hT_ready)

        dve.wait_ge(lat_rms, 1)
        inverse(rq[:, :], rq[:, :])
        for j in range(2):
            step(v.scalar_tensor_tensor(cq[:, j, :], cq[:, j, :], g_q[:, j:j + 1], rq[:, :], ALU.mult, ALU.mult))
        step.settle()
        step(v.tensor_copy(cqn_hi[:, :, :], cq[:, :, :]))
        step.settle()
        v.tensor_tensor(cqn_lo[:, :, :], cq[:, :, :], cqn_hi[:, :, :].bitcast(F32), ALU.subtract).then_inc(cqn_ready, 1)
        dve.wait_ge(lat_rms, 2)
        inverse(rk[:, :], rk[:, :])
        for dst, c0, n in ((0, 0, SEQ), (SEQ + PAST, SEQ, DEC)):
            last = v.scalar_tensor_tensor(ckvA[:, dst:dst + n], kvr[:, c0:c0 + n], g_kv[:, 0:1], rk[:, c0:c0 + n],
                                          ALU.mult, ALU.mult)
        last.then_inc(ckv_ready, 1)
        o = OUT_INDEX["kr", 0]
        dve.wait_ge(proj_read[o % 2], o // 2 + 1)

        def rotate(src, outs, done):
            step.settle()
            step(v.tensor_tensor(rtmp[64:96, 0, :], src[64:96], con("rope")[64:96], ALU.mult))
            step(v.tensor_tensor(rtmp[64:96, 1, :], src[96:128], con("rope")[96:128], ALU.mult))
            step.settle()
            for dst, c0, n in outs:
                last = v.tensor_tensor(dst, rtmp[64:96, 0, c0:c0 + n], rtmp[64:96, 1, c0:c0 + n], ALU.add)
            last.then_inc(done, 1)
            dve.wait_ge(done, rotated[done.name])
            rotated[done.name] += 1

        rotated = {kpe_ready.name: 1, q_ready.name: 1}
        rotate(kr[:, :], ((kpeA[64:96, 0:SEQ], 0, SEQ), (kpeA[64:96, SEQ + PAST:KEYS], SEQ, DEC)), kpe_ready)
        dve.wait_ge(cache_T, 1)
        v.tensor_copy(ckvA[:, SEQ:SEQ + PAST], bank[:, 0, 0:2 * P])
        v.tensor_copy(kpeA[64:96, SEQ:SEQ + PAST], bank[64:96, 0, 2 * P:4 * P]).then_inc(keys_ready, 1)
        dve.wait_ge(out_T, 1)
        v.tensor_copy(obuf[:, 0:4, :], bank[:, 1, :].rearrange("p (c d) -> p c d", c=4))
        v.tensor_copy(obuf[0:DEC, 4, :], bank[0:DEC, 2, 0:P])
        v.tensor_copy(kbuf[:, 0:4, :], bank[:, 2, P:2 * P].rearrange("p (c d) -> p c d", c=4))
        v.tensor_copy(kbuf[0:DEC, 4, :], bank[0:DEC, 2, 256:256 + ROPE]).then_inc(out_copied, 1)
        dve.wait_ge(keys_ready, 1)
        dve.wait_ge(cqn_ready, 1)
        for n in range(2):
            for a in range(2):
                last = v.tensor_copy(kcat[n][64:96, a, :], kpeA[64:96, :])
        last.then_inc(kcat_pe, 1)
        for h in range(HEADS):
            o = OUT_INDEX["uq", h]
            dve.wait_ge(proj_read[o % 2], o // 2 + 1)
            rotate(qT[:, h, :], ((qT[64:96, h, :], 0, TOK),), q_ready)

        def maximum(u):
            hp, i, a = UNITS[u]
            r, _, _, n = unit_shape(i)
            dve.wait_ge(scores_ready, u + 1)
            v.tensor_reduce(stat[0:r, 1, u:u + 1], bank[0:r, u % 2, 0:n], AX.X, ALU.min).then_inc(negmax_ready, 1)

        def normalise(u):
            hp, i, a = UNITS[u]
            r, _, _, n = unit_shape(i)
            dve.wait_ge(exp_done, u + 1)
            step(v.reciprocal(stat[0:r, 3, u:u + 1], stat[0:r, 2, u:u + 1]))
            step.settle()
            v.tensor_scalar(prob[u % 3][0:r, 0:n], prob[u % 3][0:r, 0:n], stat[0:r, 3, u:u + 1], None, ALU.mult)\
                .then_inc(prob_ready, 1)

        def copy_out(w):
            hp, i, _ = UNITS[2 * w]
            r, q0, _, _ = unit_shape(i)
            dve.wait_ge(pv_done, 2 * w + 2)
            src = bank[:, 3, 0:r]
            step(v.tensor_copy(oa_hi[:, hp, q0:q0 + r], src))
            step.settle()
            v.tensor_tensor(oa_lo[:, hp, q0:q0 + r], src, oa_hi[:, hp, q0:q0 + r].bitcast(F32), ALU.subtract).then_inc(oa_done, 1)

        NU = len(UNITS)
        for u in range(NU + 4):
            if u >= 5 and u % 2 == 1:
                copy_out((u - 5) // 2)
            if u < NU:
                maximum(u)
            if 1 <= u <= NU:
                normalise(u - 1)

        for c in range(NT):
            L = ROWS[c]
            dve.wait_ge(gate_done, c + 1)
            v.tensor_scalar(lmin[0:L, c, :], bank[0:L, c % 4, :], 0.0, None, ALU.min).then_inc(gate_min, 1)
        dve.wait_ge(gate_min, NT)
        dve.wait_ge(la_log, 1)
        v.tensor_tensor(la[:, 0:4, :], lmin[:, 0:4, :], la[:, 0:4, :], ALU.subtract).then_inc(la_ready, 1)
        v.tensor_tensor(la[0:DEC, 4, :], lmin[0:DEC, 4, :], la[0:DEC, 4, :], ALU.subtract).then_inc(la_ready, 1)
        def exponents(c):
            L = ROWS[c]
            ns = L // SUB
            exK, exQ2, exKd, _, _ = chunk_views(L, c)
            b = bS[:, :, 0:L]
            bs = b.rearrange("p h (s l) -> p h s l", l=SUB)
            mid = bs[:, :, :, SUB // 2 - 1:SUB // 2]
            dve.wait_ge(bS_ready, c + 1)
            if c:
                dve.wait_ge(att_done, c)
                dve.wait_ge(kdT_done, c)
            for h in range(GH):
                step(v.tensor_tensor(exK[:, h], mid[:, h].to_broadcast([P, ns, L]),
                                     b[:, h].unsqueeze(1).to_broadcast([P, ns, L]), ALU.subtract))
            step.settle()
            step(v.tensor_scalar(ex[:, 0:GH * ns * L], ex[:, 0:GH * ns * L], EXP_CAP, None, ALU.min))
            step(v.tensor_tensor(exQ2, bs, mid.to_broadcast([P, GH, ns, SUB]), ALU.subtract))
            v.tensor_tensor(exKd, b[:, :, L - 1:L].to_broadcast([P, GH, L]), b, ALU.subtract).then_inc(ex_arg, 1)

        def decayed(c):
            L = ROWS[c]
            ns = L // SUB
            tok = slice(c * P, c * P + L)
            exK, exQ2, exKd, exQ1, _ = chunk_views(L, c)
            q, k = gqk[:, 0:GH, tok], gqk[:, GH:2 * GH, tok]
            dve.wait_ge(ex_ready, c + 1)
            dve.wait_ge(ex_arg, c + 1)
            for h in range(GH):
                v.tensor_tensor(exK[:, h], exK[:, h], k[:, h].unsqueeze(1).to_broadcast([P, ns, L]), ALU.mult)
            v.tensor_tensor(exQ2, exQ2, q.rearrange("p h (s l) -> p h s l", l=SUB), ALU.mult)
            v.tensor_tensor(exQ1, exQ1, q, ALU.mult)
            v.tensor_tensor(exKd, exKd, k, ALU.mult).then_inc(kq_ready, 1)

        for j in range(8):
            dve.wait_ge(gvT_done, j + 1)
            v.tensor_copy(vtok[:, 0:4, j * P:(j + 1) * P], bank[:, j % 2, :].rearrange("p (i l) -> p i l", i=4))
            v.tensor_copy(vtok[0:DEC, 4, j * P:(j + 1) * P], bank[0:DEC, 2 + j % 2, 0:P]).then_inc(vtok_ready, 1)
            if j == EARLY_CUM - 1:
                exponents(0)
            if j == EARLY_CUM + 1:
                decayed(0)

        def new_state(c):
            _, _, _, _, exD = chunk_views(ROWS[c], c)
            o, _ = out_of("st", c)
            new = proj[:, o % 2, :, :].rearrange("p a (n v) -> p (a n) v", v=DV)
            state = S_smp if c == 4 else S_st
            if c == 0:
                step(v.tensor_copy(state[:, :, :], new))
            else:
                if c == 4:
                    dve.wait_ge(state_loaded, 16)
                for h in range(GH):
                    step(v.scalar_tensor_tensor(state[:, h, :], state[:, h, :], exD[:, h, :], new[:, h, :], ALU.mult, ALU.add))
            step.settle()
            v.nop().then_inc(S_ready, 1)
            dve.sem_inc(proj_read[o % 2], 1)

        dve.wait_ge(sides_loaded, 112)
        v.tensor_tensor(w_rt[:, :, :], w_rt[:, :, :], g_ffn[:, :].unsqueeze(2).to_broadcast([P, KD, 64]), ALU.mult)\
            .then_inc(w_rt_ready, 1)

        for c in range(NT):
            L = ROWS[c]
            dve.wait_ge(att_done, c + 1)
            if c:
                dve.wait_ge(attT_done, c)
            v.tensor_tensor(att[0:L, :, 0:L], bank[0:L, 1, :].rearrange("p (h l) -> p h l", h=GH)[:, :, 0:L],
                            con("causal")[0:L, 0:L].unsqueeze(1).to_broadcast([L, GH, L]), ALU.mult).then_inc(att_masked, 1)
            if c + 1 < NT:
                exponents(c + 1)
                decayed(c + 1)
            new_state(c)

        def normed_output(h):
            o = OUT_INDEX["om", h]
            r2 = ors[h % 2]
            dve.wait_ge(proj_read[o % 2], o // 2 + 1)
            inverse(r2[:, :], r2[:, :])
            dve.wait_ge(og_gated, h + 1)
            og = gqk[:, 2 * h:2 * h + 2, :]
            for n in range(2):
                last = v.scalar_tensor_tensor(og[:, n, :], og[:, n, :], g_gla[:, n:n + 1], r2[:, :], ALU.mult, ALU.mult)
            last.then_inc(og_ready, 1)

        def branch(n, j):
            g = OUT_INDEX[("ga", "gb")[n], j]
            dve.wait_ge(proj_read[g % 2], g // 2 + 1)
            o, ps = out_of(("wa", "wb")[n], j)
            dst = mtmp if n else msum1 if j == 1 else msum
            v.tensor_tensor(halves(dst[:, :]), ps, halves(sg[n][:, :]), ALU.mult).then_inc(proj_read[o % 2], 1)
            dve.wait_ge(proj_read[o % 2], o // 2 + 1)

        normed_output(0)
        branch(0, 0)
        normed_output(1)
        normed_output(2)
        normed_output(3)
        dve.wait_ge(S_stored, 32)
        branch(0, 1)
        for j in range(8):
            if j >= 2:
                branch(0, j)
            branch(1, j)
            step(v.tensor_tensor(mtmp[:, :], mtmp[:, :], (msum1 if j == 1 else msum)[:, :], ALU.add))
            step.settle()
            step(v.tensor_copy(mg_hi[:, j, :], mtmp[:, :]))
            step.settle()
            v.tensor_tensor(mg_lo[:, j, :], mtmp[:, :], mg_hi[:, j, :].bitcast(F32), ALU.subtract).then_inc(mg_ready, 1)
            dve.wait_ge(mg_ready, j + 1)

        dve.wait_ge(proj_done, OUT_INDEX["wo", 7] + 1)
        step(v.memset(LG[:, :, :], 0.0))
        for i in range(NT):
            r = ROWS[i]
            dve.wait_ge(x2_squared, i + 1)
            v.tensor_copy(X[0:r, i, :].rearrange("p (a b) -> p a b", a=2), x2_source(i)[0:r]).then_inc(x2_ready, 1)
            if i not in (0, 3):
                dve.wait_ge(x2_ready, i + 1)
                dve.sem_inc(proj_read[OUT_INDEX["x2", i] % 2], 1)
        dve.wait_ge(x2_rms, 1)
        v.reciprocal(st_x[:, 4, :], st_x[:, 1, :]).then_inc(x2_inv, 1)
        dve.wait_ge(x2_inv, 1)
        dve.wait_ge(lg_done, 1)
        raw_logits = bank[:, 2, 0:NT * 64].rearrange("p (i c) -> p i c", i=NT)[:, :, 0:GROUPS + NE]
        for r, a, b in ((P, 0, 4), (DEC, 4, 5)):
            step(v.tensor_tensor(LG[0:r, a:b, :], raw_logits[0:r, a:b], st_x[0:r, 4, a:b].unsqueeze(2).to_broadcast([r, b - a, GROUPS + NE]),
                                 ALU.mult))
        step.settle()
        for r, a, b in ((P, 0, 4), (DEC, 4, 5)):
            step(v.tensor_tensor(LG[0:r, a:b, :], LG[0:r, a:b, :], b_rt[0:r, :].unsqueeze(1).to_broadcast([r, b - a, GROUPS + NE]),
                                 ALU.add))
        step.settle()

        def bc(ap, n):
            return ap.unsqueeze(2).to_broadcast([P, NT, n])

        def row(name, n):
            return con(name).unsqueeze(1).to_broadcast([P, NT, n])

        def run(ins):
            step(ins)
            step.settle()

        def first_max(out, val, m, iota, n):
            run(v.tensor_tensor(out, val, bc(m, n), ALU.is_equal))
            run(v.tensor_tensor(out, out, row(iota, n), ALU.mult))
            run(v.tensor_reduce(r5[2], out, AX.X, ALU.min))
            run(v.tensor_tensor(out, row(iota, n), bc(r5[2], n), ALU.is_equal))

        G_, E_l = LG[:, :, 0:GROUPS], LG[:, :, GROUPS:]
        run(v.tensor_reduce(r5[0], G_, AX.X, ALU.max))
        v.tensor_tensor(rG, G_, bc(r5[0], GROUPS), ALU.subtract).then_inc(rt_exp_in, 1)
        first_max(rOG, G_, r5[0], "iota4", GROUPS)
        run(v.tensor_scalar(rPen, rOG, 1.0, BIG, ALU.subtract, ALU.mult))
        em = rE.rearrange("p i (g e) -> p i g e", g=GROUPS)
        run(v.tensor_tensor(em, E_l.rearrange("p i (g e) -> p i g e", g=GROUPS),
                            rOG.unsqueeze(3).to_broadcast([P, NT, GROUPS, PER_GROUP]), ALU.mult))
        run(v.tensor_tensor(em, em, rPen.unsqueeze(3).to_broadcast([P, NT, GROUPS, PER_GROUP]), ALU.add))
        run(v.tensor_reduce(r5[0], rE, AX.X, ALU.max))
        first_max(O1, rE, r5[0], "iota32", NE)
        run(v.tensor_scalar(rT, O1, -2.0 * BIG, None, ALU.mult))
        run(v.tensor_tensor(rE, rE, rT, ALU.add))
        run(v.tensor_reduce(r5[1], rE, AX.X, ALU.max))
        first_max(O2, rE, r5[1], "iota32", NE)
        v.tensor_tensor(rd, r5[1], r5[0], ALU.subtract).then_inc(rt_exp_in, 1)
        run(v.tensor_tensor(rT, O1, O2, ALU.add))
        v.tensor_tensor(picks[:, :, :], rT, bc(con("valid"), NE), ALU.mult).then_inc(chosen, 1)
        dve.wait_ge(rt_exp_out, 2)
        run(v.tensor_reduce(r5[2], rG, AX.X, ALU.add))
        run(v.tensor_scalar(r5[3], rd, 1.0, None, ALU.add))
        run(v.tensor_tensor(r5[3], r5[3], r5[2], ALU.mult))
        run(v.reciprocal(gate[:, 0, :], r5[3]))
        run(v.tensor_tensor(gate[:, 1, :], gate[:, 0, :], rd, ALU.mult))

        dve.wait_ge(ranks_done, 1)
        totals = bank[:, 1, 0:NT * NE].rearrange("p (i e) -> p i e", i=NT)
        run(v.memset(base[:, 0, :], 0.0))
        for i in range(NT):
            run(v.tensor_tensor(base[:, i + 1, :], base[:, i, :], totals[:, i, :], ALU.add))
        run(v.tensor_tensor(rank, bank[:, 0, 0:NT * NE].rearrange("p (i e) -> p i e", i=NT), base[:, 0:NT, :], ALU.add))
        run(v.tensor_tensor(nb8, base[:, NT, :].unsqueeze(2).to_broadcast([P, NE, 8]),
                            con("steps").unsqueeze(1).to_broadcast([P, NE, 8]), ALU.is_gt))
        run(v.tensor_reduce(cum[0], nb8, AX.X, ALU.add))
        run(v.tensor_copy(nb, cum[0]))
        for n, sh in enumerate((1, 2, 4, 8, 16)):
            a, b_ = cum[n % 2], cum[(n + 1) % 2]
            step(v.tensor_copy(b_[:, 0:sh], a[:, 0:sh]))
            run(v.tensor_tensor(b_[:, sh:], a[:, sh:], a[:, 0:NE - sh], ALU.add))
        end = cum[1]
        run(v.tensor_tensor(cum[0], end, nb, ALU.subtract))
        run(v.tensor_scalar(cum[0], cum[0], float(SLOTS), float(NMAIN - SLOTS), ALU.mult, ALU.add))
        run(v.tensor_tensor(cum[0], cum[0], con("base"), ALU.subtract))
        run(v.tensor_scalar(rT, rank, float(SLOTS), None, ALU.is_ge))
        run(v.tensor_tensor(rT, rT, cum[0].unsqueeze(1).to_broadcast([P, NT, NE]), ALU.mult))
        run(v.tensor_tensor(rank, rank, row("base", NE), ALU.add))
        run(v.tensor_tensor(rank, rank, rT, ALU.add))
        for c, O in enumerate((O1, O2)):
            run(v.tensor_tensor(rT, O, rank, ALU.mult))
            run(v.tensor_reduce(slotF[:, c, :], rT, AX.X, ALU.add))
        NC = 2 * NT

        def cross(ap, n):
            return ap.rearrange("p c i -> p (c i)").unsqueeze(2).to_broadcast([P, NC, n])

        def along(name, n):
            return con(name).unsqueeze(1).to_broadcast([P, NC, n])

        run(v.tensor_tensor(over_blk[:, :, :], cross(slotF[:, :, :], NBLK - 1), along("blk_start", NBLK - 1), ALU.is_ge))
        run(v.tensor_reduce(blkF[:, :, :].rearrange("p c i -> p (c i)"), over_blk[:, :, :], AX.X, ALU.add))
        step(v.scalar_tensor_tensor(slotF[:, :, :], blkF[:, :, :], -float(SLOTS), slotF[:, :, :], ALU.mult, ALU.add))
        v.tensor_tensor(is_blk[:, :, :], cross(blkF[:, :, :], NBLK), along("iota_blk", NBLK), ALU.is_equal).then_inc(blk_ready, 1)
        dve.wait_ge(blk_ready, 1)
        v.tensor_tensor(lanes[:, :, :], cross(slotF[:, :, :], P), along("lane", P), ALU.is_equal)
        for c in range(2):
            mine = slice(c * NT, (c + 1) * NT)
            v.tensor_tensor(q_p[:, mine, :], is_blk[:, mine, :], bc(con("tok_p"), NBLK), ALU.mult).then_inc(onehots_ready, 1)
        run(v.tensor_tensor(nbe, end[0:1, :].unsqueeze(1).to_broadcast([1, NOVER, NE]),
                            con("blocks", 1).unsqueeze(2).to_broadcast([1, NOVER, NE]), ALU.is_le))
        run(v.tensor_reduce(bef, nbe, AX.X, ALU.add))
        run(v.tensor_scalar(bef, bef, float(NE - 1), None, ALU.min))
        run(v.tensor_copy(meta[0:1, 0:NOVER], bef))
        v.tensor_copy(meta[0:1, NOVER:NOVER + 1], end[0:1, NE - 1:NE]).then_inc(meta_ready, 1)

        dve.wait_ge(maps_done, 1)
        token, choice = bank[:, 3, 0:NBLK], bank[:, 2, 0:NBLK]
        run(v.tensor_scalar(vacant[:, :], token, 0.0, 4.0 * D, ALU.is_equal, ALU.mult))
        run(v.scalar_tensor_tensor(G1[:, :], token, -1.0, vacant[:, :], ALU.add, ALU.add))

        def gather_numbers(q, done):
            for s in range(2):
                cols = bass.ds(q * 2 + s, 1) if not isinstance(q, int) else slice(2 * q + s, 2 * q + s + 1)
                lane = slice(s * SLOTS, (s + 1) * SLOTS)
                last = v.tensor_scalar(gidx[lane, :], G1[lane, cols], 1.0, None, ALU.mult)
            last.then_inc(done, 1)

        gather_numbers(0, gidx_ready)
        run(v.scalar_tensor_tensor(S1[:, :], choice, 2.0, vacant[:, :], ALU.mult, ALU.add))
        run(v.scalar_tensor_tensor(S1[:, :], token, 4.0, S1[:, :], ALU.mult, ALU.add))
        run(v.tensor_scalar(S1[:, :], S1[:, :], con("half"), None, ALU.add))

        def gated(s, done):
            v.tensor_tensor(hg[0:SLOTS, s, :], hg[0:SLOTS, s, :], proj[64:64 + SLOTS, s, 0, :], ALU.mult).then_inc(done, 1)

        def hidden_copy(s, done):
            v.tensor_copy(hT2[:, s, :, :], bank[:, 2 + s, 0:4 * SLOTS].rearrange("p (k l) -> p k l", k=4)).then_inc(done, 1)

        def turned_rows(done):
            for b in range(2):
                last = v.tensor_tensor(xsT[:, 4 * b:4 * b + 4, :], bank[:, b, :].rearrange("p (k l) -> p k l", k=4),
                                       g_ffn[:, 4 * b:4 * b + 4].unsqueeze(2).to_broadcast([P, 4, P]), ALU.mult)
            last.then_inc(done, 1)

        def pair(it, m):
            dve.wait_ge(xsT_done, it * NSETS + m + 1)
            turned_rows(xsT_copied)
            gather_numbers(it * NSETS + m + 1, gidx_ready)
            for s in range(2):
                dve.wait_ge(silu_done, it * (2 * NSETS) + 2 * m + s + 1)
                gated(s, act_done[s])
            for s in range(2):
                e = it * (2 * NSETS) + 2 * m + s
                dve.wait_ge(hT2_done, e + 1)
                hidden_copy(s, hT2_copied[s])
                dve.wait_ge(down_done, e + 1)
                if m:
                    dve.wait_ge(ys_stored[s], it * (16 * NSETS) + 16 * m)
                v.tensor_copy(yo[:, s, :], proj[:, s, 1, :])
                cols = bass.ds(e, 1) if not isinstance(e, int) else slice(e, e + 1)
                v.tensor_scalar(sidx[s][:, :], S1[:, cols], 1.0, None, ALU.mult).then_inc(yo_ready, 1)

        run_pairs(dve, pair)
        for s in range(2):
            dve.wait_ge(ys_stored[s], 16 * PAIRS)
        dve.wait_ge(xs_loaded, 16 * (PAIRS + 1))
        dve.wait_ge(meta_ready, 1)
        n_more = dve.value_load(meta[0:1, NOVER:NOVER + 1], min_val=0, max_val=NOVER)
        with dve.If(n_more > 0):
            with dve.Fori(0, NOVER) as b:
                with dve.If(b < n_more):
                    dve.wait_ge(more_free, b + 1)
                    v.tensor_scalar(sidx[0][:, :], S1[:, bass.ds(b + NE, 1)], 1.0, None, ALU.mult)
                    v.tensor_scalar(gidx[0:SLOTS, :], G1[0:SLOTS, bass.ds(b + NE, 1)], 1.0, None, ALU.mult).then_inc(more_idx, 1)
                    dve.wait_ge(more_xT, b + 1)
                    turned_rows(more_xT_copied)
                    dve.wait_ge(more_silu, b + 1)
                    gated(0, more_act)
                    dve.wait_ge(more_hT, b + 1)
                    hidden_copy(0, more_hT_copied)
                    dve.wait_ge(more_down, b + 1)
                    v.tensor_copy(yo[:, 0, :], proj[:, 0, 1, :]).then_inc(more_yo, 1)

        def combine(i):
            r = ROWS[i]
            xi = X[0:r, i, :]
            dve.wait_ge(combined_loaded[i], 16)
            step(v.scalar_tensor_tensor(xi, zc[i][0:r, 0, :], gate[0:r, 0, i:i + 1], xi, ALU.mult, ALU.add))
            step.settle()
            v.scalar_tensor_tensor(xi, zc[i][0:r, 1, :], gate[0:r, 1, i:i + 1], xi, ALU.mult, ALU.add).then_inc(comb_done, 1)

        combine(0)
        for i in range(NT):
            if i + 1 < NT:
                combine(i + 1)
            dve.wait_ge(comb_rms, i + 1)
            v.reciprocal(st_x[0:ROWS[i], 5, i:i + 1], st_x[0:ROWS[i], 2, i:i + 1]).then_inc(comb_inv, 1)
        i, r = NT - 1, ROWS[NT - 1]
        dve.wait_ge(comb_inv, NT)
        v.scalar_tensor_tensor(zo[i][0:r, :], X[0:r, i, :], st_x[0:r, 5, i:i + 1], g_fin[0:r, :], ALU.mult, ALU.mult)\
            .then_inc(y_last, 1)


INS = ["x_prompt", "x_sample", "cache_ckv", "cache_krope", "state_gla", "w_in", "w_uq", "w_ukv", "w_gate2", "b_gate2",
       "w_branch_a", "w_branch_b", "w_out", "w_router_group", "b_router_group", "w_router_expert",
       "b_router_expert", "w_exp_gate", "w_exp_up", "w_exp_down", "g_norm_final"]
OUTS = [("y_prompt", (1, SEQ, D)), ("y_sample", (1, DEC, D)), ("ckv_prompt", (1, 1, SEQ, KV_LORA)),
        ("krope_prompt", (1, 1, SEQ, ROPE)), ("gla_prompt", (1, 1, GH, DK, DV)), ("ckv_sample", (1, 1, DEC, KV_LORA)),
        ("krope_sample", (1, 1, DEC, ROPE)), ("gla_sample", (1, 1, GH, DK, DV))]


def kernel(**inputs):
    import concourse.bacc as bacc
    from concourse.bass_utils import run_bass_kernel_spmd

    nc = bacc.Bacc("TRN2", target_bir_lowering=False, num_devices=1)
    arrays = {n: np.ascontiguousarray(inputs[n]) for n in INS}
    arrays["shape_constants"] = shape_constants()
    for n, src in (("g_mix_cols", "g_norm_mix"), ("g_q_cols", "g_qnorm"), ("g_kv_cols", "g_kvnorm"), ("g_gla_cols", "g_gla_norm"),
                   ("g_ffn_cols", "g_norm_ffn")):
        arrays[n] = np.ascontiguousarray(np.asarray(inputs[src]).reshape(-1, P).T)
    t = {n: nc.dram_tensor(f"in_{n}", a.shape, mybir.dt.from_np(a.dtype), kind="ExternalInput").ap() for n, a in arrays.items()}
    for n, shape in OUTS:
        t[n] = nc.dram_tensor(f"out_{n}", shape, F32, kind="ExternalOutput").ap()
    build(nc, t)
    r = run_bass_kernel_spmd(nc, [{f"in_{n}": a for n, a in arrays.items()}], core_ids=[0])
    return tuple(r.results[0][f"out_{n}"] for n, _ in OUTS)
```
